# Optimizing a Trainium2 kernel written in Bass

```python
import jax, jax.numpy as jnp
from jax import lax
import numpy as np

D_MODEL = 1024
BATCH = 1
SEQ = 256
DEPTH = 2

N_MIXERS = 2
EPS = 1e-6
GLA_HEADS = 4
GLA_DK = D_MODEL // 2 // GLA_HEADS
GLA_DV = D_MODEL // GLA_HEADS
GLA_GATE_RANK = 16
GLA_GATE_NORM = 16.0
GLA_CHUNK = 64
GLA_IN = 2 * GLA_HEADS * GLA_DK + 2 * GLA_HEADS * GLA_DV + GLA_GATE_RANK
MOBA_HEADS = 8
MOBA_HD = D_MODEL // MOBA_HEADS
MOBA_BLOCK = 256
MOBA_TOPK = 3
MOBA_QCHUNK = 64
MOBA_IN = 3 * MOBA_HEADS * MOBA_HD
ROPE_THETA = 10000.0
D_FF = 4 * D_MODEL
N_GLA_LAYERS = (DEPTH + 1) // 2
N_MOBA_LAYERS = DEPTH // 2

kernel_name = "hybrid_gla_moba_adaln_trunk"

def rms_norm(t, g):
    tf = t.astype(jnp.float32)
    y = tf * lax.rsqrt(jnp.mean(tf * tf, axis=-1, keepdims=True) + EPS)
    return (y * g.astype(jnp.float32)).astype(t.dtype)

def rope(t, positions):
    half = t.shape[-1] // 2
    inv_freq = ROPE_THETA ** (-jnp.arange(half, dtype=jnp.float32) / half)
    ang = positions.astype(jnp.float32)[..., None] * inv_freq
    cos = jnp.cos(ang)[:, :, None, :]
    sin = jnp.sin(ang)[:, :, None, :]
    t1, t2 = t[..., :half], t[..., half:]
    return jnp.concatenate([t1 * cos - t2 * sin, t2 * cos + t1 * sin], axis=-1)

def gla_mixer(h, w_in, w_gate_up, b_gate, onorm_g, w_out):
    B, S, _ = h.shape
    H, DK, DV, L = GLA_HEADS, GLA_DK, GLA_DV, GLA_CHUNK
    NC = S // L
    f32 = jnp.float32
    splits = np.cumsum([H * DK, H * DK, H * DV, H * DV]).tolist()
    q, k, v, r, glr = jnp.split(h @ w_in, splits, axis=-1)
    g = jax.nn.log_sigmoid((glr @ w_gate_up + b_gate).astype(f32)) / GLA_GATE_NORM
    q = q.astype(f32).reshape(B, NC, L, H, DK) * (DK ** -0.5)
    k = k.astype(f32).reshape(B, NC, L, H, DK)
    v = v.astype(f32).reshape(B, NC, L, H, DV)
    G = jnp.cumsum(g.reshape(B, NC, L, H, DK), axis=2)
    G_last = G[:, :, -1]
    q_dec = q * jnp.exp(G)
    k_inv = k * jnp.exp(-G)
    causal = jnp.tril(jnp.ones((L, L), dtype=bool))
    A = jnp.where(causal, jnp.einsum('bnihd,bnjhd->bnhij', q_dec, k_inv), 0.0)
    o_intra = jnp.einsum('bnhij,bnjhv->bnihv', A, v)
    k_tail = k * jnp.exp(G_last[:, :, None] - G)
    U = jnp.einsum('bnjhd,bnjhv->bnhdv', k_tail, v)
    decay = jnp.exp(G_last)

    def step(state, inp):
        a, u = inp
        return a[..., None] * state + u, state

    _, states = lax.scan(step, jnp.zeros((B, H, DK, DV), f32),
                         (jnp.moveaxis(decay, 1, 0), jnp.moveaxis(U, 1, 0)))
    states = jnp.moveaxis(states, 0, 1)
    o_inter = jnp.einsum('bnihd,bnhdv->bnihv', q_dec, states)
    o = (o_intra + o_inter).reshape(B, S, H, DV)
    o = rms_norm(o, onorm_g).reshape(B, S, H * DV) * jax.nn.silu(r.astype(f32))
    return o.astype(h.dtype) @ w_out

def moba_mixer(h, positions, w_in, q_norm_g, k_norm_g, w_out):
    B, S, _ = h.shape
    H, HD, BS, C = MOBA_HEADS, MOBA_HD, MOBA_BLOCK, MOBA_QCHUNK
    f32 = jnp.float32
    q, k, v = jnp.split(h @ w_in, 3, axis=-1)
    q = rope(rms_norm(q.reshape(B, S, H, HD).astype(f32), q_norm_g), positions)
    k = rope(rms_norm(k.reshape(B, S, H, HD).astype(f32), k_norm_g), positions)
    v = v.reshape(B, S, H, HD).astype(f32)
    NB = -(-S // BS)
    Sp = NB * BS
    pad = ((0, 0), (0, Sp - S), (0, 0), (0, 0))
    q, k, v = jnp.pad(q, pad), jnp.pad(k, pad), jnp.pad(v, pad)
    k_blocks = k.reshape(B, NB, BS, H, HD).transpose(0, 3, 1, 2, 4)
    v_blocks = v.reshape(B, NB, BS, H, HD).transpose(0, 3, 1, 2, 4)
    k_mean = jnp.mean(k_blocks, axis=3)
    gate = jnp.einsum('bshd,bhnd->bshn', q, k_mean)
    own_blk = jnp.arange(Sp) // BS
    past = jnp.arange(NB)[None, :] < own_blk[:, None]
    gate = jnp.where(past[None, :, None, :], gate, -jnp.inf)
    topk = min(MOBA_TOPK, NB)
    _, sel = lax.top_k(gate, topk)
    valid = sel < own_blk[None, :, None, None]

    NQ = Sp // C

    def chunkify(t):
        return jnp.moveaxis(t.reshape(B, NQ, C, *t.shape[2:]), 1, 0)

    scale = HD ** -0.5
    b_idx = jnp.arange(B)[:, None, None, None]
    h_idx = jnp.arange(H)[None, None, :, None]
    q_off = jnp.arange(C)
    k_off = jnp.arange(BS)

    def attend(args):
        ci, qc, sc, vc = args
        s0 = ci * C
        start = (s0 // BS) * BS
        k_own = lax.dynamic_slice_in_dim(k, start, BS, axis=1)
        v_own = lax.dynamic_slice_in_dim(v, start, BS, axis=1)
        kg = k_blocks[b_idx, h_idx, sc]
        vg = v_blocks[b_idx, h_idx, sc]
        s_sel = jnp.einsum('bchd,bchjkd->bchjk', qc, kg) * scale
        s_sel = jnp.where(vc[..., None], s_sel, -jnp.inf).reshape(B, C, H, topk * BS)
        s_own = jnp.einsum('bchd,bkhd->bchk', qc, k_own) * scale
        causal = (start + k_off)[None, :] <= (s0 + q_off)[:, None]
        s_own = jnp.where(causal[None, :, None, :], s_own, -jnp.inf)
        p = jax.nn.softmax(jnp.concatenate([s_sel, s_own], axis=-1), axis=-1)
        p_sel = p[..., :topk * BS].reshape(B, C, H, topk, BS)
        p_own = p[..., topk * BS:]
        return (jnp.einsum('bchjk,bchjkd->bchd', p_sel, vg)
                + jnp.einsum('bchk,bkhd->bchd', p_own, v_own))

    out = lax.map(attend, (jnp.arange(NQ), chunkify(q), chunkify(sel), chunkify(valid)))
    out = jnp.moveaxis(out, 0, 1).reshape(B, Sp, H * HD)[:, :S]
    return out.astype(h.dtype) @ w_out

def sq_relu_mlp(h, w1, w2):
    return jnp.square(jax.nn.relu(h @ w1)) @ w2

def setup_inputs(seed: int = 0) -> dict:
    key = jax.random.key(seed)
    ks = jax.random.split(key, 20)
    D = D_MODEL
    nrm = lambda k, shape, fan_in: jax.random.normal(k, shape, jnp.float32) * (fan_in ** -0.5)
    x = jax.random.normal(ks[0], (BATCH, SEQ, D), jnp.float32)
    c = jax.random.normal(ks[1], (BATCH, D), jnp.float32)
    positions = jnp.broadcast_to(jnp.arange(SEQ, dtype=jnp.int32), (BATCH, SEQ))
    return {
        "x": x,
        "c": c,
        "positions": positions,
        "ada_w": nrm(ks[2], (DEPTH, D, 6 * D), D),
        "ada_b": 0.01 * jax.random.normal(ks[3], (DEPTH, 6 * D), jnp.float32),
        "norm_mix_g": 1.0 + 0.05 * jax.random.normal(ks[4], (DEPTH, D), jnp.float32),
        "norm_mlp_g": 1.0 + 0.05 * jax.random.normal(ks[5], (DEPTH, D), jnp.float32),
        "gla_w_in": nrm(ks[6], (N_GLA_LAYERS, D, GLA_IN), D),
        "gla_w_gate_up": nrm(ks[7], (N_GLA_LAYERS, GLA_GATE_RANK, GLA_HEADS * GLA_DK), GLA_GATE_RANK),
        "gla_b_gate": 0.01 * jax.random.normal(ks[8], (N_GLA_LAYERS, GLA_HEADS * GLA_DK), jnp.float32),
        "gla_onorm_g": 1.0 + 0.05 * jax.random.normal(ks[9], (N_GLA_LAYERS, GLA_DV), jnp.float32),
        "gla_w_out": nrm(ks[10], (N_GLA_LAYERS, GLA_HEADS * GLA_DV, D), GLA_HEADS * GLA_DV),
        "moba_w_in": nrm(ks[11], (N_MOBA_LAYERS, D, MOBA_IN), D),
        "moba_q_norm_g": 1.0 + 0.05 * jax.random.normal(ks[12], (N_MOBA_LAYERS, MOBA_HD), jnp.float32),
        "moba_k_norm_g": 1.0 + 0.05 * jax.random.normal(ks[13], (N_MOBA_LAYERS, MOBA_HD), jnp.float32),
        "moba_w_out": nrm(ks[14], (N_MOBA_LAYERS, MOBA_HEADS * MOBA_HD, D), MOBA_HEADS * MOBA_HD),
        "mlp_w1": nrm(ks[15], (DEPTH, D, D_FF), D),
        "mlp_w2": nrm(ks[16], (DEPTH, D_FF, D), D_FF),
    }

def reference(x, c, positions, ada_w, ada_b, norm_mix_g, norm_mlp_g,
              gla_w_in, gla_w_gate_up, gla_b_gate, gla_onorm_g, gla_w_out,
              moba_w_in, moba_q_norm_g, moba_k_norm_g, moba_w_out,
              mlp_w1, mlp_w2):
    c_act = jax.nn.silu(c)
    for i in range(DEPTH):
        mod = (c_act @ ada_w[i] + ada_b[i])[:, None, :]
        sh1, sc1, g1, sh2, sc2, g2 = jnp.split(mod, 6, axis=-1)
        h = rms_norm(x, norm_mix_g[i]) * (1 + sc1) + sh1
        j = i // N_MIXERS
        if i % N_MIXERS == 0:
            y = gla_mixer(h, gla_w_in[j], gla_w_gate_up[j], gla_b_gate[j],
                          gla_onorm_g[j], gla_w_out[j])
        else:
            y = moba_mixer(h, positions, moba_w_in[j], moba_q_norm_g[j],
                           moba_k_norm_g[j], moba_w_out[j])
        x = x + g1 * y
        h = rms_norm(x, norm_mlp_g[i]) * (1 + sc2) + sh2
        x = x + g2 * sq_relu_mlp(h, mlp_w1[i], mlp_w2[i])
    return x


_drawn_inputs = setup_inputs


def setup_inputs(seed=0):
    import zlib

    import numpy as np

    out = dict(_drawn_inputs(seed))
    spreads = {}
    factors = {'gla_b_gate': 8.0, 'moba_q_norm_g': 8.0, 'moba_k_norm_g': 8.0}
    for name, (base, spread) in spreads.items():
        noise = np.random.default_rng([zlib.crc32(name.encode()), seed]).standard_normal(out[name].shape)
        drawn = base * np.exp(spread * noise) if base else spread * noise
        out[name] = __import__('jax').numpy.asarray(drawn.astype(out[name].dtype))
    for name, factor in factors.items():
        out[name] = (out[name] * factor).astype(out[name].dtype)
    return out
```

```python
from contextlib import ExitStack

import concourse.bass as bass
from concourse import mybir

F32 = mybir.dt.float32
F32R = mybir.dt.float32r
I32 = mybir.dt.int32
ALU = mybir.AluOpType
ACT = mybir.ActivationFunctionType
X_AXIS = mybir.AxisListType.X

P = 128
TB = 2
COLS = 512
RAW = 4
SPLIT = 4
UNIT = 1024
ADA_ACC = 8
L = 64
EPS = 1e-6
NEG = -1.0e30
MAGIC = 1.5 * 2.0 ** 23
TWO_PI = (6.28125, 0.0019350051879882812, 3.019916050561733e-07)


def trunk_kernel(nc, x_d, c_d, pos_d, ada_w, ada_b, mix_g, mlp_g, gla_in, gla_up, gla_bg, gla_og,
                 gla_out, moba_in, moba_qg, moba_kg, moba_out, w1_d, w2_d, eye_d, keep_d, amask_d,
                 restart_d, invf_d, out_d):
    DEPTH, D = mix_g.shape
    KC = D // P
    SEQ = x_d.shape[1]
    RANK, HDK = gla_up.shape[1:]
    DV = gla_og.shape[1]
    GH = gla_out.shape[1] // DV
    DK = HDK // GH
    NCH = SEQ // L
    HD = moba_qg.shape[1]
    MH = D // HD
    NJ = w1_d.shape[2] // COLS
    HC = COLS // P
    assert (SEQ, D, DK, HD, DV) == (TB * P, 1024, P, P, 256) and D == 2 * COLS and 2 * GH == MH

    MIX_BLOCKS = 8
    mix_base = [l * 4 * (MIX_BLOCKS + 2 * NJ) for l in range(DEPTH)]
    mlp_base = [b + 4 * MIX_BLOCKS for b in mix_base]
    MIX_IN = [[1, 0, 2, 3, 4, 5], [2, 0, 3, 1, 4, 5]]
    mix_w = [(gla_in[0], gla_out[0]), (moba_in[0], moba_out[0])]
    ADA_AT = [{1: [4], 2: [5], 3: [6], 4: [7], 5: [8], 6: [9], 7: [10, 11]},
              {1: [20], 2: [21], 4: [22], 6: [23]}]

    ctx = ExitStack()
    with ctx:
        def sb(name, shape, dt=F32):
            return ctx.enter_context(nc.sbuf_tensor(name, shape, dt))

        def sem(name):
            return ctx.enter_context(nc.semaphore(name))

        w_raw = sb("w_raw", [P, RAW, 2, UNIT])
        w_hi = sb("w_hi", [P, SPLIT, UNIT], F32R)
        w_lo = sb("w_lo", [P, SPLIT, UNIT], F32R)
        ada_raw = sb("ada_raw", [P, 2, KC // 2, COLS])
        ada_acc = sb("ada_acc", [P, ADA_ACC, COLS])
        x = sb("x", [P, TB, D])
        a_hi = sb("a_hi", [P, KC, SEQ], F32R)
        a_lo = sb("a_lo", [P, KC, SEQ], F32R)
        m_hi = sb("m_hi", [P, HC, SEQ], F32R)
        m_lo = sb("m_lo", [P, HC, SEQ], F32R)
        gates = sb("gates", [P, 2, D])
        eye = sb("eye", [P, P])
        keep = sb("keep", [P, P], I32)
        ones = sb("ones", [P, P])
        rows = sb("rows", [P, P])
        cols = sb("cols", [P, P])
        c_act = sb("c_act", [P, 3, KC])
        modc = sb("modc", [P, DEPTH, 4, KC])
        g_bias = sb("g_bias", [P, D])
        stat = sb("stat", [P, 192])
        eps = sb("eps", [P, 1])
        onorm = sb("onorm", [P, DV])
        amask = sb("amask", [P, 3 * P])
        glr_w = sb("glr_w", [P, KC, RANK])
        glr_up = sb("glr_up", [RANK, HDK])
        glrT = sb("glrT", [RANK, SEQ])
        dec = sb("dec", [P, GH, NCH])
        pos_i = sb("pos_i", [P, TB], I32)
        K1 = 1024
        ARENA = 14 * K1 + 512
        arena = sb("arena", [P, ARENA])

        def area(at, *shape):
            n = 1
            for s in shape:
                n *= s
            assert at + n <= ARENA
            v = arena[:, at:at + n]
            if len(shape) == 2:
                v = v.rearrange("p (a b) -> p a b", a=shape[0])
            elif len(shape) == 3:
                v = v.rearrange("p (a b c) -> p a b c", a=shape[0], b=shape[1])
            return v

        xn = area(0, TB, D)
        hT = area(2 * K1, KC, SEQ)
        y_tmp = area(2 * K1, 2 * TB, COLS)
        relu = area(4 * K1, TB, COLS)
        sq = area(5 * K1, HC, SEQ)
        g_v = area(0, TB, D)
        silu_r = area(2 * K1, TB, D)
        g_tok = area(4 * K1, 2, TB, COLS)
        o_tok = area(4 * K1, TB, D)
        g_z = area(6 * K1, GH, SEQ)
        k_tailT = area(6 * K1, GH, SEQ)
        g_t = area(7 * K1, GH, SEQ)
        g_e = area(8 * K1, GH, SEQ)
        att = area(8 * K1, TB, GH, P)
        g_i = area(9 * K1, GH, SEQ)
        k_inv = area(10 * K1, GH, SEQ)
        q_dec = area(11 * K1, GH, SEQ)
        k_tail = area(12 * K1, TB, GH, DK)
        g_s = area(3 * K1, GH, SEQ)
        state = [None, area(7 * K1, GH, DV), area(9 * K1, GH, DV), area(6 * K1, GH, DV)]
        restart = area(12 * K1, GH * NCH, L)
        b_tok = area(0, TB, COLS)
        b_t = area(1 * K1, TB, COLS)
        b_u = area(2 * K1, TB, COLS)
        b_r = area(3 * K1, TB, COLS)
        b_kT = area(4 * K1, MH, SEQ)
        b_qT = area(6 * K1, MH, SEQ)
        b_v = area(8 * K1, TB, D)
        b_p = area(10 * K1, 4, 3 * P)
        b_pT = area(11 * K1 + 512, 4, 3 * P)
        tab = area(13 * K1 + 512, 2, 2, TB * P)
        r_w = area(4 * K1, 8, TB * P)

        ps = ctx.enter_context(nc.psum_tensor("ps", [P, 8, COLS], F32))

        S_SS, S_LN, S_R0, S_V, S_B, S_RS = 0, 8, 16, 24, 32, 40
        S_O = 48
        S_MX = 112

        raw_in = [sem(f"raw_in{i}") for i in range(RAW)]
        ada_in = [sem(f"ada_in{i}") for i in range(2)]
        vec_in, x_in, glr_in, out_sem = sem("vec_in"), sem("x_in"), sem("glr_in"), sem("out_sem")
        tab_in, con_in, gb_in = sem("tab_in"), sem("con_in"), sem("gb_in")
        hi_made, lo_made = sem("hi_made"), sem("lo_made")
        unit_used = sem("unit_used")
        ada_mac = sem("ada_mac")
        set_up = sem("set_up")
        vec_T, vec_ok, ec_ok, c_ok = sem("vec_T"), sem("vec_ok"), sem("ec_ok"), sem("c_ok")
        mod_T, mod_red, mod_ok = sem("mod_T"), sem("mod_red"), sem("mod_ok")
        gate_p, gate_ok = sem("gate_p"), sem("gate_ok")
        sc_arg, sc_ok = sem("sc_arg"), sem("sc_ok")
        x_new = sem("x_new")
        ss_ok, ln_ok, r0_ok, xn_ok = sem("ss_ok"), sem("ln_ok"), sem("r0_ok"), sem("xn_ok")
        xT_ok, hA_ok, hD_ok = sem("xT_ok"), sem("hA_ok"), sem("hD_ok")
        ahi_ok, a_ok = sem("ahi_ok"), sem("a_ok")
        in_out = sem("in_out")
        relu_ok, tr_ok, sq_ok, mhi_ok, m_ok = (sem("relu_ok"), sem("tr_ok"), sem("sq_ok"),
                                               sem("mhi_ok"), sem("m_ok"))
        y_ok = sem("y_ok")
        dve_step, act_step = sem("dve_step"), sem("act_step")
        oT_ok = sem("oT_ok")
        z_p, kT_p, qT_p, kt_p, att_p, u_p, o_p, glr_p = (sem("z_p"), sem("kT_p"), sem("qT_p"), sem("kt_p"),
                                                         sem("att_p"), sem("u_p"), sem("o_p"), sem("glr_p"))
        glr_ok, z_ok, ez_ok, G_ok, eG_ok, kd_ok, qd_ok = (sem("glr_ok"), sem("z_ok"), sem("ez_ok"), sem("G_ok"),
                                                          sem("eG_ok"), sem("kd_ok"), sem("qd_ok"))
        kt_ok, zero_ok, att_ok, st_ok, oss_ok, or0_ok = (sem("kt_ok"), sem("zero_ok"), sem("att_ok"), sem("st_ok"),
                                                         sem("oss_ok"), sem("or0_ok"))
        ot_ok = sem("ot_ok")
        bss_ok, br0_ok, rot_ok, rT_p, rT_ok = (sem("bss_ok"), sem("br0_ok"), sem("rot_ok"), sem("rT_p"),
                                               sem("rT_ok"))
        s_p, mx_ok, ex_ok, pn_ok, pT_p, pT_ok = (sem("s_p"), sem("mx_ok"), sem("ex_ok"), sem("pn_ok"),
                                                 sem("pT_p"), sem("pT_ok"))

        C_C, C_MIX, C_MLP = 0, KC, KC + DEPTH * KC
        C_BG = C_MLP + DEPTH * KC
        C_AB = C_BG + GH
        N_ROWS = C_AB + DEPTH * 4 * KC
        N_VEC = 5 + 2 * DEPTH

        def acc_slot(b):
            return (b + 4) % ADA_ACC

        def in_bank(n, tb):
            return 4 + 2 * (n % 2) + tb

        def y_bank(mlp, half, tb):
            return 4 + 2 * tb + half if mlp else 2 * half + tb

        def norm_bank(v):
            return 4 if v % 2 else 0

        def chunk_at(v, k):
            return norm_bank(v) + 2 * (k // 4) + k % 2, ((k % 4) // 2) * SEQ

        block = ctx.enter_context(nc.Block())

        @block.sync
        def _(sp):
            def load_ada(b, half):
                l, n = b // 12, b % 12
                if b > 0:
                    sp.wait_ge(ada_mac, 4 * (2 * b + half - 1))
                src = ada_w[l, half * 4 * P:(half + 1) * 4 * P, n * COLS:(n + 1) * COLS]
                sp.dma_start(ada_raw[:, half], src.rearrange("(k p) n -> p k n", p=P)
                             ).then_inc(ada_in[half], 16)

            def load_piece(m, slot, src):
                if not (isinstance(m, int) and m < RAW):
                    sp.wait_ge(lo_made, 2 * (m - RAW) + 2)
                dst = w_raw[:, slot]
                if src.shape[1] == COLS:
                    dst = dst.rearrange("p u (k n) -> p (u k) n", k=2)
                sp.dma_start(dst, src.rearrange("(k p) n -> p k n", p=P)).then_inc(raw_in[slot], 16)

            def vec(at, n, src):
                sp.dma_start(rows[at:at + n, :], src).then_inc(vec_in, 16)

            vec(C_C, KC, c_d[0, :].rearrange("(k p) -> k p", p=P))
            vec(C_MIX, DEPTH * KC, mix_g.rearrange("l (k p) -> (l k) p", p=P))
            vec(C_MLP, DEPTH * KC, mlp_g.rearrange("l (k p) -> (l k) p", p=P))
            vec(C_BG, GH, gla_bg[0, :].rearrange("(k p) -> k p", p=P))
            for l in range(DEPTH):
                for s in range(2):
                    vec(C_AB + (2 * l + s) * 2 * KC, 2 * KC,
                        ada_b[l, 3 * s * D:(3 * s + 2) * D].rearrange("(k p) -> k p", p=P))
            sp.dma_start(eye[:, :], eye_d).then_inc(vec_in, 16)
            for half in range(2):
                load_ada(0, half)
            for tb in range(TB):
                sp.dma_start(x[:, tb], x_d[0, tb * P:(tb + 1) * P, :]).then_inc(x_in, 16)
            with nc.allow_non_contiguous_dma(reason="256 numbers"):
                sp.dma_start(pos_i[:, :], pos_d[0, :].rearrange("(b p) -> p b", p=P)).then_inc(tab_in, 16)
            sp.dma_start(r_w[:, 7, 0:HD // 2], invf_d.to_broadcast([P, HD // 2])).then_inc(tab_in, 16)
            sp.dma_start(r_w[:, 6, 0:HD], moba_qg.to_broadcast([P, HD])).then_inc(tab_in, 16)
            sp.dma_start(r_w[:, 6, HD:2 * HD], moba_kg.to_broadcast([P, HD])).then_inc(tab_in, 16)
            for b in range(1, 4):
                for half in range(2):
                    load_ada(b, half)
            with nc.allow_non_contiguous_dma(reason="sixteen columns"):
                sp.dma_start(glr_w[:, :, :], gla_in[0, :, gla_in.shape[2] - RANK:].rearrange("(k p) n -> p k n", p=P)
                             ).then_inc(glr_in, 16)
            sp.dma_start(glr_up[:, :], gla_up[0]).then_inc(glr_in, 16)
            sp.dma_start(keep[:, :], keep_d).then_inc(con_in, 16)
            sp.dma_start(amask[:, :], amask_d).then_inc(con_in, 16)
            sp.dma_start(onorm[:, :], gla_og.to_broadcast([P, DV])).then_inc(con_in, 16)
            sp.dma_start(restart.rearrange("p a b -> p (a b)"), restart_d.to_broadcast([P, GH * SEQ])
                         ).then_inc(con_in, 16)
            for l in range(DEPTH):
                for s in range(2):
                    q = 32 * (2 * l + s)
                    sp.dma_start(g_bias[q:q + 1, :], ada_b[l:l + 1, (3 * s + 2) * D:(3 * s + 3) * D]
                                 ).then_inc(gb_in, 16)

            def mixer(l):
                w_in, w_out = mix_w[l]
                for n in range(MIX_BLOCKS):
                    w, c0 = (w_in, MIX_IN[l][n] * COLS) if n < 6 else (w_out, (n - 6) * COLS)
                    for d in range(2):
                        m = mix_base[l] // 2 + 2 * n + d
                        load_piece(m, m % RAW, w[4 * d * P:4 * (d + 1) * P, c0:c0 + COLS])
                    for b in ADA_AT[l].get(n, []):
                        for half in range(2):
                            load_ada(b, half)

            def mlp(l):
                base = mlp_base[l] // 2

                def w1(j, d, m, slot):
                    load_piece(m, slot, w1_d[l, 4 * d * P:4 * (d + 1) * P, bass.ds(j * COLS, COLS)])

                def w2(j, d, m, slot):
                    load_piece(m, slot, w2_d[l, bass.ds(j * COLS + 2 * d * P, 2 * P), :])

                for j in range(2):
                    for d in range(2):
                        w1(j, d, base + 2 * j + d, 2 * j + d)
                    if l == 0:
                        for half in range(2):
                            load_ada(12 + j, half)
                with sp.Fori(0, NJ - 2) as i:
                    for d in range(2):
                        w2(i, d, base + 4 + 4 * i + d, d)
                    for d in range(2):
                        w1(i + 2, d, base + 6 + 4 * i + d, 2 + d)
                    if l == 0:
                        for half in range(2):
                            sp.wait_ge(ada_mac, 8 * i + 8 * 14 + 4 * (half - 1))
                            src = ada_w[1, half * 4 * P:(half + 1) * 4 * P, bass.ds((i + 2) * COLS, COLS)]
                            sp.dma_start(ada_raw[:, half], src.rearrange("(k p) n -> p k n", p=P)
                                         ).then_inc(ada_in[half], 16)
                for j in range(NJ - 2, NJ):
                    for d in range(2):
                        m = base + 4 + 4 * (NJ - 2) + 2 * (j - NJ + 2) + d
                        w2(j, d, m, m % RAW)

            mixer(0)
            mlp(0)
            mixer(1)
            mlp(1)
            for tb in range(TB):
                sp.wait_ge(x_new, 2 * (2 * DEPTH - 1) + tb + 1)
                sp.dma_start(out_d[0, tb * P:(tb + 1) * P, :], x[:, tb]).then_inc(out_sem, 16)
            sp.wait_ge(out_sem, TB * 16)

        @block.tensor
        def _(pe):
            mm, tr = nc.tensor.matmul, nc.tensor.transpose

            def tile(tb):
                return slice(tb * P, (tb + 1) * P)

            def three(out, hi, lo, slot, wc, first, last):
                mm(out, hi, w_hi[:, slot, wc], start=first, stop=False)
                mm(out, hi, w_lo[:, slot, wc], start=False, stop=False)
                return mm(out, lo, w_hi[:, slot, wc], start=False, stop=last)

            def project(u0, banks, a_wait=None, side={}):
                for u in range(4):
                    pe.wait_ge(lo_made, u0 + u + 1)
                    if a_wait is not None:
                        pe.wait_ge(a_ok, a_wait + u + 1)
                    for k in range(2):
                        for tb in range(TB):
                            z = three(ps[:, banks[tb], :], a_hi[:, 2 * u + k, tile(tb)],
                                      a_lo[:, 2 * u + k, tile(tb)], u, slice(k * COLS, (k + 1) * COLS),
                                      u == 0 and k == 0, u == 3 and k == 1)
                    z.then_inc(unit_used, 1)
                    if u in side:
                        side[u]()

            def fin_mod(b, bank):
                pe.wait_ge(ada_mac, 8 * (b + 1))
                for q in range(4):
                    z = tr(ps[:, bank, q * P:(q + 1) * P], ada_acc[:, acc_slot(b), q * P:(q + 1) * P], eye[:, :])
                z.then_inc(mod_T, 1)

            def fin_gate(b, bank):
                q = 32 * (2 * (b // 12) + (b % 12) // 6)
                half = b % 2
                pe.wait_ge(ada_mac, 8 * (b + 1))
                mm(ps[:, bank, :], ones[:, :], ada_acc[:, acc_slot(b)], start=True, stop=False)
                mm(ps[:, bank, :], ones[q:q + 1, :], g_bias[q:q + 1, half * COLS:(half + 1) * COLS],
                   start=False, stop=True).then_inc(gate_p, 1)

            def norm(v):
                for tb in range(TB):
                    pe.wait_ge(xn_ok, 2 * v + tb + 1)
                    for k in range(KC):
                        bank, at = chunk_at(v, k)
                        z = tr(ps[:, bank, at + tb * P:at + (tb + 1) * P], xn[:, tb, k * P:(k + 1) * P], eye[:, :])
                        if tb == TB - 1 and k % 4 >= 2:
                            z.then_inc(xT_ok, 1)

            def out_project(l):
                def shifts():
                    pe.wait_ge(a_ok, 4 * (3 * l + 2))
                    for i in range(4):
                        fin_mod(12 * l + 6 + i, 4 + i)

                def gate():
                    pe.wait_ge(mod_red, 4 + 8 * l + 4)
                    for i in range(2):
                        fin_gate(12 * l + 10 + i, 4 + i)

                u0 = mix_base[l] + 6 * 4
                project(u0, (0, 1), 4 * (3 * l + 1), {3: shifts})
                project(u0 + 4, (2, 3), None, {2: gate})

            def mlp(l):
                base, m0 = mlp_base[l], l * NJ

                def turn(j, first=False):
                    pe.wait_ge(relu_ok, 2 * (m0 + j) + 2)
                    if not first:
                        pe.wait_ge(sq_ok, 2 * (m0 + j))
                    for c in range(HC):
                        for tb in range(TB):
                            z = tr(ps[:, 2 + c // 2, (c % 2) * SEQ + tb * P:(c % 2) * SEQ + (tb + 1) * P],
                                   relu[:, tb, c * P:(c + 1) * P], eye[:, :])
                        if c % 2 == 1:
                            z.then_inc(tr_ok, 1)

                def down(u0, j, first):
                    for u in range(4):
                        pe.wait_ge(lo_made, u0 + u + 1)
                        if u % 2 == 0:
                            pe.wait_ge(m_ok, 2 * (m0 + j) + u // 2 + 1)
                        for tb in range(TB):
                            for h in range(2):
                                z = three(ps[:, y_bank(1, h, tb), :], m_hi[:, u, tile(tb)], m_lo[:, u, tile(tb)],
                                          u, slice(h * COLS, (h + 1) * COLS), first and u == 0, False)
                        z.then_inc(unit_used, 1)

                project(base, (0, 1), 4 * (3 * l + 2))
                pe.wait_ge(relu_ok, 2 * m0 + 2)
                project(base + 4, (0, 1), None, {1: lambda: turn(0, first=True)})
                down(base + 8, 0, True)
                with pe.Fori(1, NJ - 1) as j:
                    pe.wait_ge(relu_ok, 2 * j + 2 * m0 + 2)
                    project(8 * j + base + 4, (0, 1), None, {1: lambda: turn(j)})
                    down(8 * j + base + 8, j, False)
                j, u0 = NJ - 1, base + 4 * (2 * NJ - 1)
                turn(j)
                if l == 0:
                    for i in range(2):
                        fin_mod(12 + i, i)
                for tb in range(TB):
                    for u in range(4):
                        if tb == 0:
                            pe.wait_ge(lo_made, u0 + u + 1)
                            if u % 2 == 0:
                                pe.wait_ge(m_ok, 2 * (m0 + j) + u // 2 + 1)
                        for h in range(2):
                            z = three(ps[:, y_bank(1, h, tb), :], m_hi[:, u, tile(tb)], m_lo[:, u, tile(tb)],
                                      u, slice(h * COLS, (h + 1) * COLS), False, u == 3)
                        if tb == 1:
                            z.then_inc(unit_used, 1)
                    if tb == 0:
                        z.then_inc(y_ok, 1)
                        if l == 0:
                            pe.wait_ge(m_ok, 2 * (m0 + j) + 2)
                            for i in range(2):
                                fin_mod(14 + i, 2 + i)

            def gla():
                def glr():
                    pe.wait_ge(glr_in, 32)
                    for k in range(KC):
                        z = mm(ps[0:RANK, 0, 0:SEQ], glr_w[:, k, :], hT[:, k, :], start=k == 0, stop=k == KC - 1)
                    z.then_inc(glr_p, 1)

                def logits():
                    pe.wait_ge(glr_ok, 1)
                    for h in range(GH):
                        z = mm(ps[:, h // 2, (h % 2) * SEQ:(h % 2 + 1) * SEQ], glr_up[:, h * DK:(h + 1) * DK],
                               glrT[:, :], start=True, stop=True)
                    z.then_inc(z_p, 1)

                def turn_tok(which, bank, done):
                    for h in range(GH):
                        for tb in range(TB):
                            z = tr(ps[:, bank + h // 2, (h % 2) * SEQ + tb * P:(h % 2) * SEQ + (tb + 1) * P],
                                   g_tok[:, which, tb, h * DK:(h + 1) * DK], eye[:, :])
                    z.then_inc(done, 1)

                def turn_k():
                    pe.wait_ge(in_out, 2)
                    turn_tok(0, 2, kT_p)

                def turn_q():
                    pe.wait_ge(in_out, 4)
                    pe.wait_ge(z_ok, 1)
                    turn_tok(1, 0, qT_p)

                def turn_tail():
                    pe.wait_ge(kd_ok, 1)
                    for tb in range(TB):
                        for h in range(GH):
                            z = tr(ps[:, 2 + tb, h * DK:(h + 1) * DK], k_tailT[:, h, tile(tb)], eye[:, :])
                    z.then_inc(kt_p, 1)

                def scores():
                    pe.wait_ge(qd_ok, 1)
                    for tb in range(TB):
                        for h in range(GH):
                            z = mm(ps[:, tb, h * P:(h + 1) * P], k_inv[:, h, tile(tb)], q_dec[:, h, tile(tb)],
                                   start=True, stop=True)
                    z.then_inc(att_p, 1)

                def gate1():
                    pe.wait_ge(kt_ok, 1)
                    pe.wait_ge(gb_in, 16 * 2 * DEPTH)
                    for i in range(2):
                        fin_gate(4 + i, 2 + i)

                def update(h):
                    if h == 0:
                        pe.wait_ge(att_ok, 1)
                        pe.wait_ge(in_out, 8)
                    elif h == 1:
                        pe.wait_ge(gate_ok, 2)
                    else:
                        pe.wait_ge(st_ok, h - 1)
                    for c in range(NCH - 1):
                        q = slice(64 * (c % 2), 64 * (c % 2) + 64)
                        z = mm(ps[:, 2 * (h % 2) + c % 2, (c // 2) * DV:(c // 2 + 1) * DV],
                               k_tail[q, c // 2, h, :], g_v[q, c // 2, h * DV:(h + 1) * DV], start=True, stop=True)
                    z.then_inc(u_p, 1)

                def output(i):
                    tb, h0 = i // 2, 2 * (i % 2)
                    pe.wait_ge(st_ok, GH)
                    for h in (h0, h0 + 1):
                        o = ps[:, 2 * tb + h // 2, (h % 2) * DV:(h % 2 + 1) * DV]
                        z = mm(o, att[:, tb, h, :], g_v[:, tb, h * DV:(h + 1) * DV], start=True, stop=True)
                        for c in (2 * tb, 2 * tb + 1):
                            if c == 0:
                                continue
                            q = slice(64 * (c % 2), 64 * (c % 2) + 64)
                            z = mm(o[q], q_dec[:, h, c * L:(c + 1) * L], state[c][:, h, :],
                                   start=False, stop=True, skip_group_check=True)
                    z.then_inc(o_p, 1)

                sides = [{3: glr}, {0: logits, 2: turn_k}, {0: turn_q, 3: turn_tail}, {1: scores, 3: gate1},
                         {u: (lambda h=u: update(h)) for u in range(4)},
                         {u: (lambda i=u: output(i)) for u in range(4)}]
                for n in range(6):
                    if n >= 2:
                        pe.wait_ge(in_out, 2 * (n - 1))
                    project(mix_base[0] + 4 * n, (in_bank(n, 0), in_bank(n, 1)), 0 if n == 0 else None, sides[n])
                pe.wait_ge(in_out, 12)
                for h in range(GH):
                    pe.wait_ge(ot_ok, h + 1)
                    for k in (2 * h, 2 * h + 1):
                        for tb in range(TB):
                            z = tr(ps[:, 4 + h, (k % 2) * SEQ + tb * P:(k % 2) * SEQ + (tb + 1) * P],
                                   o_tok[:, tb, k * P:(k + 1) * P], eye[:, :])
                    z.then_inc(oT_ok, 1)

            def moba():
                def gate1():
                    for i in range(2):
                        fin_gate(16 + i, i)

                def turn_rot(n):
                    pe.wait_ge(rot_ok, n + 1)
                    if n > 0:
                        pe.wait_ge(rT_ok, n)
                    for h in range(4):
                        for tb in range(TB):
                            z = tr(ps[:, 2 + h // 2, (h % 2) * SEQ + tb * P:(h % 2) * SEQ + (tb + 1) * P],
                                   b_r[:, tb, h * HD:(h + 1) * HD], eye[:, :])
                    z.then_inc(rT_p, 1)

                def scores(h):
                    if h == 0:
                        pe.wait_ge(gate_ok, 6)
                    if h >= 2:
                        pe.wait_ge(mx_ok, 2 * (h - 1))
                    pe.wait_ge(rT_ok, 2 if h < 4 else 4)
                    mm(ps[:, h % 2, 0:P], b_qT[:, h, 0:P], b_kT[:, h, 0:P], start=True, stop=True)
                    mm(ps[:, h % 2, P:3 * P], b_qT[:, h, P:2 * P], b_kT[:, h, :], start=True, stop=True
                       ).then_inc(s_p, 1)

                def turn_p(h):
                    pe.wait_ge(pn_ok, h + 1)
                    if h >= 2:
                        pe.wait_ge(pT_ok, h - 1)
                    for i in range(3):
                        z = tr(ps[:, 2 + h % 2, i * P:(i + 1) * P], b_p[:, h % 4, i * P:(i + 1) * P], eye[:, :])
                    z.then_inc(pT_p, 1)

                def values(h):
                    pe.wait_ge(pT_ok, h + 1)
                    o = ps[:, 4 + h // 2, (h % 2) * SEQ:(h % 2 + 1) * SEQ]
                    mm(o, b_v[:, 0, h * HD:(h + 1) * HD], b_pT[:, h % 4, 0:SEQ], start=True, stop=True)
                    z = mm(o[:, P:2 * P], b_v[:, 1, h * HD:(h + 1) * HD], b_pT[:, h % 4, SEQ:3 * P],
                           start=False, stop=True, skip_group_check=True)
                    if h % 2 == 1:
                        z.then_inc(oT_ok, 1)

                sides = [{}, {1: gate1}] + [{3: (lambda n=n: turn_rot(n))} for n in range(4)]
                for n in range(6):
                    if n >= 2:
                        pe.wait_ge(in_out, 12 + 2 * (n - 1))
                    else:
                        pe.wait_ge(x_new, 4)
                    project(mix_base[1] + 4 * n, (in_bank(n, 0), in_bank(n, 1)), 12 if False else (4 * 3 if n == 0 else None), sides[n])
                LAG_T, LAG_V = 2, 3
                for i in range(MH + LAG_V):
                    if i < MH:
                        scores(i)
                    if i == 1:
                        pe.wait_ge(rT_ok, 4)
                    if 0 <= i - LAG_T < MH:
                        turn_p(i - LAG_T)
                    if i == LAG_V:
                        pe.wait_ge(in_out, 24)
                    if i >= LAG_V:
                        values(i - LAG_V)

            pe.wait_ge(vec_in, 16 * N_VEC)
            tr(ps[:, 0, 0:N_ROWS], rows[0:N_ROWS, :], eye[0:N_ROWS, 0:N_ROWS]).then_inc(vec_T, 1)
            pe.wait_ge(vec_ok, 1)
            for b in range(4):
                fin_mod(b, b)
            pe.wait_ge(mod_red, 4)
            for l in range(DEPTH):
                norm(2 * l)
                if l == 0:
                    gla()
                else:
                    moba()
                out_project(l)
                norm(2 * l + 1)
                mlp(l)

        @block.scalar
        def _(act):
            A = nc.scalar.activation
            steps = [0]

            def link(ins):
                steps[0] += 1
                ins.then_inc(act_step, 1)
                act.wait_ge(act_step, steps[0])

            def hi(u, c, round_):
                if c % 2 == 0:
                    act.wait_ge(raw_in[c // 2], 16 * round_ + 16)
                if not (isinstance(u, int) and u < SPLIT):
                    act.wait_ge(unit_used, u - SPLIT + 1)
                A(w_hi[:, c % SPLIT], w_raw[:, c // 2, c % 2], ACT.Copy).then_inc(hi_made, 1)

            def hi_at(u):
                hi(u, u % 8, u // 8)

            def squares(v, tb):
                if v == 0:
                    if tb == 0:
                        act.wait_ge(x_in, 32)
                else:
                    act.wait_ge(x_new, 2 * (v - 1) + tb + 1)
                i = 2 * v + tb
                A(xn[:, tb], x[:, tb], ACT.Square, accum_out=stat[:, S_SS + i:S_SS + i + 1]).then_inc(ss_ok, 1)
                act.wait_ge(ss_ok, i + 1)
                A(stat[:, S_LN + i:S_LN + i + 1], stat[:, S_SS + i:S_SS + i + 1], ACT.Ln, scale=1.0 / D,
                  bias=eps[:, :]).then_inc(ln_ok, 1)
                act.wait_ge(ln_ok, i + 1)
                A(stat[:, S_R0 + i:S_R0 + i + 1], stat[:, S_LN + i:S_LN + i + 1], ACT.Exp, scale=-0.5
                  ).then_inc(r0_ok, 1)

            def modulate(v):
                l, s = v // 2, v % 2
                act.wait_ge(mod_ok, 2 * v + 2)
                for q in range(4):
                    act.wait_ge(xT_ok, 4 * v + 2 * (q // 2) + 1)
                    k = 2 * q
                    bank, at = chunk_at(v, k)
                    A(hT[:, k], ps[:, bank, at:at + SEQ], ACT.Identity,
                      scale=modc[:, l, 2 * s + 1, k:k + 1], bias=modc[:, l, 2 * s, k:k + 1]).then_inc(hA_ok, 1)
                    act.wait_ge(hA_ok, 4 * v + q + 1)
                    act.wait_ge(hD_ok, 4 * v + q + 1)
                    A(a_hi[:, k:k + 2], hT[:, k:k + 2], ACT.Copy).then_inc(ahi_ok, 1)

            def norm(v):
                for tb in range(TB):
                    squares(v, tb)
                u0 = (mix_base, mlp_base)[v % 2][v // 2]
                for u in range(0 if v == 0 else 3, 4):
                    hi_at(u0 + u)
                modulate(v)

            def o_hi(l):
                for q in range(4):
                    act.wait_ge(oT_ok, 4 * l + q + 1)
                    A(a_hi[:, 2 * q:2 * q + 2], ps[:, 4 + q, :], ACT.Copy).then_inc(ahi_ok, 1)

            def gate_out(i, bank, s):
                act.wait_ge(gate_p, i + 1)
                A(gates[:, s, (i % 2) * COLS:(i % 2 + 1) * COLS], ps[:, bank, :], ACT.Copy).then_inc(gate_ok, 1)

            def read_in(l, n, dst, func=ACT.Copy):
                act.wait_ge(unit_used, mix_base[l] + 4 * n + 4)
                for tb in range(TB):
                    A(dst[tb], ps[:, in_bank(n, tb), :], func).then_inc(in_out, 1)

            def gla():
                def glr():
                    act.wait_ge(glr_p, 1)
                    A(glrT[:, :], ps[0:RANK, 0, 0:SEQ], ACT.Copy).then_inc(glr_ok, 1)

                def softplus():
                    act.wait_ge(z_ok, 1)
                    link(A(g_t, g_t, ACT.Exp))
                    A(g_t, g_t, ACT.Ln, bias=1.0).then_inc(ez_ok, 1)

                def decays():
                    act.wait_ge(G_ok, 1)
                    A(g_i, g_s, ACT.Exp, scale=-1.0 / 16).then_inc(eG_ok, 1)
                    A(g_t, g_t, ACT.Exp, scale=1.0 / 16).then_inc(eG_ok, 1)
                    A(g_e, g_s, ACT.Exp, scale=1.0 / 16).then_inc(eG_ok, 1)

                def tail():
                    act.wait_ge(kt_p, 1)
                    for tb in range(TB):
                        z = A(k_tail[:, tb], ps[:, 2 + tb, :].rearrange("p (h d) -> p h d", h=GH), ACT.Copy)
                    z.then_inc(kt_ok, 1)

                def gate1():
                    for i in range(2):
                        gate_out(i, 2 + i, 0)

                def o_squares(i):
                    act.wait_ge(o_p, i + 1)
                    tb, h0 = i // 2, 2 * (i % 2)
                    for h in (h0, h0 + 1):
                        j = S_O + 4 * tb + h
                        A(o_tok[:, tb, h * DV:(h + 1) * DV], ps[:, 2 * tb + h // 2, (h % 2) * DV:(h % 2 + 1) * DV],
                          ACT.Square, accum_out=stat[:, j:j + 1]).then_inc(oss_ok, 1)

                def o_root():
                    act.wait_ge(oss_ok, 8)
                    link(A(stat[:, S_O + 8:S_O + 16], stat[:, S_O:S_O + 8], ACT.Ln, scale=1.0 / DV, bias=eps[:, :]))
                    A(stat[:, S_O + 16:S_O + 24], stat[:, S_O + 8:S_O + 16], ACT.Exp, scale=-0.5).then_inc(or0_ok, 1)

                def k_in():
                    read_in(0, 0, [g_tok[:, 0, tb] for tb in range(TB)])
                    glr()

                tasks = {
                    (1, 3): [k_in],
                    (2, 0): [softplus],
                    (2, 2): [decays],
                    (2, 3): [lambda: read_in(0, 1, [g_tok[:, 1, tb] for tb in range(TB)])],
                    (3, 3): [tail, lambda: read_in(0, 2, [g_v[:, tb, 0:COLS] for tb in range(TB)])],
                    (4, 1): [gate1],
                    (4, 3): [lambda: read_in(0, 3, [g_v[:, tb, COLS:D] for tb in range(TB)])],
                    (5, 3): [lambda: read_in(0, 4, [silu_r[:, tb, 0:COLS] for tb in range(TB)], ACT.Silu)],
                    (6, 0): [lambda: o_squares(0)],
                    (6, 1): [lambda: o_squares(1)],
                    (6, 2): [lambda: o_squares(2)],
                    (6, 3): [lambda: read_in(0, 5, [silu_r[:, tb, COLS:D] for tb in range(TB)], ACT.Silu),
                             lambda: o_squares(3), o_root],
                }
                for n in range(1, 7):
                    for u in range(4):
                        hi_at(mix_base[0] + 4 * n + u)
                        for t in tasks.get((n, u), []):
                            t()
                o_hi(0)

            def moba():
                def stats(n):
                    if n > 0:
                        act.wait_ge(rot_ok, n)
                    read_in(1, n, [b_tok[:, tb] for tb in range(TB)])
                    act.wait_ge(in_out, 12 + 2 * n + 2)
                    for tb in range(TB):
                        z = A(b_u[:, tb], b_tok[:, tb], ACT.Square)
                    z.then_inc(bss_ok, 1)

                def root(n):
                    act.wait_ge(bss_ok, 2 * n + 2)
                    link(A(stat[:, S_O + 8:S_O + 16], stat[:, S_O:S_O + 8], ACT.Ln, scale=1.0 / HD, bias=eps[:, :]))
                    A(stat[:, S_O + 16:S_O + 24], stat[:, S_O + 8:S_O + 16], ACT.Exp, scale=-0.5).then_inc(br0_ok, 1)

                def read_rot(n):
                    act.wait_ge(rT_p, n + 1)
                    dst = (b_kT, b_qT)[n % 2]
                    for i in range(2):
                        z = A(dst[:, 4 * (n // 2) + 2 * i:4 * (n // 2) + 2 * i + 2],
                              ps[:, 2 + i, :].rearrange("p (h t) -> p h t", h=2), ACT.Copy)
                    z.then_inc(rT_ok, 1)

                def read_v(half):
                    read_in(1, 4 + half, [b_v[:, tb, half * COLS:(half + 1) * COLS] for tb in range(TB)])

                def gate1():
                    for i in range(2):
                        gate_out(4 + i, i, 0)

                tasks = {(2, 1): [gate1]}
                for n in range(4):
                    tasks.setdefault((n + 1, 3), []).append(lambda n=n: stats(n))
                    tasks.setdefault((n + 2, 0), []).append(lambda n=n: root(n))
                    tasks.setdefault((n + 3 if n < 3 else 6, 3 if n == 3 else 0), []).append(lambda n=n: read_rot(n))
                tasks[(5, 3)] = [lambda: read_v(0)]
                tasks[(6, 3)] = [lambda: read_v(1), lambda: read_rot(3)]

                for n in range(1, 7):
                    for u in range(4):
                        hi_at(mix_base[1] + 4 * n + u)
                        for t in tasks.get((n, u), []):
                            t()

                def exps(h):
                    act.wait_ge(mx_ok, 2 * h + 2)
                    for i, (a, b) in enumerate(((0, P), (P, 3 * P))):
                        j = S_MX + 6 * h + i
                        z = A(b_p[:, h % 4, a:b], b_p[:, h % 4, a:b], ACT.Exp, scale=-1.0, bias=stat[:, j:j + 1],
                              accum_out=stat[:, j + 2:j + 3])
                    z.then_inc(ex_ok, 1)

                def read_pT(h):
                    act.wait_ge(pT_p, h + 1)
                    if h >= 4:
                        act.wait_ge(oT_ok, 4 + (h - 4) // 2 + 1)
                    A(b_pT[:, h % 4], ps[:, 2 + h % 2, 0:3 * P], ACT.Copy).then_inc(pT_ok, 1)

                for i in range(MH + 2):
                    if i < MH:
                        exps(i)
                    if i >= 2:
                        read_pT(i - 2)
                o_hi(1)

            def out_project(l):
                for u in range(4):
                    hi_at(mix_base[l] + 28 + u)
                for u in range(3):
                    hi_at(mlp_base[l] + u)
                    if u == 1:
                        for i in range(2):
                            gate_out(4 * l + 2 + i, 4 + i, 1)

            def mlp(l):
                base, m0 = mlp_base[l], l * NJ

                def relus(j, u_done):
                    act.wait_ge(unit_used, u_done)
                    for tb in range(TB):
                        A(relu[:, tb], ps[:, tb, :], ACT.Relu).then_inc(relu_ok, 1)

                def square(j, first=False):
                    for b in range(2):
                        act.wait_ge(tr_ok, 2 * (m0 + j) + b + 1)
                        if not first:
                            act.wait_ge(m_ok, 2 * (m0 + j) - 1 + b)
                        A(sq[:, 2 * b:2 * b + 2], ps[:, 2 + b, :].rearrange("p (c t) -> p c t", c=2), ACT.Square
                          ).then_inc(sq_ok, 1)

                def step(u0, round_, j, first=False, more=True, relu_more=True):
                    for c in range(4):
                        hi(u0 + c, c, round_)
                        if c == 1:
                            square(j, first)
                    if relu_more:
                        relus(j + 1, u0)
                    if more:
                        for c in range(4):
                            hi(u0 + 4 + c, 4 + c, round_)

                for u in range(4):
                    hi_at(base + 4 + u)
                    if u == 2:
                        relus(0, base + 4)
                step(base + 8, base // 8 + 1, 0, first=(l == 0))
                with act.Fori(1, NJ - 2) as j:
                    step(8 * j + base + 8, j + base // 8 + 1, j)
                j = NJ - 2
                step(base + 8 * NJ - 8, base // 8 + NJ - 1, j, more=False)
                for c in range(4):
                    hi(base + 8 * NJ - 4 + c, 4 + c, base // 8 + NJ - 1)
                    if c == 1:
                        square(NJ - 1)
                if l == 0:
                    for u in range(3):
                        hi_at(mix_base[1] + u)

            act.wait_ge(vec_ok, 1)
            A(c_act[:, 0], cols[:, C_C:C_C + KC], ACT.Exp, scale=-1.0).then_inc(ec_ok, 1)
            act.wait_ge(sc_arg, 2)
            n = TB * HD // 2
            A(r_w[:, 4:6, 0:n], r_w[:, 2:4, 0:n], ACT.Sin).then_inc(sc_ok, 1)
            act.wait_ge(set_up, 2)
            for l in range(DEPTH):
                norm(2 * l)
                if l == 0:
                    gla()
                else:
                    moba()
                out_project(l)
                norm(2 * l + 1)
                mlp(l)

        @block.vector
        def _(dve):
            V = nc.vector
            steps = [0]

            def link(ins):
                steps[0] += 1
                ins.then_inc(dve_step, 1)
                dve.wait_ge(dve_step, steps[0])

            def lo(u, c):
                dve.wait_ge(hi_made, u + 1)
                V.tensor_tensor(w_lo[:, c % SPLIT], w_raw[:, c // 2, c % 2], w_hi[:, c % SPLIT].bitcast(F32),
                                ALU.subtract).then_inc(lo_made, 1)

            def lo_at(u):
                lo(u, u % 8)

            def ada(b, half, acc=None):
                acc = ada_acc[:, acc_slot(b)] if acc is None else acc
                dve.wait_ge(ada_in[half], 16 * b + 16)
                for k in range(4):
                    w, s = ada_raw[:, half, k], c_act[:, 2, 4 * half + k:4 * half + k + 1]
                    if half == 0 and k == 0:
                        z = V.tensor_scalar(acc, w, s, None, ALU.mult)
                    else:
                        dve.wait_ge(ada_mac, 8 * b + 4 * half + k)
                        z = V.scalar_tensor_tensor(acc, w, s, acc, op0=ALU.mult, op1=ALU.add)
                    z.then_inc(ada_mac, 1)

            def modc_sum(i, b, bank):
                l, vec = b // 12, 2 * ((b % 12) // 6) + ((b % 12) % 6) // 2
                dve.wait_ge(mod_T, i + 1)
                m = modc[:, l, vec]
                V.tensor_reduce(m[:, 4 * (b % 2):4 * (b % 2) + 4], ps[:, bank, :].rearrange("p (a b) -> p a b", a=4),
                                X_AXIS, ALU.add).then_inc(mod_red, 1)
                if b % 2 == 0:
                    return
                dve.wait_ge(mod_red, i + 1)
                at = C_AB + (4 * l + vec) * KC
                z = V.tensor_tensor(m, m, cols[:, at:at + KC], ALU.add)
                if vec % 2 == 1:
                    link(z)
                    g = (C_MLP if vec == 3 else C_MIX) + l * KC
                    z = V.scalar_tensor_tensor(m, m, 1.0, cols[:, g:g + KC], op0=ALU.add, op1=ALU.mult)
                z.then_inc(mod_ok, 1)

            def newton(r, v, b, r0):
                link(V.tensor_tensor(b, v, r0, ALU.mult))
                link(V.tensor_tensor(b, b, r0, ALU.mult))
                link(V.tensor_scalar(b, b, -0.5, 1.5, ALU.mult, ALU.add))
                link(V.tensor_tensor(r, r0, b, ALU.mult))

            def norm(v):
                l, s = v // 2, v % 2
                for tb in range(TB):
                    i = 2 * v + tb
                    dve.wait_ge(ss_ok, i + 1)
                    cl = [stat[:, a + i:a + i + 1] for a in (S_SS, S_R0, S_V, S_B, S_RS)]
                    link(V.tensor_scalar(cl[2], cl[0], 1.0 / D, EPS, ALU.mult, ALU.add))
                    dve.wait_ge(r0_ok, i + 1)
                    newton(cl[4], cl[2], cl[3], cl[1])
                    V.tensor_scalar(xn[:, tb], x[:, tb], cl[4], None, ALU.mult).then_inc(xn_ok, 1)
                    if tb == 1 and v > 0:
                        lo_at((mix_base if s == 0 else mlp_base)[l] + 3)
                if v == 0:
                    startup_mods()

                def odd(q):
                    k = 2 * q + 1
                    bank, at = chunk_at(v, k)
                    dve.wait_ge(xT_ok, 4 * v + 2 * (q // 2) + 2)
                    V.tensor_scalar(hT[:, k], ps[:, bank, at:at + SEQ], modc[:, l, 2 * s + 1, k:k + 1],
                                    modc[:, l, 2 * s, k:k + 1], ALU.mult, ALU.add).then_inc(hD_ok, 1)

                dve.wait_ge(mod_ok, 2 * v + 2)
                odd(0)
                for q in range(4):
                    if q < 3:
                        odd(q + 1)
                    a_low(4 * 3 * l + (8 if s else 0) + q, q, hT[:, 2 * q:2 * q + 2])
                    if v == 0:
                        lo_at(q)

            def a_low(i, q, src):
                dve.wait_ge(ahi_ok, i + 1)
                V.tensor_tensor(a_lo[:, 2 * q:2 * q + 2], src, a_hi[:, 2 * q:2 * q + 2].bitcast(F32),
                                ALU.subtract).then_inc(a_ok, 1)

            def o_low(l):
                for q in range(4):
                    a_low(4 * (3 * l + 1) + q, q, ps[:, 4 + q, :].rearrange("p (c t) -> p c t", c=2))

            def residual(mlp_, s, half, tb, last):
                cs = slice(half * COLS, (half + 1) * COLS)
                t = y_tmp[:, 2 * half + tb]
                link(V.tensor_tensor(t, ps[:, y_bank(mlp_, half, tb), :], gates[:, s, cs], ALU.mult))
                z = V.tensor_tensor(x[:, tb, cs], x[:, tb, cs], t, ALU.add)
                if last:
                    z.then_inc(x_new, 1)

            def out_project(l):
                for u in range(4):
                    lo_at(mix_base[l] + 28 + u)
                    if l == 0 and u == 0:
                        ada(11, 0)
                    if l == 0 and u == 1:
                        ada(11, 1)
                    if u == 3:
                        for i in range(4):
                            modc_sum(4 + 8 * l + i, 12 * l + 6 + i, 4 + i)
                dve.wait_ge(unit_used, mix_base[l] + 28)
                dve.wait_ge(gate_ok, 4 * l + 2)
                for tb in range(TB):
                    residual(0, 0, 0, tb, False)
                for u in range(3):
                    lo_at(mlp_base[l] + u)
                dve.wait_ge(unit_used, mix_base[l] + 32)
                for tb in range(TB):
                    residual(0, 0, 1, tb, True)

            def gla():
                def logits():
                    dve.wait_ge(z_p, 1)
                    for h in range(GH):
                        z = V.tensor_scalar(g_z[:, h], ps[:, h // 2, (h % 2) * SEQ:(h % 2 + 1) * SEQ],
                                            cols[:, C_BG + h:C_BG + h + 1], None, ALU.add)
                    link(z)
                    V.scalar_tensor_tensor(g_t, g_z, -1.0, g_z, op0=ALU.mult, op1=ALU.min).then_inc(z_ok, 1)

                def cumulate():
                    dve.wait_ge(ez_ok, 1)
                    dve.wait_ge(con_in, 64)
                    link(V.scalar_tensor_tensor(g_z, g_z, 0.0, g_t, op0=ALU.min, op1=ALU.subtract))
                    flat = "p h t -> p (h t)"
                    link(V.tensor_tensor_scan(g_s.rearrange(flat), restart.rearrange("p a b -> p (a b)"),
                                              g_z.rearrange(flat), 0.0, ALU.mult, ALU.add))
                    G = g_s.rearrange("p h (c i) -> p (h c) i", i=L)
                    V.tensor_tensor(g_t.rearrange("p h (c i) -> p (h c) i", i=L),
                                    G[:, :, L - 1:L].to_broadcast([P, GH * NCH, L]), G, ALU.subtract).then_inc(G_ok, 1)

                def keys():
                    dve.wait_ge(kT_p, 1)
                    dve.wait_ge(eG_ok, 2)
                    for i in range(2):
                        kT = ps[:, 2 + i, :].rearrange("p (h t) -> p h t", h=2)
                        V.tensor_tensor(k_inv[:, 2 * i:2 * i + 2], kT, g_i[:, 2 * i:2 * i + 2], ALU.mult)
                        z = V.tensor_tensor(k_tailT[:, 2 * i:2 * i + 2], kT, g_t[:, 2 * i:2 * i + 2], ALU.mult)
                    z.then_inc(kd_ok, 1)

                def queries():
                    dve.wait_ge(qT_p, 1)
                    dve.wait_ge(eG_ok, 3)
                    V.tensor_copy(dec[:, :, :], g_e.rearrange("p h (c i) -> p h c i", i=L)[:, :, :, L - 1])
                    for i in range(2):
                        qT = ps[:, i, :].rearrange("p (h t) -> p h t", h=2)
                        z = V.scalar_tensor_tensor(q_dec[:, 2 * i:2 * i + 2], qT, float(DK) ** -0.5,
                                                   g_e[:, 2 * i:2 * i + 2], op0=ALU.mult, op1=ALU.mult)
                    z.then_inc(qd_ok, 1)

                def zero():
                    dve.wait_ge(qd_ok, 1)
                    V.memset(att[:, :, :, :], 0.0).then_inc(zero_ok, 1)

                def masked():
                    dve.wait_ge(zero_ok, 1)
                    dve.wait_ge(att_p, 1)
                    for tb in range(TB):
                        z = V.copy_predicated(att[:, tb], keep[:, None, :].to_broadcast([P, GH, P]),
                                              ps[:, tb, :].rearrange("p (h q) -> p h q", h=GH))
                    z.then_inc(att_ok, 1)

                def states(h):
                    dve.wait_ge(u_p, h + 1)
                    b = 2 * (h % 2)
                    link(V.tensor_copy(state[1][:, h], ps[:, b, 0:DV]))
                    link(V.scalar_tensor_tensor(state[2][:, h], state[1][:, h], dec[:, h, 1:2], ps[:, b + 1, 0:DV],
                                                op0=ALU.mult, op1=ALU.add))
                    V.scalar_tensor_tensor(state[3][:, h], state[2][:, h], dec[:, h, 2:3], ps[:, b, DV:2 * DV],
                                           op0=ALU.mult, op1=ALU.add).then_inc(st_ok, 1)

                def gains(half, tb):
                    r = silu_r[:, tb, half * COLS:(half + 1) * COLS].rearrange("p (h v) -> p h v", h=2)
                    return V.tensor_tensor(r, r, onorm[:, None, :].to_broadcast([P, 2, DV]), ALU.mult)

                def outputs():
                    dve.wait_ge(in_out, 12)
                    for tb in range(TB):
                        z = gains(1, tb)
                    link(z)
                    dve.wait_ge(or0_ok, 1)
                    ss, r0, v, b, r = [stat[:, S_O + a:S_O + a + 8] for a in (0, 16, 24, 32, 40)]
                    link(V.tensor_scalar(v, ss, 1.0 / DV, EPS, ALU.mult, ALU.add))
                    newton(r, v, b, r0)
                    for h in range(GH):
                        for tb in range(TB):
                            hv = slice(h * DV, (h + 1) * DV)
                            z = V.scalar_tensor_tensor(o_tok[:, tb, hv], ps[:, 2 * tb + h // 2, (h % 2) * DV:(h % 2 + 1) * DV],
                                                       r[:, 4 * tb + h:4 * tb + h + 1], silu_r[:, tb, hv],
                                                       op0=ALU.mult, op1=ALU.mult)
                        z.then_inc(ot_ok, 1)

                def gains0():
                    dve.wait_ge(in_out, 10)
                    for tb in range(TB):
                        gains(0, tb)

                tasks = {
                    (2, 0): [logits], (2, 1): [cumulate], (2, 3): [keys], (3, 1): [queries, zero],
                    (4, 1): [masked], (5, 1): [lambda: states(0)], (5, 2): [lambda: states(1)],
                    (5, 3): [lambda: states(2)], (6, 0): [lambda: states(3), gains0], (6, 3): [outputs],
                }
                for n in range(1, 7):
                    for u in range(4):
                        lo_at(mix_base[0] + 4 * n + u)
                        if u in (0, 2):
                            ada(3 + n, u // 2)
                        for t in tasks.get((n, u), []):
                            t()
                ada(10, 0)
                ada(10, 1)
                o_low(0)

            def moba():
                def reduce(n):
                    dve.wait_ge(bss_ok, 2 * n + 1)
                    V.tensor_reduce(stat[:, S_O:S_O + 8].rearrange("p (a b) -> p a b", a=TB),
                                    b_u.rearrange("p a (h d) -> p a h d", h=4), X_AXIS, ALU.add).then_inc(bss_ok, 1)
                    t = tab[:, 1 - n % 2, 0].rearrange("p (a d) -> p a d", a=TB)
                    for tb in range(TB):
                        V.tensor_tensor(b_t[:, tb].rearrange("p (h d) -> p h d", h=4),
                                        b_tok[:, tb].rearrange("p (h d) -> p h d", h=4),
                                        t[:, tb:tb + 1].to_broadcast([P, 4, HD]), ALU.mult).then_inc(dve_step, 1)
                        steps[0] += 1

                def rotate(n):
                    dve.wait_ge(bss_ok, 2 * n + 2)
                    t = tab[:, 1 - n % 2, 1].rearrange("p (a s d) -> p a s d", a=TB, s=2)
                    for tb in range(TB):
                        src = b_tok[:, tb].rearrange("p (h s d) -> p h s d", h=4, s=2)
                        dst = b_u[:, tb].rearrange("p (h s d) -> p h s d", h=4, s=2)
                        for s in range(2):
                            z = V.tensor_tensor(dst[:, :, s], src[:, :, 1 - s],
                                                t[:, tb, s:s + 1].to_broadcast([P, 4, HD // 2]), ALU.mult)
                    link(z)
                    link(V.tensor_tensor(b_t, b_t, b_u, ALU.add))

                def scale(n):
                    dve.wait_ge(br0_ok, n + 1)
                    ss, r0, v, b, r = [stat[:, S_O + a:S_O + a + 8] for a in (0, 16, 24, 32, 40)]
                    link(V.tensor_scalar(v, ss, 1.0 / HD, EPS, ALU.mult, ALU.add))
                    newton(r, v, b, r0)
                    if n > 0:
                        dve.wait_ge(rT_p, n)
                    V.tensor_tensor(b_r.rearrange("p a (h d) -> p (a h) d", h=4),
                                    b_t.rearrange("p a (h d) -> p (a h) d", h=4),
                                    r[:, :, None].to_broadcast([P, 8, HD]), ALU.mult).then_inc(rot_ok, 1)

                tasks = {}
                for n in range(4):
                    tasks[(n + 2, 0)] = [lambda n=n: reduce(n)]
                    tasks[(n + 2, 1)] = [lambda n=n: rotate(n)]
                    tasks[(n + 2, 2)] = [lambda n=n: scale(n)]
                for n in range(1, 7):
                    for u in range(4):
                        lo_at(mix_base[1] + 4 * n + u)
                        if u in (0, 3):
                            for b in ADA_AT[1].get(n, []):
                                ada(b, u // 3)
                        for t in tasks.get((n, u), []):
                            t()

                def top(h):
                    dve.wait_ge(s_p, h + 1)
                    if h >= 4:
                        dve.wait_ge(pT_p, h - 3)
                    for i, (a, b) in enumerate(((0, P), (P, 3 * P))):
                        j = S_MX + 6 * h + i
                        V.tensor_tensor_reduce(b_p[:, h % 4, a:b], ps[:, h % 2, a:b], amask[:, a:b],
                                               -float(HD) ** -0.5, -NEG, ALU.add, ALU.min, stat[:, j:j + 1]
                                               ).then_inc(mx_ok, 1)

                def normal(h):
                    dve.wait_ge(ex_ok, h + 1)
                    j = S_MX + 6 * h
                    link(V.reciprocal(stat[:, j + 4:j + 6], stat[:, j + 2:j + 4]))
                    for i, (a, b) in enumerate(((0, P), (P, 3 * P))):
                        z = V.tensor_scalar(b_p[:, h % 4, a:b], b_p[:, h % 4, a:b], stat[:, j + 4 + i:j + 5 + i], None,
                                            ALU.mult)
                    z.then_inc(pn_ok, 1)

                for i in range(MH + 1):
                    if i < MH:
                        top(i)
                    if i >= 1:
                        normal(i - 1)
                o_low(1)

            def mlp(l):
                base, m0 = mlp_base[l], l * NJ

                def hidden(j, used, first=False):
                    for b in range(2):
                        dve.wait_ge(sq_ok, 2 * (m0 + j) + b + 1)
                        if b == 0 and not first:
                            dve.wait_ge(unit_used, used)
                        V.tensor_copy(m_hi[:, 2 * b:2 * b + 2], sq[:, 2 * b:2 * b + 2]).then_inc(mhi_ok, 1)
                    for b in range(2):
                        dve.wait_ge(mhi_ok, 2 * (m0 + j) + b + 1)
                        V.tensor_tensor(m_lo[:, 2 * b:2 * b + 2], sq[:, 2 * b:2 * b + 2],
                                        m_hi[:, 2 * b:2 * b + 2].bitcast(F32), ALU.subtract).then_inc(m_ok, 1)

                def step(u0, j, first=False, more=True, ada_b=None, ada_slot=None):
                    for c in range(4):
                        lo(u0 + c, c)
                        if c == 1:
                            hidden(j, u0 - 4, first)
                    if more:
                        for c in range(4):
                            lo(u0 + 4 + c, 4 + c)
                            if ada_b is not None and c in (1, 3):
                                ada(ada_b, c // 2, ada_slot)

                if l == 0:
                    dve.wait_ge(gate_p, 4)
                for u in range(4):
                    lo_at(base + 4 + u)
                    if l == 0:
                        ada(12 + u // 2, u % 2)
                first_ada = dict(ada_b=14, ada_slot=ada_acc[:, 2]) if l == 0 else {}
                step(base + 8, 0, first=True, **first_ada)
                with dve.Fori(1, NJ - 2) as j:
                    more = dict(ada_b=j + 14, ada_slot=ada_acc[:, bass.ds(j + 2, 1), :].rearrange("p a n -> p (a n)")
                                ) if l == 0 else {}
                    step(8 * j + base + 8, j, **more)
                step(base + 8 * NJ - 8, NJ - 2, more=False)
                for c in range(4):
                    lo(base + 8 * NJ - 4 + c, 4 + c)
                    if c == 1:
                        hidden(NJ - 1, base + 8 * NJ - 4)
                if l == 0:
                    for i in range(2):
                        modc_sum(8 + i, 12 + i, i)
                dve.wait_ge(gate_ok, 4 * l + 4)
                dve.wait_ge(y_ok, l + 1)
                for half in range(2):
                    residual(1, 1, half, 0, half == 1)
                if l == 0:
                    for i in range(2):
                        modc_sum(10 + i, 14 + i, 2 + i)
                    for u in range(3):
                        lo_at(mix_base[1] + u)
                dve.wait_ge(unit_used, base + 8 * NJ)
                for half in range(2):
                    residual(1, 1, half, 1, half == 1)

            def angles():
                dve.wait_ge(tab_in, 64)
                pos = stat[:, 188:190]
                link(V.tensor_copy(pos, pos_i[:, :]))
                H2 = HD // 2
                ang, n, out = r_w[:, 0, 0:TB * H2], r_w[:, 1, 0:TB * H2], None
                for tb in range(TB):
                    link(V.tensor_scalar(ang[:, tb * H2:(tb + 1) * H2], r_w[:, 7, 0:H2], pos[:, tb:tb + 1], None,
                                         ALU.mult))
                for i, turn in enumerate((0.0, 0.25)):
                    r = r_w[:, 2 + i, 0:TB * H2]
                    src = ang
                    for again in range(2):
                        shift = turn if again == 0 else 0.0
                        link(V.tensor_scalar(n, src, 1.0 / (2.0 * 3.141592653589793), shift, ALU.mult, ALU.add))
                        link(V.tensor_scalar(n, n, MAGIC, None, ALU.add))
                        link(V.tensor_scalar(n, n, -MAGIC, None, ALU.add))
                        for part in TWO_PI:
                            link(V.scalar_tensor_tensor(r, n, -part, src, op0=ALU.mult, op1=ALU.add))
                            src = r
                        if again == 0 and i == 1:
                            link(V.tensor_scalar(r, r, 1.5707963267948966, None, ALU.add))
                    V.tensor_scalar(r, r, 3.1415925, -3.1415925, ALU.min, ALU.max).then_inc(sc_arg, 1)

            def tables():
                dve.wait_ge(sc_ok, 1)
                H2 = HD // 2
                for which in range(2):
                    gain = r_w[:, 6, which * HD:(which + 1) * HD]
                    for tb in range(TB):
                        sin, cos = r_w[:, 4, tb * H2:(tb + 1) * H2], r_w[:, 5, tb * H2:(tb + 1) * H2]
                        o = tab[:, which].rearrange("p a (b s d) -> p a b s d", b=TB, s=2)
                        for s in range(2):
                            V.tensor_tensor(o[:, 0, tb, s], cos, gain[:, s * H2:(s + 1) * H2], ALU.mult)
                            V.scalar_tensor_tensor(o[:, 1, tb, s], sin, 1.0 if s else -1.0,
                                                   gain[:, (1 - s) * H2:(2 - s) * H2], op0=ALU.mult, op1=ALU.mult)

            def startup_mods():
                for i in range(4):
                    modc_sum(i, i, i)

            V.memset(eps[:, :], EPS).then_inc(set_up, 1)
            V.memset(ones[:, :], 1.0).then_inc(set_up, 1)
            dve.wait_ge(vec_T, 1)
            V.tensor_copy(cols[:, 0:N_ROWS], ps[:, 0, 0:N_ROWS]).then_inc(vec_ok, 1)
            dve.wait_ge(ec_ok, 1)
            link(V.tensor_scalar(c_act[:, 1], c_act[:, 0], 1.0, None, ALU.add))
            link(V.reciprocal(c_act[:, 0], c_act[:, 1]))
            link(V.tensor_tensor(c_act[:, 2], cols[:, C_C:C_C + KC], c_act[:, 0], ALU.mult))
            for half in range(2):
                ada(0, half)
            angles()
            for b in range(1, 4):
                for half in range(2):
                    ada(b, half)
            tables()
            for l in range(DEPTH):
                norm(2 * l)
                if l == 0:
                    gla()
                else:
                    moba()
                out_project(l)
                norm(2 * l + 1)
                mlp(l)


_INS = ['x', 'c', 'positions', 'ada_w', 'ada_b', 'norm_mix_g', 'norm_mlp_g', 'gla_w_in', 'gla_w_gate_up',
        'gla_b_gate', 'gla_onorm_g', 'gla_w_out', 'moba_w_in', 'moba_q_norm_g', 'moba_k_norm_g', 'moba_w_out',
        'mlp_w1', 'mlp_w2']
_OUTS = [((1, 256, 1024), 'float32')]


def kernel(**inputs):
    import numpy as _np
    import concourse.bacc as _bacc
    from concourse import mybir as _mybir
    from concourse.bass_utils import run_bass_kernel_spmd as _run

    i = _np.arange(128)
    after = i[:, None] <= i[None, :]
    same = i[:, None] // 64 == i[None, :] // 64
    tri = _np.where(after.T, 0.0, -1.0e30)
    consts = {
        "eye": _np.eye(128, dtype=_np.float32),
        "keep": (after & same).astype(_np.int32),
        "amask": _np.concatenate([tri, _np.zeros((128, 128)), tri], axis=1).astype(_np.float32),
        "restart": (_np.arange(1024) % 64 != 0).astype(_np.float32)[None],
        "invf": (10000.0 ** (-_np.arange(64) / 64.0)).astype(_np.float32)[None],
    }
    nc = _bacc.Bacc("TRN2", target_bir_lowering=False, num_devices=1)
    arrays, args = {}, []
    for name in _INS + list(consts):
        a = _np.ascontiguousarray(inputs[name] if name in inputs else consts[name])
        arrays[f"in_{name}_dram"] = a
        args.append(nc.dram_tensor(f"in_{name}_dram", a.shape, _mybir.dt.from_np(a.dtype), kind="ExternalInput").ap())
    for n, (shape, dtype) in enumerate(_OUTS):
        dt = _mybir.dt.from_np(_np.dtype(dtype))
        args.append(nc.dram_tensor(f"out_{n}_dram", shape, dt, kind="ExternalOutput").ap())
    trunk_kernel(nc, *args)
    r = _run(nc, [arrays], core_ids=[0])
    got = tuple(r.results[0][f"out_{n}_dram"] for n in range(len(_OUTS)))
    return got[0]
```

```python
from contextlib import ExitStack

import concourse.bass as bass
from concourse import mybir

F32 = mybir.dt.float32
F32R = mybir.dt.float32r
I32 = mybir.dt.int32
ALU = mybir.AluOpType
ACT = mybir.ActivationFunctionType
X_AXIS = mybir.AxisListType.X

P = 128
TB = 2
COLS = 512
RAW = 4
SPLIT = 4
UNIT = 1024
ADA_ACC = 8
L = 64
EPS = 1e-6
NEG = -1.0e30
MAGIC = 1.5 * 2.0 ** 23
TWO_PI = (6.28125, 0.0019350051879882812, 3.019916050561733e-07)


def trunk_kernel(nc, x_d, c_d, pos_d, ada_w, ada_b, mix_g, mlp_g, gla_in, gla_up, gla_bg, gla_og,
                 gla_out, moba_in, moba_qg, moba_kg, moba_out, w1_d, w2_d, eye_d, keep_d, amask_d,
                 restart_d, invf_d, out_d):
    DEPTH, D = mix_g.shape
    KC = D // P
    SEQ = x_d.shape[1]
    RANK, HDK = gla_up.shape[1:]
    DV = gla_og.shape[1]
    GH = gla_out.shape[1] // DV
    DK = HDK // GH
    NCH = SEQ // L
    HD = moba_qg.shape[1]
    MH = D // HD
    NJ = w1_d.shape[2] // COLS
    HC = COLS // P
    assert (SEQ, D, DK, HD, DV) == (TB * P, 1024, P, P, 256) and D == 2 * COLS and 2 * GH == MH

    MIX_BLOCKS = 8
    mix_base = [l * 4 * (MIX_BLOCKS + 2 * NJ) for l in range(DEPTH)]
    mlp_base = [b + 4 * MIX_BLOCKS for b in mix_base]
    MIX_IN = [[1, 0, 2, 3, 4, 5], [2, 0, 3, 1, 4, 5]]
    mix_w = [(gla_in[0], gla_out[0]), (moba_in[0], moba_out[0])]
    ADA_AT = [{1: [4], 2: [5], 3: [6], 4: [7], 5: [8], 6: [9], 7: [10, 11]},
              {1: [20], 2: [21], 4: [22], 6: [23]}]

    ctx = ExitStack()
    with ctx:
        def sb(name, shape, dt=F32):
            return ctx.enter_context(nc.sbuf_tensor(name, shape, dt))

        def sem(name):
            return ctx.enter_context(nc.semaphore(name))

        w_raw = sb("w_raw", [P, RAW, 2, UNIT])
        w_hi = sb("w_hi", [P, SPLIT, UNIT], F32R)
        w_lo = sb("w_lo", [P, SPLIT, UNIT], F32R)
        ada_raw = sb("ada_raw", [P, 2, KC // 2, COLS])
        ada_acc = sb("ada_acc", [P, ADA_ACC, COLS])
        x = sb("x", [P, TB, D])
        a_hi = sb("a_hi", [P, KC, SEQ], F32R)
        a_lo = sb("a_lo", [P, KC, SEQ], F32R)
        m_hi = sb("m_hi", [P, HC, SEQ], F32R)
        m_lo = sb("m_lo", [P, HC, SEQ], F32R)
        gates = sb("gates", [P, 2, D])
        eye = sb("eye", [P, P])
        keep = sb("keep", [P, P], I32)
        ones = sb("ones", [P, P])
        rows = sb("rows", [P, P])
        cols = sb("cols", [P, P])
        c_act = sb("c_act", [P, KC])
        modc = sb("modc", [P, DEPTH, 4, KC])
        g_bias = sb("g_bias", [P, D])
        stat = sb("stat", [P, 192])
        eps = sb("eps", [P, 1])
        onorm = sb("onorm", [P, DV])
        amask = sb("amask", [P, 3 * P])
        glr_w = sb("glr_w", [P, KC, RANK])
        glr_up = sb("glr_up", [RANK, HDK])
        glrT = sb("glrT", [RANK, SEQ])
        dec = sb("dec", [P, GH, NCH])
        pos_i = sb("pos_i", [P, TB], I32)
        K1 = 1024
        ARENA = 14 * K1 + 512
        arena = sb("arena", [P, ARENA])

        def area(at, *shape):
            n = 1
            for s in shape:
                n *= s
            assert at + n <= ARENA
            v = arena[:, at:at + n]
            if len(shape) == 2:
                v = v.rearrange("p (a b) -> p a b", a=shape[0])
            elif len(shape) == 3:
                v = v.rearrange("p (a b c) -> p a b c", a=shape[0], b=shape[1])
            return v

        xn = area(0, TB, D)
        hT = area(2 * K1, KC, SEQ)
        y_tmp = area(2 * K1, 2 * TB, COLS)
        relu = area(4 * K1, TB, COLS)
        sq = area(5 * K1, HC, SEQ)
        g_v = area(0, TB, D)
        silu_r = area(2 * K1, TB, D)
        g_tok = area(4 * K1, 2, TB, COLS)
        o_tok = area(4 * K1, TB, D)
        g_z = area(6 * K1, GH, SEQ)
        k_tailT = area(6 * K1, GH, SEQ)
        g_t = area(7 * K1, GH, SEQ)
        g_e = area(8 * K1, GH, SEQ)
        att = area(8 * K1, TB, GH, P)
        g_i = area(9 * K1, GH, SEQ)
        k_inv = area(10 * K1, GH, SEQ)
        q_dec = area(11 * K1, GH, SEQ)
        k_tail = area(12 * K1, TB, GH, DK)
        g_s = area(3 * K1, GH, SEQ)
        state = [None, area(7 * K1, GH, DV), area(9 * K1, GH, DV), area(6 * K1, GH, DV)]
        restart = area(12 * K1, GH * NCH, L)
        b_tok = area(0, TB, COLS)
        b_t = area(1 * K1, TB, COLS)
        b_u = area(2 * K1, TB, COLS)
        b_r = area(3 * K1, TB, COLS)
        b_kT = area(4 * K1, MH, SEQ)
        b_qT = area(6 * K1, MH, SEQ)
        b_v = area(8 * K1, TB, D)
        b_p = area(10 * K1, 4, 3 * P)
        b_pT = area(11 * K1 + 512, 4, 3 * P)
        tab = area(13 * K1 + 512, 2, 2, TB * P)
        r_w = area(7 * K1, 8, TB * P)
        c_rows = area(2 * K1, P)[0:KC]
        ada_pre = [area((4 + 2 * i) * K1, KC // 2, COLS) for i in range(4)]
        ada_row = area(13 * K1, 2, COLS)[0:97]

        ps = ctx.enter_context(nc.psum_tensor("ps", [P, 8, COLS], F32))

        S_SS, S_LN, S_R0, S_V, S_B, S_RS = 0, 8, 16, 24, 32, 40
        S_O = 48
        S_MX = 112

        raw_in = [sem(f"raw_in{i}") for i in range(RAW)]
        ada_in = [sem(f"ada_in{i}") for i in range(2)]
        vec_in, x_in, glr_in, out_sem = sem("vec_in"), sem("x_in"), sem("glr_in"), sem("out_sem")
        tab_in, con_in, gb_in = sem("tab_in"), sem("con_in"), sem("gb_in")
        hi_made, lo_made = sem("hi_made"), sem("lo_made")
        unit_used = sem("unit_used")
        ada_mac = sem("ada_mac")
        set_up = sem("set_up")
        ada_pre_in = [sem(f"ada_pre_in{i}") for i in range(4)]
        ada_pe = sem("ada_pe")
        row_ok = sem("row_ok")
        c_in, c_T, c_ok = sem("c_in"), sem("c_T"), sem("c_ok")
        vec_T, vec_ok = sem("vec_T"), sem("vec_ok")
        mod_T, mod_red, mod_ok = sem("mod_T"), sem("mod_red"), sem("mod_ok")
        gate_p, gate_ok = sem("gate_p"), sem("gate_ok")
        sc_arg, sc_ok = sem("sc_arg"), sem("sc_ok")
        x_new = sem("x_new")
        ss_ok, ln_ok, r0_ok, xn_ok = sem("ss_ok"), sem("ln_ok"), sem("r0_ok"), sem("xn_ok")
        xT_ok, hA_ok, hD_ok = sem("xT_ok"), sem("hA_ok"), sem("hD_ok")
        ahi_ok, a_ok = sem("ahi_ok"), sem("a_ok")
        in_out = sem("in_out")
        relu_ok, tr_ok, sq_ok, mhi_ok, m_ok = (sem("relu_ok"), sem("tr_ok"), sem("sq_ok"),
                                               sem("mhi_ok"), sem("m_ok"))
        y_ok = sem("y_ok")
        dve_step, act_step = sem("dve_step"), sem("act_step")
        oT_ok = sem("oT_ok")
        z_p, kT_p, qT_p, kt_p, att_p, u_p, o_p, glr_p = (sem("z_p"), sem("kT_p"), sem("qT_p"), sem("kt_p"),
                                                         sem("att_p"), sem("u_p"), sem("o_p"), sem("glr_p"))
        glr_ok, z_ok, ez_ok, G_ok, eG_ok, kd_ok, qd_ok = (sem("glr_ok"), sem("z_ok"), sem("ez_ok"), sem("G_ok"),
                                                          sem("eG_ok"), sem("kd_ok"), sem("qd_ok"))
        kt_ok, zero_ok, att_ok, st_ok, oss_ok, or0_ok = (sem("kt_ok"), sem("zero_ok"), sem("att_ok"), sem("st_ok"),
                                                         sem("oss_ok"), sem("or0_ok"))
        on_ok, ot_ok = sem("on_ok"), sem("ot_ok")
        bss_ok, br0_ok, rot_ok, rT_p, rT_ok = (sem("bss_ok"), sem("br0_ok"), sem("rot_ok"), sem("rT_p"),
                                               sem("rT_ok"))
        s_p, mx_ok, ex_ok, pn_ok, pT_p, pT_ok = (sem("s_p"), sem("mx_ok"), sem("ex_ok"), sem("pn_ok"),
                                                 sem("pT_p"), sem("pT_ok"))

        C_MIX, C_MLP = 0, DEPTH * KC
        C_BG = C_MLP + DEPTH * KC
        C_AB = C_BG + GH
        N_ROWS = C_AB + DEPTH * 4 * KC
        N_VEC = 3 + 2 * DEPTH
        ADA_FIRST = [0, 2, 1, 3]
        SETS_SILU_SIN, SETS_LN_EXP = "silu_and_others", "natural_log_exp_and_others"

        def ada_turn(b):
            return b - 4

        def acc_slot(b):
            return (b + 4) % ADA_ACC

        def in_bank(n, tb):
            return 4 + 2 * (n % 2) + tb

        def y_bank(mlp, half, tb):
            return 4 + 2 * tb + half if mlp else 2 * half + tb

        def norm_bank(v):
            return 4 if v % 2 else 0

        def chunk_at(v, k):
            return norm_bank(v) + 2 * (k // 4) + k % 2, ((k % 4) // 2) * SEQ

        block = ctx.enter_context(nc.Block())

        @block.sync
        def _(sp):
            def ada_part(b, half):
                l, n = b // 12, b % 12
                src = ada_w[l, half * 4 * P:(half + 1) * 4 * P, n * COLS:(n + 1) * COLS]
                return src.rearrange("(k p) n -> p k n", p=P)

            def load_ada(b, half):
                if b == 3:
                    sp.wait_ge(ada_pe, half + 1)
                elif b == 4:
                    sp.wait_ge(ada_pe, 6 + half + 1)
                elif b > 4:
                    sp.wait_ge(ada_mac, 8 * ada_turn(b - 1) + 4 * (half + 1))
                sp.dma_start(ada_raw[:, half], ada_part(b, half)).then_inc(ada_in[half], 16)

            def load_pre(i, b):
                for half in range(2):
                    sp.dma_start(ada_pre[2 * i + half], ada_part(b, half)).then_inc(ada_pre_in[2 * i + half], 16)

            def load_piece(m, slot, src):
                if not (isinstance(m, int) and m < RAW):
                    sp.wait_ge(lo_made, 2 * (m - RAW) + 2)
                dst = w_raw[:, slot]
                if src.shape[1] == COLS:
                    dst = dst.rearrange("p u (k n) -> p (u k) n", k=2)
                sp.dma_start(dst, src.rearrange("(k p) n -> p k n", p=P)).then_inc(raw_in[slot], 16)

            sp.dma_start(c_rows[:, :], c_d[0, :].rearrange("(k p) -> k p", p=P)).then_inc(c_in, 16)
            sp.dma_start(eye[:, :], eye_d).then_inc(c_in, 16)
            for half in range(2):
                load_ada(0, half)
            for tb in range(TB):
                sp.dma_start(x[:, tb], x_d[0, tb * P:(tb + 1) * P, :]).then_inc(x_in, 16)

            def vec(at, n, src):
                sp.dma_start(rows[at:at + n, :], src).then_inc(vec_in, 16)

            vec(C_MIX, DEPTH * KC, mix_g.rearrange("l (k p) -> (l k) p", p=P))
            vec(C_MLP, DEPTH * KC, mlp_g.rearrange("l (k p) -> (l k) p", p=P))
            vec(C_BG, GH, gla_bg[0, :].rearrange("(k p) -> k p", p=P))
            for l in range(DEPTH):
                for s in range(2):
                    vec(C_AB + (2 * l + s) * 2 * KC, 2 * KC,
                        ada_b[l, 3 * s * D:(3 * s + 2) * D].rearrange("(k p) -> k p", p=P))

            def constants():
                with nc.allow_non_contiguous_dma(reason="sixteen columns"):
                    sp.dma_start(glr_w[:, :, :],
                                 gla_in[0, :, gla_in.shape[2] - RANK:].rearrange("(k p) n -> p k n", p=P)
                                 ).then_inc(glr_in, 16)
                sp.dma_start(glr_up[:, :], gla_up[0]).then_inc(glr_in, 16)
                sp.dma_start(keep[:, :], keep_d).then_inc(con_in, 16)
                sp.dma_start(amask[:, :], amask_d).then_inc(con_in, 16)
                sp.dma_start(onorm[:, :], gla_og.to_broadcast([P, DV])).then_inc(con_in, 16)
                sp.dma_start(restart.rearrange("p a b -> p (a b)"), restart_d.to_broadcast([P, GH * SEQ])
                             ).then_inc(con_in, 16)
                for l in range(DEPTH):
                    for s in range(2):
                        q = 32 * (2 * l + s)
                        sp.dma_start(g_bias[q:q + 1, :], ada_b[l:l + 1, (3 * s + 2) * D:(3 * s + 3) * D]
                                     ).then_inc(gb_in, 16)

            def rotary_in():
                sp.wait_ge(x_new, 2)
                with nc.allow_non_contiguous_dma(reason="256 numbers"):
                    sp.dma_start(pos_i[:, :], pos_d[0, :].rearrange("(b p) -> p b", p=P)).then_inc(tab_in, 16)
                sp.dma_start(r_w[:, 7, 0:HD // 2], invf_d.to_broadcast([P, HD // 2])).then_inc(tab_in, 16)
                sp.dma_start(r_w[:, 6, 0:HD], moba_qg.to_broadcast([P, HD])).then_inc(tab_in, 16)
                sp.dma_start(r_w[:, 6, HD:2 * HD], moba_kg.to_broadcast([P, HD])).then_inc(tab_in, 16)

            def mixer(l):
                w_in, w_out = mix_w[l]
                for n in range(MIX_BLOCKS):
                    w, c0 = (w_in, MIX_IN[l][n] * COLS) if n < 6 else (w_out, (n - 6) * COLS)
                    if l == 0 and n == 0:
                        load_pre(0, 2)
                    for d in range(2):
                        m = mix_base[l] // 2 + 2 * n + d
                        load_piece(m, m % RAW, w[4 * d * P:4 * (d + 1) * P, c0:c0 + COLS])
                        if l == 0 and n == 0 and d == 0:
                            load_pre(1, 1)
                            for half in range(2):
                                load_ada(3, half)
                    if l == 0 and n == 0:
                        constants()
                    for b in ADA_AT[l].get(n, []):
                        for half in range(2):
                            load_ada(b, half)

            def mlp(l):
                base = mlp_base[l] // 2

                def w1(j, d, m, slot):
                    load_piece(m, slot, w1_d[l, 4 * d * P:4 * (d + 1) * P, bass.ds(j * COLS, COLS)])

                def w2(j, d, m, slot):
                    load_piece(m, slot, w2_d[l, bass.ds(j * COLS + 2 * d * P, 2 * P), :])

                for j in range(2):
                    for d in range(2):
                        w1(j, d, base + 2 * j + d, 2 * j + d)
                    if l == 0:
                        for half in range(2):
                            load_ada(12 + j, half)
                with sp.Fori(0, NJ - 2) as i:
                    for d in range(2):
                        w2(i, d, base + 4 + 4 * i + d, d)
                    for d in range(2):
                        w1(i + 2, d, base + 6 + 4 * i + d, 2 + d)
                    if l == 0:
                        for half in range(2):
                            sp.wait_ge(ada_mac, 8 * i + 8 * ada_turn(13) + 4 * (half + 1))
                            src = ada_w[1, half * 4 * P:(half + 1) * 4 * P, bass.ds((i + 2) * COLS, COLS)]
                            sp.dma_start(ada_raw[:, half], src.rearrange("(k p) n -> p k n", p=P)
                                         ).then_inc(ada_in[half], 16)
                if l == 0:
                    rotary_in()
                for j in range(NJ - 2, NJ):
                    for d in range(2):
                        m = base + 4 + 4 * (NJ - 2) + 2 * (j - NJ + 2) + d
                        w2(j, d, m, m % RAW)

            mixer(0)
            mlp(0)
            mixer(1)
            mlp(1)
            for tb in range(TB):
                sp.wait_ge(x_new, 2 * (2 * DEPTH - 1) + tb + 1)
                sp.dma_start(out_d[0, tb * P:(tb + 1) * P, :], x[:, tb]).then_inc(out_sem, 16)
            sp.wait_ge(out_sem, TB * 16)

        @block.tensor
        def _(pe):
            mm, tr = nc.tensor.matmul, nc.tensor.transpose

            def tile(tb):
                return slice(tb * P, (tb + 1) * P)

            def three(out, hi, lo, slot, wc, first, last):
                mm(out, hi, w_hi[:, slot, wc], start=first, stop=False)
                mm(out, hi, w_lo[:, slot, wc], start=False, stop=False)
                return mm(out, lo, w_hi[:, slot, wc], start=False, stop=last)

            def project(u0, banks, a_wait=None, side={}):
                for u in range(4):
                    pe.wait_ge(lo_made, u0 + u + 1)
                    if a_wait is not None:
                        pe.wait_ge(a_ok, a_wait + u + 1)
                    for k in range(2):
                        for tb in range(TB):
                            z = three(ps[:, banks[tb], :], a_hi[:, 2 * u + k, tile(tb)],
                                      a_lo[:, 2 * u + k, tile(tb)], u, slice(k * COLS, (k + 1) * COLS),
                                      u == 0 and k == 0, u == 3 and k == 1)
                    z.then_inc(unit_used, 1)
                    if u in side:
                        side[u]()

            def fin_mod(b, bank):
                pe.wait_ge(ada_mac, 8 * (ada_turn(b) + 1))
                for q in range(4):
                    z = tr(ps[:, bank, q * P:(q + 1) * P], ada_acc[:, acc_slot(b), q * P:(q + 1) * P], eye[:, :])
                z.then_inc(mod_T, 1)

            def ada_rows(b, half, bank):
                if b in (0, 3):
                    raw = ada_raw[:, half]
                    pe.wait_ge(ada_in[half], 16 if b == 0 else 32)
                else:
                    raw = ada_pre[2 * (2 - b) + half]
                    pe.wait_ge(ada_pre_in[2 * (2 - b) + half], 16)
                for k in range(4):
                    z = mm(ps[32 * k:32 * k + 1, bank, :], c_act[:, 4 * half + k:4 * half + k + 1], raw[:, k],
                           start=half == 0, stop=half == 1)
                z.then_inc(ada_pe, 1)

            def ada_cols(i, bank):
                pe.wait_ge(row_ok, i + 1)
                for q in range(4):
                    z = mm(ps[:, bank, q:q + 1], ada_row[:, i % 2, q * P:(q + 1) * P], ones[0:97, 0:1],
                           start=True, stop=True)
                z.then_inc(mod_T, 1)

            def fin_gate(b, bank):
                q = 32 * (2 * (b // 12) + (b % 12) // 6)
                half = b % 2
                pe.wait_ge(ada_mac, 8 * (ada_turn(b) + 1))
                mm(ps[:, bank, :], ones[:, :], ada_acc[:, acc_slot(b)], start=True, stop=False)
                mm(ps[:, bank, :], ones[q:q + 1, :], g_bias[q:q + 1, half * COLS:(half + 1) * COLS],
                   start=False, stop=True).then_inc(gate_p, 1)

            def norm(v):
                if v == 0:
                    pe.wait_ge(c_ok, 1)
                    pe.wait_ge(set_up, 2)
                    for half in range(2):
                        ada_rows(0, half, 6)
                    pe.wait_ge(vec_in, 16 * N_VEC)
                    tr(ps[:, 5, 0:N_ROWS], rows[0:N_ROWS, :], eye[0:N_ROWS, 0:N_ROWS]).then_inc(vec_T, 1)
                    ada_cols(0, 4)
                for tb in range(TB):
                    pe.wait_ge(xn_ok, 2 * v + tb + 1)
                    for k in range(KC):
                        bank, at = chunk_at(v, k)
                        z = tr(ps[:, bank, at + tb * P:at + (tb + 1) * P], xn[:, tb, k * P:(k + 1) * P], eye[:, :])
                        if tb == TB - 1 and k % 4 >= 2:
                            z.then_inc(xT_ok, 1)
                if v == 0:
                    for half in range(2):
                        ada_rows(2, half, 7)
                    pe.wait_ge(vec_ok, 1)
                    ada_cols(1, 5)

            def out_project(l):
                def shifts():
                    pe.wait_ge(a_ok, 4 * (3 * l + 2))
                    for i in range(4):
                        fin_mod(12 * l + 6 + i, 4 + i)

                def gate():
                    pe.wait_ge(mod_red, 4 + 8 * l + 4)
                    for i in range(2):
                        fin_gate(12 * l + 10 + i, 4 + i)

                u0 = mix_base[l] + 6 * 4
                project(u0, (0, 1), 4 * (3 * l + 1), {3: shifts})
                pe.wait_ge(gate_ok, 4 * l + 2)
                project(u0 + 4, (2, 3), None, {2: gate})

            def mlp(l):
                base, m0 = mlp_base[l], l * NJ

                def turn(j, first=False):
                    pe.wait_ge(relu_ok, 2 * (m0 + j) + 2)
                    if not first:
                        pe.wait_ge(sq_ok, 2 * (m0 + j))
                    for c in range(HC):
                        for tb in range(TB):
                            z = tr(ps[:, 2 + c // 2, (c % 2) * SEQ + tb * P:(c % 2) * SEQ + (tb + 1) * P],
                                   relu[:, tb, c * P:(c + 1) * P], eye[:, :])
                        if c % 2 == 1:
                            z.then_inc(tr_ok, 1)

                def down(u0, j, first):
                    for u in range(4):
                        pe.wait_ge(lo_made, u0 + u + 1)
                        if u % 2 == 0:
                            pe.wait_ge(m_ok, 2 * (m0 + j) + u // 2 + 1)
                        for tb in range(TB):
                            for h in range(2):
                                z = three(ps[:, y_bank(1, h, tb), :], m_hi[:, u, tile(tb)], m_lo[:, u, tile(tb)],
                                          u, slice(h * COLS, (h + 1) * COLS), first and u == 0, False)
                        z.then_inc(unit_used, 1)

                project(base, (0, 1), 4 * (3 * l + 2))
                pe.wait_ge(relu_ok, 2 * m0 + 2)
                project(base + 4, (0, 1), None, {1: lambda: turn(0, first=True)})
                down(base + 8, 0, True)
                with pe.Fori(1, NJ - 1) as j:
                    pe.wait_ge(relu_ok, 2 * j + 2 * m0 + 2)
                    project(8 * j + base + 4, (0, 1), None, {1: lambda: turn(j)})
                    down(8 * j + base + 8, j, False)
                j, u0 = NJ - 1, base + 4 * (2 * NJ - 1)
                turn(j)
                if l == 0:
                    for i in range(2):
                        fin_mod(12 + i, i)
                for tb in range(TB):
                    for u in range(4):
                        if tb == 0:
                            pe.wait_ge(lo_made, u0 + u + 1)
                            if u % 2 == 0:
                                pe.wait_ge(m_ok, 2 * (m0 + j) + u // 2 + 1)
                        for h in range(2):
                            z = three(ps[:, y_bank(1, h, tb), :], m_hi[:, u, tile(tb)], m_lo[:, u, tile(tb)],
                                      u, slice(h * COLS, (h + 1) * COLS), False, u == 3)
                        if tb == 1:
                            z.then_inc(unit_used, 1)
                    if tb == 0:
                        z.then_inc(y_ok, 1)
                        if l == 0:
                            pe.wait_ge(m_ok, 2 * (m0 + j) + 2)
                            for i in range(2):
                                fin_mod(14 + i, 2 + i)

            def gla():
                def glr():
                    pe.wait_ge(glr_in, 32)
                    for k in range(KC):
                        z = mm(ps[0:RANK, 0, 0:SEQ], glr_w[:, k, :], hT[:, k, :], start=k == 0, stop=k == KC - 1)
                    z.then_inc(glr_p, 1)

                def logits():
                    pe.wait_ge(glr_ok, 1)
                    for h in range(GH):
                        z = mm(ps[:, h // 2, (h % 2) * SEQ:(h % 2 + 1) * SEQ], glr_up[:, h * DK:(h + 1) * DK],
                               glrT[:, :], start=True, stop=True)
                    z.then_inc(z_p, 1)

                def turn_tok(which, bank, done):
                    for h in range(GH):
                        for tb in range(TB):
                            z = tr(ps[:, bank + h // 2, (h % 2) * SEQ + tb * P:(h % 2) * SEQ + (tb + 1) * P],
                                   g_tok[:, which, tb, h * DK:(h + 1) * DK], eye[:, :])
                    z.then_inc(done, 1)

                def turn_k():
                    pe.wait_ge(in_out, 2)
                    turn_tok(0, 2, kT_p)

                def turn_q():
                    pe.wait_ge(in_out, 4)
                    pe.wait_ge(z_ok, 1)
                    turn_tok(1, 0, qT_p)

                def turn_tail():
                    pe.wait_ge(kd_ok, 1)
                    for tb in range(TB):
                        for h in range(GH):
                            z = tr(ps[:, 2 + tb, h * DK:(h + 1) * DK], k_tailT[:, h, tile(tb)], eye[:, :])
                    z.then_inc(kt_p, 1)

                def scores():
                    pe.wait_ge(qd_ok, 1)
                    for tb in range(TB):
                        for h in range(GH):
                            z = mm(ps[:, tb, h * P:(h + 1) * P], k_inv[:, h, tile(tb)], q_dec[:, h, tile(tb)],
                                   start=True, stop=True)
                    z.then_inc(att_p, 1)

                def update(h):
                    if h == 0:
                        pe.wait_ge(att_ok, 1)
                        pe.wait_ge(kt_ok, 1)
                        pe.wait_ge(in_out, 6)
                    elif h >= 2:
                        pe.wait_ge(in_out, 8)
                        pe.wait_ge(st_ok, h - 1)
                    for c in range(NCH - 1):
                        q = slice(64 * (c % 2), 64 * (c % 2) + 64)
                        z = mm(ps[:, 2 * (h % 2) + c % 2, (c // 2) * DV:(c // 2 + 1) * DV],
                               k_tail[q, c // 2, h, :], g_v[q, c // 2, h * DV:(h + 1) * DV], start=True, stop=True)
                    z.then_inc(u_p, 1)

                def output(pair):
                    pe.wait_ge(st_ok, 3 + pair)
                    for tb in range(TB):
                        for h in (2 * pair, 2 * pair + 1):
                            o = ps[:, 2 * pair + tb, (h % 2) * DV:(h % 2 + 1) * DV]
                            z = mm(o, att[:, tb, h, :], g_v[:, tb, h * DV:(h + 1) * DV], start=True, stop=True)
                            for c in (2 * tb, 2 * tb + 1):
                                if c == 0:
                                    continue
                                q = slice(64 * (c % 2), 64 * (c % 2) + 64)
                                z = mm(o[q], q_dec[:, h, c * L:(c + 1) * L], state[c][:, h, :],
                                       start=False, stop=True, skip_group_check=True)
                    z.then_inc(o_p, 1)

                def turn_o(pair):
                    pe.wait_ge(in_out, 10 + 2 * pair)
                    pe.wait_ge(ot_ok, pair + 1)
                    for h in (2 * pair, 2 * pair + 1):
                        for k in (2 * h, 2 * h + 1):
                            for tb in range(TB):
                                z = tr(ps[:, 4 + h, (k % 2) * SEQ + tb * P:(k % 2) * SEQ + (tb + 1) * P],
                                       o_tok[:, tb, k * P:(k + 1) * P], eye[:, :])
                        z.then_inc(oT_ok, 1)

                def second_mods():
                    for i in range(2, 4):
                        for half in range(2):
                            ada_rows(ADA_FIRST[i], half, 4 + i)
                        ada_cols(i, 4 + i)

                sides = [{1: second_mods, 3: glr},
                         {0: logits, 2: turn_k},
                         {1: turn_q, 2: turn_tail, 3: scores},
                         {2: lambda: update(0), 3: lambda: update(1)},
                         {0: lambda: update(2), 1: lambda: update(3), 2: lambda: output(0), 3: lambda: output(1)},
                         {}]
                pe.wait_ge(mod_red, 2)
                for n in range(6):
                    if n == 1:
                        pe.wait_ge(mod_red, 4)
                    if n >= 2:
                        pe.wait_ge(in_out, 2 * (n - 1))
                    project(mix_base[0] + 4 * n, (in_bank(n, 0), in_bank(n, 1)), 0 if n == 0 else None, sides[n])
                turn_o(0)
                pe.wait_ge(on_ok, 2)
                pe.wait_ge(gb_in, 16 * 2 * DEPTH)
                for i in range(2):
                    fin_gate(4 + i, 2 + i)
                turn_o(1)

            def moba():
                def gate1():
                    for i in range(2):
                        fin_gate(16 + i, i)

                def turn_rot(n):
                    pe.wait_ge(rot_ok, n + 1)
                    if n > 0:
                        pe.wait_ge(rT_ok, n)
                    for h in range(4):
                        for tb in range(TB):
                            z = tr(ps[:, 2 + h // 2, (h % 2) * SEQ + tb * P:(h % 2) * SEQ + (tb + 1) * P],
                                   b_r[:, tb, h * HD:(h + 1) * HD], eye[:, :])
                    z.then_inc(rT_p, 1)

                def scores(h):
                    if h == 0:
                        pe.wait_ge(gate_ok, 6)
                    if h >= 2:
                        pe.wait_ge(mx_ok, 2 * (h - 1))
                    pe.wait_ge(rT_ok, 2 if h < 4 else 4)
                    mm(ps[:, h % 2, 0:P], b_qT[:, h, 0:P], b_kT[:, h, 0:P], start=True, stop=True)
                    mm(ps[:, h % 2, P:3 * P], b_qT[:, h, P:2 * P], b_kT[:, h, :], start=True, stop=True
                       ).then_inc(s_p, 1)

                def turn_p(h):
                    pe.wait_ge(pn_ok, h + 1)
                    if h >= 2:
                        pe.wait_ge(pT_ok, h - 1)
                    for i in range(3):
                        z = tr(ps[:, 2 + h % 2, i * P:(i + 1) * P], b_p[:, h % 4, i * P:(i + 1) * P], eye[:, :])
                    z.then_inc(pT_p, 1)

                def values(h):
                    pe.wait_ge(pT_ok, h + 1)
                    o = ps[:, 4 + h // 2, (h % 2) * SEQ:(h % 2 + 1) * SEQ]
                    mm(o, b_v[:, 0, h * HD:(h + 1) * HD], b_pT[:, h % 4, 0:SEQ], start=True, stop=True)
                    z = mm(o[:, P:2 * P], b_v[:, 1, h * HD:(h + 1) * HD], b_pT[:, h % 4, SEQ:3 * P],
                           start=False, stop=True, skip_group_check=True)
                    if h % 2 == 1:
                        z.then_inc(oT_ok, 1)

                sides = [{}, {1: gate1}] + [{3: (lambda n=n: turn_rot(n))} for n in range(4)]
                for n in range(6):
                    if n >= 2:
                        pe.wait_ge(in_out, 12 + 2 * (n - 1))
                    else:
                        pe.wait_ge(x_new, 4)
                    project(mix_base[1] + 4 * n, (in_bank(n, 0), in_bank(n, 1)), 4 * 3 if n == 0 else None,
                            sides[n])
                LAG_T, LAG_V = 2, 3
                for i in range(MH + LAG_V):
                    if i < MH:
                        scores(i)
                    if i == 1:
                        pe.wait_ge(rT_ok, 4)
                    if 0 <= i - LAG_T < MH:
                        turn_p(i - LAG_T)
                    if i == LAG_V:
                        pe.wait_ge(in_out, 24)
                    if i >= LAG_V:
                        values(i - LAG_V)

            pe.wait_ge(c_in, 32)
            tr(ps[:, 4, 0:KC], c_rows[:, :], eye[0:KC, 0:KC]).then_inc(c_T, 1)
            for l in range(DEPTH):
                norm(2 * l)
                if l == 0:
                    gla()
                else:
                    moba()
                out_project(l)
                norm(2 * l + 1)
                mlp(l)

        @block.scalar
        def _(act):
            A = nc.scalar.activation
            steps = [0]

            def link(ins):
                steps[0] += 1
                ins.then_inc(act_step, 1)
                act.wait_ge(act_step, steps[0])

            def hi(u, c, round_):
                if c % 2 == 0:
                    act.wait_ge(raw_in[c // 2], 16 * round_ + 16)
                if not (isinstance(u, int) and u < SPLIT):
                    act.wait_ge(unit_used, u - SPLIT + 1)
                A(w_hi[:, c % SPLIT], w_raw[:, c // 2, c % 2], ACT.Copy).then_inc(hi_made, 1)

            def hi_at(u):
                hi(u, u % 8, u // 8)

            def squares(v, tb):
                if v == 0:
                    if tb == 0:
                        act.wait_ge(x_in, 32)
                else:
                    act.wait_ge(x_new, 2 * (v - 1) + tb + 1)
                i = 2 * v + tb
                A(xn[:, tb], x[:, tb], ACT.Square, accum_out=stat[:, S_SS + i:S_SS + i + 1]).then_inc(ss_ok, 1)
                act.wait_ge(ss_ok, i + 1)
                A(stat[:, S_LN + i:S_LN + i + 1], stat[:, S_SS + i:S_SS + i + 1], ACT.Ln, scale=1.0 / D,
                  bias=eps[:, :]).then_inc(ln_ok, 1)
                act.wait_ge(ln_ok, i + 1)
                A(stat[:, S_R0 + i:S_R0 + i + 1], stat[:, S_LN + i:S_LN + i + 1], ACT.Exp, scale=-0.5
                  ).then_inc(r0_ok, 1)

            def modulate(v, quarters):
                l, s = v // 2, v % 2
                for q in quarters:
                    act.wait_ge(mod_ok, 4 * v + (2 if v == 0 and q < 2 else 4))
                    act.wait_ge(xT_ok, 4 * v + 2 * (q // 2) + 1)
                    k = 2 * q
                    bank, at = chunk_at(v, k)
                    A(hT[:, k], ps[:, bank, at:at + SEQ], ACT.Identity,
                      scale=modc[:, l, 2 * s + 1, k:k + 1], bias=modc[:, l, 2 * s, k:k + 1]).then_inc(hA_ok, 1)
                    act.wait_ge(hA_ok, 4 * v + q + 1)
                    act.wait_ge(hD_ok, 4 * v + q + 1)
                    A(a_hi[:, k:k + 2], hT[:, k:k + 2], ACT.Copy).then_inc(ahi_ok, 1)

            def ada_out(i):
                act.wait_ge(ada_pe, 2 * i + 2)
                if i >= 2:
                    act.wait_ge(mod_T, i - 1)
                A(ada_row[:, i % 2], ps[0:97, 6 + i % 2, :], ACT.Copy).then_inc(row_ok, 1)

            def norm(v):
                if v == 0:
                    ada_out(0)
                for tb in range(TB):
                    squares(v, tb)
                u0 = (mix_base, mlp_base)[v % 2][v // 2]
                if v > 0:
                    hi_at(u0 + 3)
                    modulate(v, range(4))
                else:
                    ada_out(1)
                    for u in range(2):
                        hi_at(u)
                    modulate(v, range(2))
                    for i in range(2, 4):
                        ada_out(i)
                    for u in range(2, 4):
                        hi_at(u)
                    modulate(v, range(2, 4))

            def o_hi(l):
                for q in range(4):
                    act.wait_ge(oT_ok, 4 * l + q + 1)
                    A(a_hi[:, 2 * q:2 * q + 2], ps[:, 4 + q, :], ACT.Copy).then_inc(ahi_ok, 1)

            def gate_out(i, bank, s):
                act.wait_ge(gate_p, i + 1)
                A(gates[:, s, (i % 2) * COLS:(i % 2 + 1) * COLS], ps[:, bank, :], ACT.Copy).then_inc(gate_ok, 1)

            def read_in(l, n, dst, func=ACT.Copy):
                act.wait_ge(unit_used, mix_base[l] + 4 * n + 4)
                for tb in range(TB):
                    A(dst[tb], ps[:, in_bank(n, tb), :], func).then_inc(in_out, 1)

            def gla():
                def glr():
                    act.wait_ge(glr_p, 1)
                    A(glrT[:, :], ps[0:RANK, 0, 0:SEQ], ACT.Copy).then_inc(glr_ok, 1)

                def softplus():
                    act.wait_ge(z_ok, 1)
                    link(A(g_t, g_t, ACT.Exp))
                    A(g_t, g_t, ACT.Ln, bias=1.0).then_inc(ez_ok, 1)

                def decays():
                    act.wait_ge(G_ok, 1)
                    A(g_i, g_s, ACT.Exp, scale=-1.0 / 16).then_inc(eG_ok, 1)
                    A(g_t, g_t, ACT.Exp, scale=1.0 / 16).then_inc(eG_ok, 1)
                    A(g_e, g_s, ACT.Exp, scale=1.0 / 16).then_inc(eG_ok, 1)

                def tail():
                    act.wait_ge(kt_p, 1)
                    for tb in range(TB):
                        z = A(k_tail[:, tb], ps[:, 2 + tb, :].rearrange("p (h d) -> p h d", h=GH), ACT.Copy)
                    z.then_inc(kt_ok, 1)

                def gate1():
                    for i in range(2):
                        gate_out(i, 2 + i, 0)

                def o_squares(pair):
                    act.wait_ge(o_p, pair + 1)
                    for tb in range(TB):
                        for h in (2 * pair, 2 * pair + 1):
                            j = S_O + 4 * tb + h
                            A(o_tok[:, tb, h * DV:(h + 1) * DV],
                              ps[:, 2 * pair + tb, (h % 2) * DV:(h % 2 + 1) * DV],
                              ACT.Square, accum_out=stat[:, j:j + 1]).then_inc(oss_ok, 1)

                def o_root():
                    act.wait_ge(oss_ok, 8)
                    link(A(stat[:, S_O + 8:S_O + 16], stat[:, S_O:S_O + 8], ACT.Ln, scale=1.0 / DV, bias=eps[:, :]))
                    A(stat[:, S_O + 16:S_O + 24], stat[:, S_O + 8:S_O + 16], ACT.Exp, scale=-0.5).then_inc(or0_ok, 1)

                def silu_set():
                    nc.scalar.preload_act_table_set(SETS_SILU_SIN)

                def ln_exp_set():
                    nc.scalar.preload_act_table_set(SETS_LN_EXP)

                def k_in():
                    read_in(0, 0, [g_tok[:, 0, tb] for tb in range(TB)])
                    glr()

                tasks = {
                    (1, 3): [k_in],
                    (2, 0): [softplus],
                    (2, 3): [lambda: read_in(0, 1, [g_tok[:, 1, tb] for tb in range(TB)]), decays],
                    (3, 2): [tail],
                    (3, 3): [lambda: read_in(0, 2, [g_v[:, tb, 0:COLS] for tb in range(TB)])],
                    (4, 3): [lambda: read_in(0, 3, [g_v[:, tb, COLS:D] for tb in range(TB)])],
                    (5, 2): [lambda: o_squares(0)],
                    (5, 3): [lambda: o_squares(1), o_root, silu_set,
                             lambda: read_in(0, 4, [silu_r[:, tb, 0:COLS] for tb in range(TB)], ACT.Silu)],
                    (6, 3): [lambda: read_in(0, 5, [silu_r[:, tb, COLS:D] for tb in range(TB)], ACT.Silu),
                             ln_exp_set, gate1],
                }
                for n in range(1, 7):
                    for u in range(4):
                        hi_at(mix_base[0] + 4 * n + u)
                        for t in tasks.get((n, u), []):
                            t()
                o_hi(0)

            def moba():
                def stats(n):
                    if n > 0:
                        act.wait_ge(rot_ok, n)
                    read_in(1, n, [b_tok[:, tb] for tb in range(TB)])
                    act.wait_ge(in_out, 12 + 2 * n + 2)
                    for tb in range(TB):
                        z = A(b_u[:, tb], b_tok[:, tb], ACT.Square)
                    z.then_inc(bss_ok, 1)

                def root(n):
                    act.wait_ge(bss_ok, 2 * n + 2)
                    link(A(stat[:, S_O + 8:S_O + 16], stat[:, S_O:S_O + 8], ACT.Ln, scale=1.0 / HD, bias=eps[:, :]))
                    A(stat[:, S_O + 16:S_O + 24], stat[:, S_O + 8:S_O + 16], ACT.Exp, scale=-0.5).then_inc(br0_ok, 1)

                def read_rot(n):
                    act.wait_ge(rT_p, n + 1)
                    dst = (b_kT, b_qT)[n % 2]
                    for i in range(2):
                        z = A(dst[:, 4 * (n // 2) + 2 * i:4 * (n // 2) + 2 * i + 2],
                              ps[:, 2 + i, :].rearrange("p (h t) -> p h t", h=2), ACT.Copy)
                    z.then_inc(rT_ok, 1)

                def read_v(half):
                    read_in(1, 4 + half, [b_v[:, tb, half * COLS:(half + 1) * COLS] for tb in range(TB)])

                def gate1():
                    for i in range(2):
                        gate_out(4 + i, i, 0)

                tasks = {(2, 1): [gate1]}
                for n in range(4):
                    tasks.setdefault((n + 1, 3), []).append(lambda n=n: stats(n))
                    tasks.setdefault((n + 2, 0), []).append(lambda n=n: root(n))
                    tasks.setdefault((n + 3 if n < 3 else 6, 3 if n == 3 else 0), []).append(lambda n=n: read_rot(n))
                tasks[(5, 3)] = [lambda: read_v(0)]
                tasks[(6, 3)] = [lambda: read_v(1), lambda: read_rot(3)]

                for n in range(1, 7):
                    for u in range(4):
                        hi_at(mix_base[1] + 4 * n + u)
                        for t in tasks.get((n, u), []):
                            t()

                def exps(h):
                    act.wait_ge(mx_ok, 2 * h + 2)
                    for i, (a, b) in enumerate(((0, P), (P, 3 * P))):
                        j = S_MX + 6 * h + i
                        z = A(b_p[:, h % 4, a:b], b_p[:, h % 4, a:b], ACT.Exp, scale=-1.0, bias=stat[:, j:j + 1],
                              accum_out=stat[:, j + 2:j + 3])
                    z.then_inc(ex_ok, 1)

                def read_pT(h):
                    act.wait_ge(pT_p, h + 1)
                    if h >= 4:
                        act.wait_ge(oT_ok, 4 + (h - 4) // 2 + 1)
                    A(b_pT[:, h % 4], ps[:, 2 + h % 2, 0:3 * P], ACT.Copy).then_inc(pT_ok, 1)

                for i in range(MH + 2):
                    if i < MH:
                        exps(i)
                    if i >= 2:
                        read_pT(i - 2)
                o_hi(1)

            def out_project(l):
                for u in range(4):
                    hi_at(mix_base[l] + 28 + u)
                for u in range(3):
                    hi_at(mlp_base[l] + u)
                    if u == 1:
                        for i in range(2):
                            gate_out(4 * l + 2 + i, 4 + i, 1)

            def mlp(l):
                base, m0 = mlp_base[l], l * NJ

                def relus(j, u_done):
                    act.wait_ge(unit_used, u_done)
                    for tb in range(TB):
                        A(relu[:, tb], ps[:, tb, :], ACT.Relu).then_inc(relu_ok, 1)

                def square(j, first=False):
                    for b in range(2):
                        act.wait_ge(tr_ok, 2 * (m0 + j) + b + 1)
                        if not first:
                            act.wait_ge(m_ok, 2 * (m0 + j) - 1 + b)
                        A(sq[:, 2 * b:2 * b + 2], ps[:, 2 + b, :].rearrange("p (c t) -> p c t", c=2), ACT.Square
                          ).then_inc(sq_ok, 1)

                def step(u0, round_, j, first=False, more=True, relu_more=True):
                    for c in range(4):
                        hi(u0 + c, c, round_)
                        if c == 1:
                            square(j, first)
                    if relu_more:
                        relus(j + 1, u0)
                    if more:
                        for c in range(4):
                            hi(u0 + 4 + c, 4 + c, round_)

                for u in range(4):
                    hi_at(base + 4 + u)
                    if u == 2:
                        relus(0, base + 4)
                step(base + 8, base // 8 + 1, 0, first=(l == 0))
                with act.Fori(1, NJ - 2) as j:
                    step(8 * j + base + 8, j + base // 8 + 1, j)
                j = NJ - 2
                step(base + 8 * NJ - 8, base // 8 + NJ - 1, j, more=False)
                for c in range(4):
                    hi(base + 8 * NJ - 4 + c, 4 + c, base // 8 + NJ - 1)
                    if c == 1:
                        square(NJ - 1)
                        if l == 0:
                            sines()
                if l == 0:
                    for u in range(3):
                        hi_at(mix_base[1] + u)

            def sines():
                nc.scalar.preload_act_table_set(SETS_SILU_SIN)
                act.wait_ge(sc_arg, 1)
                n = TB * HD // 2
                A(r_w[:, 4:6, 0:n], r_w[:, 2:4, 0:n], ACT.Sin).then_inc(sc_ok, 1)
                nc.scalar.preload_act_table_set(SETS_LN_EXP)

            nc.scalar.preload_act_table_set(SETS_SILU_SIN)
            act.wait_ge(c_T, 1)
            A(c_act[:, :], ps[:, 4, 0:KC], ACT.Silu).then_inc(c_ok, 1)
            nc.scalar.preload_act_table_set(SETS_LN_EXP)
            act.wait_ge(set_up, 2)
            for l in range(DEPTH):
                norm(2 * l)
                if l == 0:
                    gla()
                else:
                    moba()
                out_project(l)
                norm(2 * l + 1)
                mlp(l)

        @block.vector
        def _(dve):
            V = nc.vector
            steps = [0]

            def link(ins):
                steps[0] += 1
                ins.then_inc(dve_step, 1)
                dve.wait_ge(dve_step, steps[0])

            def lo(u, c):
                dve.wait_ge(hi_made, u + 1)
                V.tensor_tensor(w_lo[:, c % SPLIT], w_raw[:, c // 2, c % 2], w_hi[:, c % SPLIT].bitcast(F32),
                                ALU.subtract).then_inc(lo_made, 1)

            def lo_at(u):
                lo(u, u % 8)

            def ada(b, half, acc=None):
                acc = ada_acc[:, acc_slot(b)] if acc is None else acc
                t = ada_turn(b)
                dve.wait_ge(ada_in[half], 16 * (b - 1))
                raw = ada_raw[:, half]
                for k in range(4):
                    w, s = raw[:, k], c_act[:, 4 * half + k:4 * half + k + 1]
                    if half == 0 and k == 0:
                        z = V.tensor_scalar(acc, w, s, None, ALU.mult)
                    else:
                        dve.wait_ge(ada_mac, 8 * t + 4 * half + k)
                        z = V.scalar_tensor_tensor(acc, w, s, acc, op0=ALU.mult, op1=ALU.add)
                    z.then_inc(ada_mac, 1)

            def modc_sum(i, b, bank):
                l, vec = b // 12, 2 * ((b % 12) // 6) + ((b % 12) % 6) // 2
                h = slice(4 * (b % 2), 4 * (b % 2) + 4)
                m = modc[:, l, vec, h]
                dve.wait_ge(mod_T, i + 1)
                if b < 4:
                    V.tensor_copy(m, ps[:, bank, 0:4]).then_inc(mod_red, 1)
                else:
                    V.tensor_reduce(m, ps[:, bank, :].rearrange("p (a b) -> p a b", a=4), X_AXIS, ALU.add
                                    ).then_inc(mod_red, 1)
                dve.wait_ge(mod_red, i + 1)
                at = C_AB + (4 * l + vec) * KC + h.start
                z = V.tensor_tensor(m, m, cols[:, at:at + 4], ALU.add)
                if vec % 2 == 1:
                    link(z)
                    g = (C_MLP if vec == 3 else C_MIX) + l * KC + h.start
                    z = V.scalar_tensor_tensor(m, m, 1.0, cols[:, g:g + 4], op0=ALU.add, op1=ALU.mult)
                z.then_inc(mod_ok, 1)

            def newton(r, v, b, r0):
                link(V.tensor_tensor(b, v, r0, ALU.mult))
                link(V.tensor_tensor(b, b, r0, ALU.mult))
                link(V.tensor_scalar(b, b, -0.5, 1.5, ALU.mult, ALU.add))
                link(V.tensor_tensor(r, r0, b, ALU.mult))

            def norm(v):
                l, s = v // 2, v % 2
                for tb in range(TB):
                    if v == 0 and tb == 0:
                        dve.wait_ge(x_in, 32)
                    i = 2 * v + tb
                    dve.wait_ge(ss_ok, i + 1)
                    cl = [stat[:, a + i:a + i + 1] for a in (S_SS, S_R0, S_V, S_B, S_RS)]
                    link(V.tensor_scalar(cl[2], cl[0], 1.0 / D, EPS, ALU.mult, ALU.add))
                    dve.wait_ge(r0_ok, i + 1)
                    newton(cl[4], cl[2], cl[3], cl[1])
                    V.tensor_scalar(xn[:, tb], x[:, tb], cl[4], None, ALU.mult).then_inc(xn_ok, 1)
                    if tb == 1 and v > 0:
                        lo_at((mix_base if s == 0 else mlp_base)[l] + 3)
                if v == 0:
                    dve.wait_ge(vec_T, 1)
                    V.tensor_copy(cols[:, 0:N_ROWS], ps[:, 5, 0:N_ROWS]).then_inc(vec_ok, 1)
                    dve.wait_ge(vec_ok, 1)

                def odd(q):
                    k = 2 * q + 1
                    bank, at = chunk_at(v, k)
                    dve.wait_ge(xT_ok, 4 * v + 2 * (q // 2) + 2)
                    V.tensor_scalar(hT[:, k], ps[:, bank, at:at + SEQ], modc[:, l, 2 * s + 1, k:k + 1],
                                    modc[:, l, 2 * s, k:k + 1], ALU.mult, ALU.add).then_inc(hD_ok, 1)

                def quarters(qs):
                    odd(qs[0])
                    for q in qs:
                        if q + 1 in qs:
                            odd(q + 1)
                        a_low(4 * 3 * l + (8 if s else 0) + q, q, hT[:, 2 * q:2 * q + 2])
                        if v == 0:
                            lo_at(q)

                if v == 0:
                    modc_sum(0, 0, 4)
                    modc_sum(1, 2, 5)
                    dve.wait_ge(mod_ok, 2)
                    quarters(range(2))
                    modc_sum(2, 1, 6)
                    modc_sum(3, 3, 7)
                    dve.wait_ge(mod_ok, 4)
                    quarters(range(2, 4))
                else:
                    dve.wait_ge(mod_ok, 4 * v + 4)
                    quarters(range(4))

            def a_low(i, q, src):
                dve.wait_ge(ahi_ok, i + 1)
                V.tensor_tensor(a_lo[:, 2 * q:2 * q + 2], src, a_hi[:, 2 * q:2 * q + 2].bitcast(F32),
                                ALU.subtract).then_inc(a_ok, 1)

            def o_low(l):
                for q in range(4):
                    a_low(4 * (3 * l + 1) + q, q, ps[:, 4 + q, :].rearrange("p (c t) -> p c t", c=2))

            def residual(mlp_, s, half, tb, last):
                cs = slice(half * COLS, (half + 1) * COLS)
                t = y_tmp[:, 2 * half + tb]
                link(V.tensor_tensor(t, ps[:, y_bank(mlp_, half, tb), :], gates[:, s, cs], ALU.mult))
                z = V.tensor_tensor(x[:, tb, cs], x[:, tb, cs], t, ALU.add)
                if last:
                    z.then_inc(x_new, 1)

            def out_project(l):
                for u in range(4):
                    if l == 0:
                        ada(10 + u // 2, u % 2)
                    lo_at(mix_base[l] + 28 + u)
                    if u == 3:
                        for i in range(4):
                            modc_sum(4 + 8 * l + i, 12 * l + 6 + i, 4 + i)
                dve.wait_ge(unit_used, mix_base[l] + 28)
                dve.wait_ge(gate_ok, 4 * l + 2)
                for tb in range(TB):
                    residual(0, 0, 0, tb, False)
                for u in range(3):
                    lo_at(mlp_base[l] + u)
                dve.wait_ge(unit_used, mix_base[l] + 32)
                for tb in range(TB):
                    residual(0, 0, 1, tb, True)

            def gla():
                def logits():
                    dve.wait_ge(z_p, 1)
                    for h in range(GH):
                        z = V.tensor_scalar(g_z[:, h], ps[:, h // 2, (h % 2) * SEQ:(h % 2 + 1) * SEQ],
                                            cols[:, C_BG + h:C_BG + h + 1], None, ALU.add)
                    link(z)
                    V.scalar_tensor_tensor(g_t, g_z, -1.0, g_z, op0=ALU.mult, op1=ALU.min).then_inc(z_ok, 1)

                def cumulate():
                    dve.wait_ge(ez_ok, 1)
                    dve.wait_ge(con_in, 64)
                    link(V.scalar_tensor_tensor(g_z, g_z, 0.0, g_t, op0=ALU.min, op1=ALU.subtract))
                    flat = "p h t -> p (h t)"
                    link(V.tensor_tensor_scan(g_s.rearrange(flat), restart.rearrange("p a b -> p (a b)"),
                                              g_z.rearrange(flat), 0.0, ALU.mult, ALU.add))
                    G = g_s.rearrange("p h (c i) -> p (h c) i", i=L)
                    V.tensor_tensor(g_t.rearrange("p h (c i) -> p (h c) i", i=L),
                                    G[:, :, L - 1:L].to_broadcast([P, GH * NCH, L]), G, ALU.subtract).then_inc(G_ok, 1)

                def keys():
                    dve.wait_ge(kT_p, 1)
                    dve.wait_ge(eG_ok, 2)
                    for i in range(2):
                        kT = ps[:, 2 + i, :].rearrange("p (h t) -> p h t", h=2)
                        V.tensor_tensor(k_inv[:, 2 * i:2 * i + 2], kT, g_i[:, 2 * i:2 * i + 2], ALU.mult)
                        z = V.tensor_tensor(k_tailT[:, 2 * i:2 * i + 2], kT, g_t[:, 2 * i:2 * i + 2], ALU.mult)
                    z.then_inc(kd_ok, 1)

                def queries():
                    dve.wait_ge(qT_p, 1)
                    dve.wait_ge(eG_ok, 3)
                    V.tensor_copy(dec[:, :, :], g_e.rearrange("p h (c i) -> p h c i", i=L)[:, :, :, L - 1])
                    for i in range(2):
                        qT = ps[:, i, :].rearrange("p (h t) -> p h t", h=2)
                        z = V.scalar_tensor_tensor(q_dec[:, 2 * i:2 * i + 2], qT, float(DK) ** -0.5,
                                                   g_e[:, 2 * i:2 * i + 2], op0=ALU.mult, op1=ALU.mult)
                    z.then_inc(qd_ok, 1)

                def zero():
                    dve.wait_ge(qd_ok, 1)
                    V.memset(att[:, :, :, :], 0.0).then_inc(zero_ok, 1)

                def masked():
                    dve.wait_ge(zero_ok, 1)
                    dve.wait_ge(att_p, 1)
                    for tb in range(TB):
                        z = V.copy_predicated(att[:, tb], keep[:, None, :].to_broadcast([P, GH, P]),
                                              ps[:, tb, :].rearrange("p (h q) -> p h q", h=GH))
                    z.then_inc(att_ok, 1)

                def states(h):
                    dve.wait_ge(u_p, h + 1)
                    b = 2 * (h % 2)
                    link(V.tensor_copy(state[1][:, h], ps[:, b, 0:DV]))
                    link(V.scalar_tensor_tensor(state[2][:, h], state[1][:, h], dec[:, h, 1:2], ps[:, b + 1, 0:DV],
                                                op0=ALU.mult, op1=ALU.add))
                    V.scalar_tensor_tensor(state[3][:, h], state[2][:, h], dec[:, h, 2:3], ps[:, b, DV:2 * DV],
                                           op0=ALU.mult, op1=ALU.add).then_inc(st_ok, 1)

                def o_scales():
                    dve.wait_ge(or0_ok, 1)
                    ss, r0, v, b, r = [stat[:, S_O + a:S_O + a + 8] for a in (0, 16, 24, 32, 40)]
                    link(V.tensor_scalar(v, ss, 1.0 / DV, EPS, ALU.mult, ALU.add))
                    newton(r, v, b, r0)

                def normed(pair):
                    r = stat[:, S_O + 40:S_O + 48]
                    for tb in range(TB):
                        for h in (2 * pair, 2 * pair + 1):
                            z = V.scalar_tensor_tensor(o_tok[:, tb, h * DV:(h + 1) * DV],
                                                       ps[:, 2 * pair + tb, (h % 2) * DV:(h % 2 + 1) * DV],
                                                       r[:, 4 * tb + h:4 * tb + h + 1], onorm[:, :],
                                                       op0=ALU.mult, op1=ALU.mult)
                    z.then_inc(on_ok, 1)

                def gated(pair):
                    cs = slice(pair * COLS, (pair + 1) * COLS)
                    dve.wait_ge(in_out, 10 + 2 * pair)
                    dve.wait_ge(on_ok, pair + 1)
                    for tb in range(TB):
                        z = V.tensor_tensor(o_tok[:, tb, cs], o_tok[:, tb, cs], silu_r[:, tb, cs], ALU.mult)
                    z.then_inc(ot_ok, 1)

                tasks = {
                    (2, 0): [logits], (2, 1): [cumulate], (2, 3): [keys], (3, 1): [queries, zero],
                    (3, 3): [masked], (4, 2): [lambda: states(0)], (4, 3): [lambda: states(1)],
                    (5, 0): [lambda: states(2)], (5, 1): [lambda: states(3)],
                    (6, 0): [o_scales, lambda: normed(0), lambda: normed(1)],
                    (6, 2): [lambda: gated(0)],
                    (6, 3): [lambda: gated(1)],
                }
                for n in range(1, 7):
                    for u in range(4):
                        lo_at(mix_base[0] + 4 * n + u)
                        for t in tasks.get((n, u), []):
                            t()
                        if u in (0, 2):
                            ada(3 + n, u // 2)
                o_low(0)

            def moba():
                def reduce(n):
                    dve.wait_ge(bss_ok, 2 * n + 1)
                    V.tensor_reduce(stat[:, S_O:S_O + 8].rearrange("p (a b) -> p a b", a=TB),
                                    b_u.rearrange("p a (h d) -> p a h d", h=4), X_AXIS, ALU.add).then_inc(bss_ok, 1)
                    t = tab[:, 1 - n % 2, 0].rearrange("p (a d) -> p a d", a=TB)
                    for tb in range(TB):
                        V.tensor_tensor(b_t[:, tb].rearrange("p (h d) -> p h d", h=4),
                                        b_tok[:, tb].rearrange("p (h d) -> p h d", h=4),
                                        t[:, tb:tb + 1].to_broadcast([P, 4, HD]), ALU.mult).then_inc(dve_step, 1)
                        steps[0] += 1

                def rotate(n):
                    dve.wait_ge(bss_ok, 2 * n + 2)
                    t = tab[:, 1 - n % 2, 1].rearrange("p (a s d) -> p a s d", a=TB, s=2)
                    for tb in range(TB):
                        src = b_tok[:, tb].rearrange("p (h s d) -> p h s d", h=4, s=2)
                        dst = b_u[:, tb].rearrange("p (h s d) -> p h s d", h=4, s=2)
                        for s in range(2):
                            z = V.tensor_tensor(dst[:, :, s], src[:, :, 1 - s],
                                                t[:, tb, s:s + 1].to_broadcast([P, 4, HD // 2]), ALU.mult)
                    link(z)
                    link(V.tensor_tensor(b_t, b_t, b_u, ALU.add))

                def scale(n):
                    dve.wait_ge(br0_ok, n + 1)
                    ss, r0, v, b, r = [stat[:, S_O + a:S_O + a + 8] for a in (0, 16, 24, 32, 40)]
                    link(V.tensor_scalar(v, ss, 1.0 / HD, EPS, ALU.mult, ALU.add))
                    newton(r, v, b, r0)
                    if n > 0:
                        dve.wait_ge(rT_p, n)
                    V.tensor_tensor(b_r.rearrange("p a (h d) -> p (a h) d", h=4),
                                    b_t.rearrange("p a (h d) -> p (a h) d", h=4),
                                    r[:, :, None].to_broadcast([P, 8, HD]), ALU.mult).then_inc(rot_ok, 1)

                tasks = {}
                for n in range(4):
                    tasks[(n + 2, 0)] = [lambda n=n: reduce(n)]
                    tasks[(n + 2, 1)] = [lambda n=n: rotate(n)]
                    tasks[(n + 2, 2)] = [lambda n=n: scale(n)]
                for n in range(1, 7):
                    for u in range(4):
                        lo_at(mix_base[1] + 4 * n + u)
                        if u in (0, 3):
                            for b in ADA_AT[1].get(n, []):
                                ada(b, u // 3)
                        for t in tasks.get((n, u), []):
                            t()

                def top(h):
                    dve.wait_ge(s_p, h + 1)
                    if h >= 4:
                        dve.wait_ge(pT_p, h - 3)
                    for i, (a, b) in enumerate(((0, P), (P, 3 * P))):
                        j = S_MX + 6 * h + i
                        V.tensor_tensor_reduce(b_p[:, h % 4, a:b], ps[:, h % 2, a:b], amask[:, a:b],
                                               -float(HD) ** -0.5, -NEG, ALU.add, ALU.min, stat[:, j:j + 1]
                                               ).then_inc(mx_ok, 1)

                def normal(h):
                    dve.wait_ge(ex_ok, h + 1)
                    j = S_MX + 6 * h
                    link(V.reciprocal(stat[:, j + 4:j + 6], stat[:, j + 2:j + 4]))
                    for i, (a, b) in enumerate(((0, P), (P, 3 * P))):
                        z = V.tensor_scalar(b_p[:, h % 4, a:b], b_p[:, h % 4, a:b], stat[:, j + 4 + i:j + 5 + i], None,
                                            ALU.mult)
                    z.then_inc(pn_ok, 1)

                for i in range(MH + 1):
                    if i < MH:
                        top(i)
                    if i >= 1:
                        normal(i - 1)
                o_low(1)

            def mlp(l):
                base, m0 = mlp_base[l], l * NJ

                def hidden(j, used, first=False):
                    for b in range(2):
                        dve.wait_ge(sq_ok, 2 * (m0 + j) + b + 1)
                        if b == 0 and not first:
                            dve.wait_ge(unit_used, used)
                        V.tensor_copy(m_hi[:, 2 * b:2 * b + 2], sq[:, 2 * b:2 * b + 2]).then_inc(mhi_ok, 1)
                    for b in range(2):
                        dve.wait_ge(mhi_ok, 2 * (m0 + j) + b + 1)
                        V.tensor_tensor(m_lo[:, 2 * b:2 * b + 2], sq[:, 2 * b:2 * b + 2],
                                        m_hi[:, 2 * b:2 * b + 2].bitcast(F32), ALU.subtract).then_inc(m_ok, 1)

                def step(u0, j, first=False, more=True, ada_b=None, ada_slot=None):
                    for c in range(4):
                        lo(u0 + c, c)
                        if c == 1:
                            hidden(j, u0 - 4, first)
                    if more:
                        for c in range(4):
                            lo(u0 + 4 + c, 4 + c)
                            if ada_b is not None and c in (1, 3):
                                ada(ada_b, c // 2, ada_slot)

                if l == 0:
                    dve.wait_ge(gate_p, 4)
                for u in range(4):
                    lo_at(base + 4 + u)
                    if l == 0:
                        ada(12 + u // 2, u % 2)
                first_ada = dict(ada_b=14, ada_slot=ada_acc[:, 2]) if l == 0 else {}
                step(base + 8, 0, first=True, **first_ada)
                with dve.Fori(1, NJ - 2) as j:
                    more = dict(ada_b=j + 14, ada_slot=ada_acc[:, bass.ds(j + 2, 1), :].rearrange("p a n -> p (a n)")
                                ) if l == 0 else {}
                    step(8 * j + base + 8, j, **more)
                step(base + 8 * NJ - 8, NJ - 2, more=False)
                if l == 0:
                    angles()
                for c in range(4):
                    lo(base + 8 * NJ - 4 + c, 4 + c)
                    if c == 1:
                        hidden(NJ - 1, base + 8 * NJ - 4)
                if l == 0:
                    tables()
                    for i in range(2):
                        modc_sum(8 + i, 12 + i, i)
                dve.wait_ge(gate_ok, 4 * l + 4)
                dve.wait_ge(y_ok, l + 1)
                for half in range(2):
                    residual(1, 1, half, 0, half == 1)
                if l == 0:
                    for i in range(2):
                        modc_sum(10 + i, 14 + i, 2 + i)
                    for u in range(3):
                        lo_at(mix_base[1] + u)
                dve.wait_ge(unit_used, base + 8 * NJ)
                for half in range(2):
                    residual(1, 1, half, 1, half == 1)

            def angles():
                dve.wait_ge(tab_in, 64)
                pos = stat[:, 188:190]
                link(V.tensor_copy(pos, pos_i[:, :]))
                H2 = HD // 2
                W = TB * H2
                ang, n, r = r_w[:, 0, 0:W], r_w[:, 4:6, 0:W], r_w[:, 2:4, 0:W]
                for tb in range(TB):
                    z = V.tensor_scalar(ang[:, tb * H2:(tb + 1) * H2], r_w[:, 7, 0:H2], pos[:, tb:tb + 1], None,
                                        ALU.mult)
                link(z)
                for i, turn in enumerate((0.0, 0.25)):
                    z = V.tensor_scalar(n[:, i], ang, 1.0 / (2.0 * 3.141592653589793), turn, ALU.mult, ALU.add)
                link(z)
                src = r_w[:, 0:1, 0:W].to_broadcast([P, 2, W])
                for again in range(2):
                    if again:
                        link(V.tensor_scalar(n, r, 1.0 / (2.0 * 3.141592653589793), None, ALU.mult))
                    link(V.tensor_scalar(n, n, MAGIC, None, ALU.add))
                    link(V.tensor_scalar(n, n, -MAGIC, None, ALU.add))
                    for part in TWO_PI:
                        link(V.scalar_tensor_tensor(r, n, -part, src, op0=ALU.mult, op1=ALU.add))
                        src = r
                    if not again:
                        link(V.tensor_scalar(r[:, 1], r[:, 1], 1.5707963267948966, None, ALU.add))
                V.tensor_scalar(r, r, 3.1415925, -3.1415925, ALU.min, ALU.max).then_inc(sc_arg, 1)

            def tables():
                dve.wait_ge(sc_ok, 1)
                H2 = HD // 2
                for which in range(2):
                    gain = r_w[:, 6, which * HD:(which + 1) * HD]
                    for tb in range(TB):
                        sin, cos = r_w[:, 4, tb * H2:(tb + 1) * H2], r_w[:, 5, tb * H2:(tb + 1) * H2]
                        o = tab[:, which].rearrange("p a (b s d) -> p a b s d", b=TB, s=2)
                        for s in range(2):
                            V.tensor_tensor(o[:, 0, tb, s], cos, gain[:, s * H2:(s + 1) * H2], ALU.mult)
                            V.scalar_tensor_tensor(o[:, 1, tb, s], sin, 1.0 if s else -1.0,
                                                   gain[:, (1 - s) * H2:(2 - s) * H2], op0=ALU.mult, op1=ALU.mult)

            V.memset(eps[:, :], EPS)
            V.memset(ones[:, :], 1.0).then_inc(set_up, 1)
            V.memset(ps[:, 6:8, :], 0.0).then_inc(set_up, 1)
            for l in range(DEPTH):
                norm(2 * l)
                if l == 0:
                    gla()
                else:
                    moba()
                out_project(l)
                norm(2 * l + 1)
                mlp(l)


_INS = ['x', 'c', 'positions', 'ada_w', 'ada_b', 'norm_mix_g', 'norm_mlp_g', 'gla_w_in', 'gla_w_gate_up',
        'gla_b_gate', 'gla_onorm_g', 'gla_w_out', 'moba_w_in', 'moba_q_norm_g', 'moba_k_norm_g', 'moba_w_out',
        'mlp_w1', 'mlp_w2']
_OUTS = [((1, 256, 1024), 'float32')]


def kernel(**inputs):
    import numpy as _np
    import concourse.bacc as _bacc
    from concourse import mybir as _mybir
    from concourse.bass_utils import run_bass_kernel_spmd as _run

    i = _np.arange(128)
    after = i[:, None] <= i[None, :]
    same = i[:, None] // 64 == i[None, :] // 64
    tri = _np.where(after.T, 0.0, -1.0e30)
    consts = {
        "eye": _np.eye(128, dtype=_np.float32),
        "keep": (after & same).astype(_np.int32),
        "amask": _np.concatenate([tri, _np.zeros((128, 128)), tri], axis=1).astype(_np.float32),
        "restart": (_np.arange(1024) % 64 != 0).astype(_np.float32)[None],
        "invf": (10000.0 ** (-_np.arange(64) / 64.0)).astype(_np.float32)[None],
    }
    nc = _bacc.Bacc("TRN2", target_bir_lowering=False, num_devices=1)
    arrays, args = {}, []
    for name in _INS + list(consts):
        a = _np.ascontiguousarray(inputs[name] if name in inputs else consts[name])
        arrays[f"in_{name}_dram"] = a
        args.append(nc.dram_tensor(f"in_{name}_dram", a.shape, _mybir.dt.from_np(a.dtype), kind="ExternalInput").ap())
    for n, (shape, dtype) in enumerate(_OUTS):
        dt = _mybir.dt.from_np(_np.dtype(dtype))
        args.append(nc.dram_tensor(f"out_{n}_dram", shape, dt, kind="ExternalOutput").ap())
    trunk_kernel(nc, *args)
    r = _run(nc, [arrays], core_ids=[0])
    got = tuple(r.results[0][f"out_{n}_dram"] for n in range(len(_OUTS)))
    return got[0]
```

```python
from contextlib import ExitStack

import concourse.bass as bass
from concourse import mybir

F32 = mybir.dt.float32
F32R = mybir.dt.float32r
I32 = mybir.dt.int32
ALU = mybir.AluOpType
ACT = mybir.ActivationFunctionType
X_AXIS = mybir.AxisListType.X

P = 128
TB = 2
COLS = 512
RAW = 4
SPLIT = 4
UNIT = 1024
ADA_ACC = 8
L = 64
EPS = 1e-6
NEG = -1.0e30
MAGIC = 1.5 * 2.0 ** 23
TWO_PI = (6.28125, 0.0019350051879882812, 3.019916050561733e-07)


def trunk_kernel(nc, x_d, c_d, pos_d, ada_w, ada_b, mix_g, mlp_g, gla_in, gla_up, gla_bg, gla_og,
                 gla_out, moba_in, moba_qg, moba_kg, moba_out, w1_d, w2_d, eye_d, keep_d, amask_d,
                 restart_d, invf_d, out_d):
    DEPTH, D = mix_g.shape
    KC = D // P
    SEQ = x_d.shape[1]
    RANK, HDK = gla_up.shape[1:]
    DV = gla_og.shape[1]
    GH = gla_out.shape[1] // DV
    DK = HDK // GH
    NCH = SEQ // L
    HD = moba_qg.shape[1]
    MH = D // HD
    NJ = w1_d.shape[2] // COLS
    HC = COLS // P
    assert (SEQ, D, DK, HD, DV) == (TB * P, 1024, P, P, 256) and D == 2 * COLS and 2 * GH == MH

    MIX_BLOCKS = 8
    mix_base = [l * 4 * (MIX_BLOCKS + 2 * NJ) for l in range(DEPTH)]
    mlp_base = [b + 4 * MIX_BLOCKS for b in mix_base]
    MIX_IN = [[1, 0, 2, 3, 4, 5], [2, 0, 3, 1, 4, 5]]
    mix_w = [(gla_in[0], gla_out[0]), (moba_in[0], moba_out[0])]
    ADA_PE = [[0, 2, 1, 3], [18, 19, 20, 21]]

    ctx = ExitStack()
    with ctx:
        def sb(name, shape, dt=F32):
            return ctx.enter_context(nc.sbuf_tensor(name, shape, dt))

        def sem(name):
            return ctx.enter_context(nc.semaphore(name))

        w_raw = sb("w_raw", [P, RAW, 2, UNIT])
        w_hi = sb("w_hi", [P, SPLIT, UNIT], F32R)
        w_lo = sb("w_lo", [P, SPLIT, UNIT], F32R)
        ada_raw = sb("ada_raw", [P, 2, KC // 2, COLS])
        ada_acc = sb("ada_acc", [P, ADA_ACC, COLS])
        x = sb("x", [P, TB, D])
        a_hi = sb("a_hi", [P, KC, SEQ], F32R)
        a_lo = sb("a_lo", [P, KC, SEQ], F32R)
        m_hi = sb("m_hi", [P, HC, SEQ], F32R)
        m_lo = sb("m_lo", [P, HC, SEQ], F32R)
        gates = sb("gates", [P, 2, D])
        eye = sb("eye", [P, P])
        keep = sb("keep", [P, P], I32)
        ones = sb("ones", [P, P])
        rows = sb("rows", [P, P])
        cols = sb("cols", [P, P])
        c_act = sb("c_act", [P, KC])
        modc = sb("modc", [P, DEPTH, 4, KC])
        stat = sb("stat", [P, 192])
        eps = sb("eps", [P, 1])
        onorm = sb("onorm", [P, DV])
        amask = sb("amask", [P, 3 * P])
        glr_w = sb("glr_w", [P, KC, RANK])
        glr_up = sb("glr_up", [RANK, HDK])
        glrT = sb("glrT", [RANK, SEQ])
        dec = sb("dec", [P, GH, NCH])
        pos_i = sb("pos_i", [P, TB], I32)
        K1 = 1024
        ARENA = 14 * K1 + 512
        arena = sb("arena", [P, ARENA])

        def area(at, *shape):
            n = 1
            for s in shape:
                n *= s
            assert at + n <= ARENA
            v = arena[:, at:at + n]
            if len(shape) == 2:
                v = v.rearrange("p (a b) -> p a b", a=shape[0])
            elif len(shape) == 3:
                v = v.rearrange("p (a b c) -> p a b c", a=shape[0], b=shape[1])
            return v

        xn = area(0, TB, D)
        hT = area(2 * K1, KC, SEQ)
        relu = area(4 * K1, TB, COLS)
        relu_c = area(4 * K1, HC, SEQ)
        sq = area(5 * K1, HC, SEQ)
        g_v = area(0, TB, D)
        silu_r = area(2 * K1, TB, D)
        g_tok = area(4 * K1, 2, TB, COLS)
        o_tok = area(4 * K1, TB, D)
        g_z = area(6 * K1, GH, SEQ)
        k_tailT = area(6 * K1, GH, SEQ)
        g_t = area(7 * K1, GH, SEQ)
        g_e = area(8 * K1, GH, SEQ)
        att = area(8 * K1, TB, GH, P)
        g_i = area(9 * K1, GH, SEQ)
        k_inv = area(10 * K1, GH, SEQ)
        q_dec = area(11 * K1, GH, SEQ)
        k_tail = area(12 * K1, TB, GH, DK)
        g_s = area(3 * K1, GH, SEQ)
        state = [None, area(7 * K1, GH, DV), area(9 * K1, GH, DV), area(6 * K1, GH, DV)]
        restart = area(12 * K1, GH * NCH, L)
        b_tok = [area(0, TB, COLS), area(12 * K1 + 512, TB, COLS)]
        b_t = area(1 * K1, TB, COLS)
        b_u = area(2 * K1, TB, COLS)
        b_r = area(3 * K1, TB, COLS)
        b_kT = area(4 * K1, MH, SEQ)
        b_qT = area(6 * K1, MH, SEQ)
        b_v = area(8 * K1, TB, D)
        b_sq = area(11 * K1 + 512, TB, COLS)
        b_p = area(10 * K1, 4, 3 * P)
        b_pT = area(11 * K1 + 512, 4, 3 * P)
        tab = area(13 * K1 + 512, 2, 2, TB * P)
        r_w = area(7 * K1, 8, TB * P)
        c_rows = area(2 * K1, P)[0:KC]
        ada_pre = [area((4 + 2 * i) * K1, KC // 2, COLS) for i in range(4)]
        ada_row = [area(13 * K1, 2, COLS)[0:97], area(10 * K1, 2, COLS)[0:97]]

        ps = ctx.enter_context(nc.psum_tensor("ps", [P, 8, COLS], F32))

        S_SS, S_LN, S_R0, S_V, S_B = 0, 8, 16, 24, 32
        S_O = 48
        S_B2 = (S_O, 160)
        S_MX = 112

        raw_in = [sem(f"raw_in{i}") for i in range(RAW)]
        ada_in = [sem(f"ada_in{i}") for i in range(2)]
        vec_in, x_in, glr_in, out_sem = sem("vec_in"), sem("x_in"), sem("glr_in"), sem("out_sem")
        tab_in, con_in, gb_in = sem("tab_in"), sem("con_in"), sem("gb_in")
        hi_made, lo_made = sem("hi_made"), sem("lo_made")
        unit_used = sem("unit_used")
        ada_mac = sem("ada_mac")
        set_up = sem("set_up")
        ada_sw_in = [sem(f"ada_sw_in{i}") for i in range(2)]
        ada_pre_in = [sem(f"ada_pre_in{i}") for i in range(4)]
        ada_pe = sem("ada_pe")
        row_ok = sem("row_ok")
        col_T = sem("col_T")
        c_in, c_T, c_ok = sem("c_in"), sem("c_T"), sem("c_ok")
        vec_T, vec_ok = sem("vec_T"), sem("vec_ok")
        mod_T, mod_red, mod_ok = sem("mod_T"), sem("mod_red"), sem("mod_ok")
        gate_p, gate_ok = sem("gate_p"), sem("gate_ok")
        sc_arg, sc_ok = sem("sc_arg"), sem("sc_ok")
        x_new = sem("x_new")
        ss_ok, ln_ok, r0_ok, xn_ok = sem("ss_ok"), sem("ln_ok"), sem("r0_ok"), sem("xn_ok")
        xT_ok, hA_ok, hD_ok = sem("xT_ok"), sem("hA_ok"), sem("hD_ok")
        ahi_ok, a_ok = sem("ahi_ok"), sem("a_ok")
        in_out = sem("in_out")
        relu_ok, tr_ok, sq_ok, mhi_ok, m_ok = (sem("relu_ok"), sem("tr_ok"), sem("sq_ok"),
                                               sem("mhi_ok"), sem("m_ok"))
        y_ok = sem("y_ok")
        dve_step, act_step = sem("dve_step"), sem("act_step")
        oT_ok = sem("oT_ok")
        z_p, kT_p, qT_p, kt_p, att_p, u_p, o_p, glr_p = (sem("z_p"), sem("kT_p"), sem("qT_p"), sem("kt_p"),
                                                         sem("att_p"), sem("u_p"), sem("o_p"), sem("glr_p"))
        glr_ok, z_ok, ez_ok, G_ok, eG_ok, kd_ok, qd_ok = (sem("glr_ok"), sem("z_ok"), sem("ez_ok"), sem("G_ok"),
                                                          sem("eG_ok"), sem("kd_ok"), sem("qd_ok"))
        kt_ok, zero_ok, att_ok, st_ok, oss_ok, or0_ok = (sem("kt_ok"), sem("zero_ok"), sem("att_ok"), sem("st_ok"),
                                                         sem("oss_ok"), sem("or0_ok"))
        on_ok, ot_ok = sem("on_ok"), sem("ot_ok")
        tok_used, tab_ok = sem("tok_used"), sem("tab_ok")
        bss_ok, br0_ok, rot_ok, rT_p, rT_ok = (sem("bss_ok"), sem("br0_ok"), sem("rot_ok"), sem("rT_p"),
                                               sem("rT_ok"))
        s_p, mx_ok, ex_ok, pn_ok, pT_p, pT_ok = (sem("s_p"), sem("mx_ok"), sem("ex_ok"), sem("pn_ok"),
                                                 sem("pT_p"), sem("pT_ok"))

        C_MIX, C_MLP = 0, DEPTH * KC
        C_BG = C_MLP + DEPTH * KC
        C_AB = C_BG + GH
        N_ROWS = C_AB + DEPTH * 4 * KC
        N_VEC = 3 + 2 * DEPTH
        ADA_FIRST = ADA_PE[0]
        SETS_SILU_SIN, SETS_LN_EXP = "silu_and_others", "natural_log_exp_and_others"

        def ada_turn(b):
            return b - 8 if isinstance(b, int) and b > ADA_PE[1][-1] else b - 4

        N_PAIRS = [0, 4, 12, 20]
        A_NORM, A_OUT = [0, 8, 16, 28], [4, 24]

        def tile(tb):
            return slice(tb * P, (tb + 1) * P)

        def acc_slot(b):
            return (b + 4) % ADA_ACC

        def in_bank(n, tb):
            return 4 + 2 * (n % 2) + tb

        def y_bank(mlp, half, tb):
            return 4 + 2 * tb + half if mlp else 2 * half + tb

        def norm_bank(v):
            return 4 if v % 2 else 0

        def chunk_at(v, k):
            return norm_bank(v) + 2 * (k // 4) + k % 2, ((k % 4) // 2) * SEQ

        block = ctx.enter_context(nc.Block())

        def ada_part(b, half):
            l, n = b // 12, b % 12
            src = ada_w[l, half * 4 * P:(half + 1) * 4 * P, n * COLS:(n + 1) * COLS]
            return src.rearrange("(k p) n -> p k n", p=P)

        @block.gpsimd
        def _(pool):
            for half in range(2):
                pool.wait_ge(ada_pe, 6 + half + 1)
                nc.gpsimd.dma_start(ada_raw[:, half], ada_part(4, half)).then_inc(ada_sw_in[half], 16)

            def load(l, n, half):
                src = ada_w[l, half * 4 * P:(half + 1) * 4 * P, bass.ds(n * COLS, COLS)]
                nc.gpsimd.dma_start(ada_raw[:, half], src.rearrange("(k p) n -> p k n", p=P)
                                    ).then_inc(ada_sw_in[half], 16)

            for l, first, end in ((0, 5, 12), (1, 0, 7)):
                with pool.Fori(first, end) as n:
                    for half in range(2):
                        pool.wait_ge(ada_mac, 8 * n + 8 * ada_turn(12 * l - 1) + 4 * (half + 1))
                        load(l, n, half)
            with pool.Fori(7, 11) as n:
                for half in range(2):
                    pool.wait_ge(ada_pe, 2 * n - 2 * 7 + 8 + half + 1)
                    load(1, n, half)
            for half in range(2):
                pool.wait_ge(ada_mac, 8 * ada_turn(22) + 4 * (half + 1))
                load(1, 11, half)

        @block.sync
        def _(sp):
            def load_ada(b, half):
                if b == 3:
                    sp.wait_ge(ada_pe, half + 1)
                sp.dma_start(ada_raw[:, half], ada_part(b, half)).then_inc(ada_in[half], 16)

            def load_pre(i, b):
                for half in range(2):
                    sp.dma_start(ada_pre[2 * i + half], ada_part(b, half)).then_inc(ada_pre_in[2 * i + half], 16)

            def load_piece(m, slot, src):
                if not (isinstance(m, int) and m < RAW):
                    sp.wait_ge(lo_made, 2 * (m - RAW) + 2)
                dst = w_raw[:, slot]
                if src.shape[1] == COLS:
                    dst = dst.rearrange("p u (k n) -> p (u k) n", k=2)
                sp.dma_start(dst, src.rearrange("(k p) n -> p k n", p=P)).then_inc(raw_in[slot], 16)

            sp.dma_start(c_rows[:, :], c_d[0, :].rearrange("(k p) -> k p", p=P)).then_inc(c_in, 16)
            sp.dma_start(eye[:, :], eye_d).then_inc(c_in, 16)
            for half in range(2):
                load_ada(0, half)
            for tb in range(TB):
                sp.dma_start(x[:, tb], x_d[0, tb * P:(tb + 1) * P, :]).then_inc(x_in, 16)

            def vec(at, n, src):
                sp.dma_start(rows[at:at + n, :], src).then_inc(vec_in, 16)

            vec(C_MIX, DEPTH * KC, mix_g.rearrange("l (k p) -> (l k) p", p=P))
            vec(C_MLP, DEPTH * KC, mlp_g.rearrange("l (k p) -> (l k) p", p=P))
            vec(C_BG, GH, gla_bg[0, :].rearrange("(k p) -> k p", p=P))
            for l in range(DEPTH):
                for s in range(2):
                    vec(C_AB + (2 * l + s) * 2 * KC, 2 * KC,
                        ada_b[l, 3 * s * D:(3 * s + 2) * D].rearrange("(k p) -> k p", p=P))

            def constants():
                with nc.allow_non_contiguous_dma(reason="sixteen columns"):
                    sp.dma_start(glr_w[:, :, :],
                                 gla_in[0, :, gla_in.shape[2] - RANK:].rearrange("(k p) n -> p k n", p=P)
                                 ).then_inc(glr_in, 16)
                sp.dma_start(glr_up[:, :], gla_up[0]).then_inc(glr_in, 16)
                sp.dma_start(keep[:, :], keep_d).then_inc(con_in, 16)
                sp.dma_start(amask[:, :], amask_d).then_inc(con_in, 16)
                sp.dma_start(onorm[:, :], gla_og.to_broadcast([P, DV])).then_inc(con_in, 16)
                sp.dma_start(restart.rearrange("p a b -> p (a b)"), restart_d.to_broadcast([P, GH * SEQ])
                             ).then_inc(con_in, 16)
                gate_biases(0)

            def gate_biases(l):
                for s in range(2):
                    sp.dma_start(gates[:, s], ada_b[l:l + 1, (3 * s + 2) * D:(3 * s + 3) * D].to_broadcast([P, D])
                                 ).then_inc(gb_in, 16)

            def rotary_in():
                sp.wait_ge(x_new, 2)
                with nc.allow_non_contiguous_dma(reason="256 numbers"):
                    sp.dma_start(pos_i[:, :], pos_d[0, :].rearrange("(b p) -> p b", p=P)).then_inc(tab_in, 16)
                sp.dma_start(r_w[:, 7, 0:HD // 2], invf_d.to_broadcast([P, HD // 2])).then_inc(tab_in, 16)
                sp.dma_start(r_w[:, 6, 0:HD], moba_qg.to_broadcast([P, HD])).then_inc(tab_in, 16)
                sp.dma_start(r_w[:, 6, HD:2 * HD], moba_kg.to_broadcast([P, HD])).then_inc(tab_in, 16)

            def mixer(l):
                w_in, w_out = mix_w[l]
                for n in range(MIX_BLOCKS):
                    w, c0 = (w_in, MIX_IN[l][n] * COLS) if n < 6 else (w_out, (n - 6) * COLS)
                    if l == 0 and n == 0:
                        load_pre(0, 2)
                    for d in range(2):
                        m = mix_base[l] // 2 + 2 * n + d
                        load_piece(m, m % RAW, w[4 * d * P:4 * (d + 1) * P, c0:c0 + COLS])
                        if l == 0 and n == 0 and d == 0:
                            load_pre(1, 1)
                            for half in range(2):
                                load_ada(3, half)
                    if l == 0 and n == 0:
                        constants()
                    if l == 1 and n == 1:
                        sp.wait_ge(x_new, 4)
                        gate_biases(1)

            def mlp(l):
                base = mlp_base[l] // 2

                def w1(j, d, m, slot):
                    load_piece(m, slot, w1_d[l, 4 * d * P:4 * (d + 1) * P, bass.ds(j * COLS, COLS)])

                def w2(j, d, m, slot):
                    load_piece(m, slot, w2_d[l, bass.ds(j * COLS + 2 * d * P, 2 * P), :])

                for j in range(2):
                    for d in range(2):
                        w1(j, d, base + 2 * j + d, 2 * j + d)
                with sp.Fori(0, NJ - 2) as i:
                    for d in range(2):
                        w2(i, d, base + 4 + 4 * i + d, d)
                    for d in range(2):
                        w1(i + 2, d, base + 6 + 4 * i + d, 2 + d)
                if l == 0:
                    rotary_in()
                for j in range(NJ - 2, NJ):
                    for d in range(2):
                        m = base + 4 + 4 * (NJ - 2) + 2 * (j - NJ + 2) + d
                        w2(j, d, m, m % RAW)

            mixer(0)
            mlp(0)
            mixer(1)
            mlp(1)
            for tb in range(TB):
                sp.wait_ge(x_new, 2 * (2 * DEPTH - 1) + tb + 1)
                sp.dma_start(out_d[0, tb * P:(tb + 1) * P, :], x[:, tb]).then_inc(out_sem, 16)
            sp.wait_ge(out_sem, TB * 16)

        @block.tensor
        def _(pe):
            mm, tr = nc.tensor.matmul, nc.tensor.transpose

            def three(out, hi, lo, slot, wc, first, last):
                mm(out, hi, w_hi[:, slot, wc], start=first, stop=False)
                mm(out, hi, w_lo[:, slot, wc], start=False, stop=False)
                return mm(out, lo, w_hi[:, slot, wc], start=False, stop=last)

            def project(u0, banks, a_wait=None, side={}):
                for u in range(4):
                    pe.wait_ge(lo_made, u0 + u + 1)
                    if a_wait is not None:
                        pe.wait_ge(a_ok, a_wait + u + 1)
                    for k in range(2):
                        for tb in range(TB):
                            z = three(ps[:, banks[tb], :], a_hi[:, 2 * u + k, tile(tb)],
                                      a_lo[:, 2 * u + k, tile(tb)], u, slice(k * COLS, (k + 1) * COLS),
                                      u == 0 and k == 0, u == 3 and k == 1)
                    z.then_inc(unit_used, 1)
                    if u in side:
                        side[u]()

            def project_tiles(u0, banks, a_wait=None, side={}, y_done=False):
                for tb in range(TB):
                    for u in range(4):
                        if tb == 0:
                            pe.wait_ge(lo_made, u0 + u + 1)
                        if a_wait is not None:
                            pe.wait_ge(a_ok, a_wait + 4 * tb + u + 1)
                        for k in range(2):
                            z = three(ps[:, banks[tb], :], a_hi[:, 2 * u + k, tile(tb)], a_lo[:, 2 * u + k, tile(tb)],
                                      u, slice(k * COLS, (k + 1) * COLS), u == 0 and k == 0, u == 3 and k == 1)
                        if tb == 1:
                            z.then_inc(unit_used, 1)
                        elif u == 3 and y_done:
                            z.then_inc(y_ok, 1)
                        if (tb, u) in side:
                            side[tb, u]()

            def fin_mods(v, bank):
                b0 = 12 * (v // 2) + 6 * (v % 2)
                pe.wait_ge(ada_mac, 8 * (ada_turn(b0 + 3) + 1))
                for i in range(4):
                    for q in range(4):
                        z = mm(ps[:, bank, 4 * i + q:4 * i + q + 1],
                               ada_acc[:, acc_slot(b0 + i), q * P:(q + 1) * P], ones[:, 0:1], start=True, stop=True)
                z.then_inc(mod_T, 1)

            def ada_rows(b, half, bank):
                if b in (0, 3):
                    raw = ada_raw[:, half]
                    pe.wait_ge(ada_in[half], 16 if b == 0 else 32)
                elif b < 4:
                    raw = ada_pre[2 * (2 - b) + half]
                    pe.wait_ge(ada_pre_in[2 * (2 - b) + half], 16)
                else:
                    raw = ada_raw[:, half]
                    pe.wait_ge(ada_sw_in[half], 16 * (b - 3))
                for k in range(4):
                    z = mm(ps[32 * k:32 * k + 1, bank, :], c_act[:, 4 * half + k:4 * half + k + 1], raw[:, k],
                           start=half == 0, stop=half == 1)
                z.then_inc(ada_pe, 1)

            def ada_cols(i, bank, c0=0):
                pe.wait_ge(row_ok, i + 1)
                for q in range(4):
                    z = mm(ps[:, bank, c0 + q:c0 + q + 1], ada_row[i // 4][:, i % 2, q * P:(q + 1) * P],
                           ones[0:97, 0:1], start=True, stop=True)
                z.then_inc(col_T, 1)

            def fin_gate(b, bank):
                pe.wait_ge(ada_mac, 8 * (ada_turn(b) + 1))
                mm(ps[:, bank, :], ones[:, :], ada_acc[:, acc_slot(b)], start=True, stop=True).then_inc(gate_p, 1)

            def turn_norm(v, tb):
                pe.wait_ge(xn_ok, 2 * v + tb + 1)
                if v > 0 and tb == 1:
                    pe.wait_ge(a_ok, A_NORM[v] + 4)
                for k in range(KC):
                    bank, at = chunk_at(v, k)
                    z = tr(ps[:, bank, at + tb * P:at + (tb + 1) * P], xn[:, tb, k * P:(k + 1) * P], eye[:, :])
                    if (v > 0 or tb == TB - 1) and k % 4 >= 2:
                        z.then_inc(xT_ok, 1)

            def first_norm():
                pe.wait_ge(c_ok, 1)
                pe.wait_ge(set_up, 2)
                for half in range(2):
                    ada_rows(0, half, 6)
                pe.wait_ge(vec_in, 16 * N_VEC)
                tr(ps[:, 5, 0:N_ROWS], rows[0:N_ROWS, :], eye[0:N_ROWS, 0:N_ROWS]).then_inc(vec_T, 1)
                ada_cols(0, 4)
                for tb in range(TB):
                    turn_norm(0, tb)
                for half in range(2):
                    ada_rows(2, half, 7)
                pe.wait_ge(vec_ok, 1)
                ada_cols(1, 5)

            def turn_o(pair):
                pe.wait_ge(in_out, 10 + 2 * pair)
                pe.wait_ge(ot_ok, pair + 1)
                for h in (2 * pair, 2 * pair + 1):
                    for k in (2 * h, 2 * h + 1):
                        for tb in range(TB):
                            z = tr(ps[:, 4 + h, (k % 2) * SEQ + tb * P:(k % 2) * SEQ + (tb + 1) * P],
                                   o_tok[:, tb, k * P:(k + 1) * P], eye[:, :])
                    z.then_inc(oT_ok, 1)

            def out_project(l, side={}):
                v = 2 * l + 1

                def turn():
                    pe.wait_ge(a_ok, A_OUT[l] + 4)
                    pe.wait_ge(mod_red, 4 + v)
                    turn_norm(v, 0)

                u0 = mix_base[l] + 6 * 4
                project(u0, (0, 1), A_OUT[l], side)
                pe.wait_ge(gate_ok, 4 * l + 2)
                project_tiles(u0 + 4, (2, 3), None, {(1, 3): turn}, y_done=True)

            def mlp(l):
                base, m0 = mlp_base[l], l * NJ

                def turn():
                    pe.wait_ge(relu_ok, 2 * m0 + 2)
                    for c in range(HC):
                        for tb in range(TB):
                            z = tr(ps[:, 4 + c // 2, (c % 2) * SEQ + tb * P:(c % 2) * SEQ + (tb + 1) * P],
                                   relu[:, tb, c * P:(c + 1) * P], eye[:, :])
                        if c % 2 == 1:
                            z.then_inc(tr_ok, 1)

                def up(u0, side={}, first=False):
                    for u in range(4):
                        pe.wait_ge(lo_made, u0 + u + 1)
                        for c in (2, 3, 0, 1):
                            if first and u == 0 and c == 0:
                                pe.wait_ge(relu_ok, 2 * m0 + 2)
                            o = ps[:, c, 0:SEQ]
                            for k in range(2):
                                w, a = slice(k * COLS + c * P, k * COLS + (c + 1) * P), 2 * u + k
                                mm(o, w_hi[:, u, w], a_hi[:, a, :], start=u == 0 and k == 0, stop=False)
                                mm(o, w_hi[:, u, w], a_lo[:, a, :], start=False, stop=False)
                                z = mm(o, w_lo[:, u, w], a_hi[:, a, :], start=False, stop=u == 3 and k == 1)
                        z.then_inc(unit_used, 1)
                        if u in side:
                            side[u]()

                def down(u0, j, first):
                    for u in range(4):
                        pe.wait_ge(lo_made, u0 + u + 1)
                        if u % 2 == 0:
                            pe.wait_ge(m_ok, 2 * (m0 + j) + u // 2 + 1)
                        for tb in range(TB):
                            for h in range(2):
                                z = three(ps[:, y_bank(1, h, tb), :], m_hi[:, u, tile(tb)], m_lo[:, u, tile(tb)],
                                          u, slice(h * COLS, (h + 1) * COLS), first and u == 0, False)
                        z.then_inc(unit_used, 1)

                v = 2 * l + 1
                pe.wait_ge(x_new, 4 * l + 1)
                project_tiles(base, (0, 1), A_NORM[v], {(0, 2): lambda: turn_norm(v, 1)})
                up(base + 4, {1: turn}, first=True)
                pe.wait_ge(sq_ok, 2 * m0 + 2)
                down(base + 8, 0, True)
                with pe.Fori(1, NJ - 1) as j:
                    pe.wait_ge(relu_ok, 2 * j + 2 * m0 + 2)
                    up(8 * j + base + 4)
                    down(8 * j + base + 8, j, False)
                j, u0 = NJ - 1, base + 4 * (2 * NJ - 1)
                pe.wait_ge(relu_ok, 2 * (m0 + j) + 2)
                for i in range(2):
                    fin_gate(12 * l + 10 + i, i)
                for tb in range(TB if l + 1 < DEPTH else 1):
                    for u in range(4):
                        if tb == 0:
                            pe.wait_ge(lo_made, u0 + u + 1)
                            if u % 2 == 0:
                                pe.wait_ge(m_ok, 2 * (m0 + j) + u // 2 + 1)
                        for h in range(2):
                            z = three(ps[:, y_bank(1, h, tb), :], m_hi[:, u, tile(tb)], m_lo[:, u, tile(tb)],
                                      u, slice(h * COLS, (h + 1) * COLS), False, u == 3)
                        if tb == 1:
                            z.then_inc(unit_used, 1)
                        elif u == 3:
                            z.then_inc(y_ok, 1)
                        if l + 1 < DEPTH and (tb, u) == (0, 3):
                            fin_mods(v + 1, 2)
                        if l + 1 < DEPTH and (tb, u) == (1, 3):
                            pe.wait_ge(gate_ok, 4 * l + 4)
                            pe.wait_ge(mod_red, 4 + v + 1)
                            turn_norm(v + 1, 0)
                for h in range(2 if l + 1 == DEPTH else 0):
                    for u in range(4):
                        z = three(ps[:, y_bank(1, h, 1), :], m_hi[:, u, tile(1)], m_lo[:, u, tile(1)],
                                  u, slice(h * COLS, (h + 1) * COLS), False, u == 3)
                        if h == 1:
                            z.then_inc(unit_used, 1)
                    if h == 0:
                        z.then_inc(y_ok, 1)

            def gla():
                def glr():
                    pe.wait_ge(glr_in, 32)
                    for k in range(KC):
                        z = mm(ps[0:RANK, 0, 0:SEQ], glr_w[:, k, :], hT[:, k, :], start=k == 0, stop=k == KC - 1)
                    z.then_inc(glr_p, 1)

                def logits():
                    pe.wait_ge(glr_ok, 1)
                    for h in range(GH):
                        z = mm(ps[:, h // 2, (h % 2) * SEQ:(h % 2 + 1) * SEQ], glr_up[:, h * DK:(h + 1) * DK],
                               glrT[:, :], start=True, stop=True)
                    z.then_inc(z_p, 1)

                def turn_tok(which, bank, done):
                    for h in range(GH):
                        for tb in range(TB):
                            z = tr(ps[:, bank + h // 2, (h % 2) * SEQ + tb * P:(h % 2) * SEQ + (tb + 1) * P],
                                   g_tok[:, which, tb, h * DK:(h + 1) * DK], eye[:, :])
                    z.then_inc(done, 1)

                def turn_k():
                    pe.wait_ge(in_out, 2)
                    turn_tok(0, 2, kT_p)

                def turn_q():
                    pe.wait_ge(in_out, 4)
                    pe.wait_ge(z_ok, 1)
                    turn_tok(1, 0, qT_p)

                def turn_tail():
                    pe.wait_ge(kd_ok, 1)
                    for tb in range(TB):
                        for h in range(GH):
                            z = tr(ps[:, 2 + tb, h * DK:(h + 1) * DK], k_tailT[:, h, tile(tb)], eye[:, :])
                    z.then_inc(kt_p, 1)

                def scores():
                    pe.wait_ge(qd_ok, 1)
                    for tb in range(TB):
                        for h in range(GH):
                            z = mm(ps[:, tb, h * P:(h + 1) * P], k_inv[:, h, tile(tb)], q_dec[:, h, tile(tb)],
                                   start=True, stop=True)
                    z.then_inc(att_p, 1)

                def update(h):
                    if h == 0:
                        pe.wait_ge(att_ok, 1)
                        pe.wait_ge(kt_ok, 1)
                        pe.wait_ge(in_out, 6)
                    elif h >= 2:
                        pe.wait_ge(in_out, 8)
                        pe.wait_ge(st_ok, h - 1)
                    for c in range(NCH - 1):
                        q = slice(64 * (c % 2), 64 * (c % 2) + 64)
                        z = mm(ps[:, 2 * (h % 2) + c % 2, (c // 2) * DV:(c // 2 + 1) * DV],
                               k_tail[q, c // 2, h, :], g_v[q, c // 2, h * DV:(h + 1) * DV], start=True, stop=True)
                    z.then_inc(u_p, 1)

                def output(pair):
                    pe.wait_ge(st_ok, 3 + pair)
                    for tb in range(TB):
                        for h in (2 * pair, 2 * pair + 1):
                            o = ps[:, 2 * pair + tb, (h % 2) * DV:(h % 2 + 1) * DV]
                            z = mm(o, att[:, tb, h, :], g_v[:, tb, h * DV:(h + 1) * DV], start=True, stop=True)
                            for c in (2 * tb, 2 * tb + 1):
                                if c == 0:
                                    continue
                                q = slice(64 * (c % 2), 64 * (c % 2) + 64)
                                z = mm(o[q], q_dec[:, h, c * L:(c + 1) * L], state[c][:, h, :],
                                       start=False, stop=True, skip_group_check=True)
                    z.then_inc(o_p, 1)

                def second_mods():
                    for i in range(2, 4):
                        for half in range(2):
                            ada_rows(ADA_FIRST[i], half, 4 + i)
                    for i in range(2, 4):
                        ada_cols(i, 4 + i)

                sides = [{1: second_mods, 3: glr},
                         {0: logits, 2: turn_k},
                         {1: turn_q, 2: turn_tail, 3: scores},
                         {2: lambda: update(0), 3: lambda: update(1)},
                         {0: lambda: update(2), 1: lambda: update(3), 2: lambda: output(0), 3: lambda: output(1)},
                         {}]
                pe.wait_ge(mod_red, 2)
                for n in range(6):
                    if n == 1:
                        pe.wait_ge(mod_red, 4)
                    if n >= 2:
                        pe.wait_ge(in_out, 2 * (n - 1))
                    project(mix_base[0] + 4 * n, (in_bank(n, 0), in_bank(n, 1)), 0 if n == 0 else None, sides[n])
                turn_o(0)
                pe.wait_ge(on_ok, 2)
                for i in range(2):
                    fin_gate(4 + i, 2 + i)

            def moba():
                def gate1():
                    pe.wait_ge(a_ok, A_NORM[2] + 8)
                    for i in range(2):
                        fin_gate(16 + i, 2 + i)

                def rows(i, half):
                    if i == 0:
                        pe.wait_ge(set_up, 3)
                    elif half == 0:
                        ada_cols(3 + i, 1, 4 * (i - 1))
                    ada_rows(18 + i, half, 0)

                def turn_rot(n):
                    pe.wait_ge(rot_ok, n + 1)
                    if n == 0:
                        pe.wait_ge(gate_ok, 6)
                    if n > 0:
                        pe.wait_ge(rT_ok, n)
                    for h in range(4):
                        for tb in range(TB):
                            z = tr(ps[:, 2 + h // 2, (h % 2) * SEQ + tb * P:(h % 2) * SEQ + (tb + 1) * P],
                                   b_r[:, tb, h * HD:(h + 1) * HD], eye[:, :])
                    z.then_inc(rT_p, 1)

                def scores(h):
                    if h == 0:
                        pe.wait_ge(mod_red, 4 + 3)
                    if h >= 2:
                        pe.wait_ge(mx_ok, 2 * (h - 1))
                    pe.wait_ge(rT_ok, 2 if h < 4 else 4)
                    mm(ps[:, h % 2, 0:P], b_qT[:, h, 0:P], b_kT[:, h, 0:P], start=True, stop=True)
                    mm(ps[:, h % 2, P:3 * P], b_qT[:, h, P:2 * P], b_kT[:, h, :], start=True, stop=True
                       ).then_inc(s_p, 1)

                def turn_p(h):
                    pe.wait_ge(pn_ok, h + 1)
                    if h >= 2:
                        pe.wait_ge(pT_ok, h - 1)
                    for i in range(3):
                        z = tr(ps[:, 2 + h % 2, i * P:(i + 1) * P], b_p[:, h % 4, i * P:(i + 1) * P], eye[:, :])
                    z.then_inc(pT_p, 1)

                def values(h):
                    pe.wait_ge(pT_ok, h + 1)
                    o = ps[:, 4 + h // 2, (h % 2) * SEQ:(h % 2 + 1) * SEQ]
                    mm(o, b_v[:, 0, h * HD:(h + 1) * HD], b_pT[:, h % 4, 0:SEQ], start=True, stop=True)
                    z = mm(o[:, P:2 * P], b_v[:, 1, h * HD:(h + 1) * HD], b_pT[:, h % 4, SEQ:3 * P],
                           start=False, stop=True, skip_group_check=True)
                    if h % 2 == 1:
                        z.then_inc(oT_ok, 1)

                sides = [{}, {0: gate1}] + [{3: (lambda n=n: turn_rot(n))} for n in range(4)]
                for i in range(4):
                    for half in range(2):
                        sides[1 + i][1 + half] = lambda i=i, half=half: rows(i, half)
                sides[5][1] = lambda: ada_cols(7, 1, 12)
                for n in range(6):
                    if n >= 2:
                        pe.wait_ge(in_out, 12 + 2 * (n - 1))
                    else:
                        pe.wait_ge(x_new, 3 + n)
                    u0, banks = mix_base[1] + 4 * n, (in_bank(n, 0), in_bank(n, 1))
                    if n == 0:
                        project_tiles(u0, banks, A_NORM[2], {(0, 3): lambda: turn_norm(2, 1)})
                    else:
                        project(u0, banks, None, sides[n])
                LAG_T, LAG_V = 2, 3
                for i in range(MH + LAG_V):
                    if i < MH:
                        scores(i)
                    if i == 1:
                        pe.wait_ge(rT_ok, 4)
                    if 0 <= i - LAG_T < MH:
                        turn_p(i - LAG_T)
                    if i == LAG_V:
                        pe.wait_ge(in_out, 24)
                    if i >= LAG_V:
                        values(i - LAG_V)

            pe.wait_ge(c_in, 32)
            tr(ps[:, 4, 0:KC], c_rows[:, :], eye[0:KC, 0:KC]).then_inc(c_T, 1)
            first_norm()
            for l in range(DEPTH):
                if l == 0:
                    gla()
                    out_project(l, {0: lambda: turn_o(1), 3: lambda: fin_mods(1, 4)})
                else:
                    moba()
                    out_project(l)
                mlp(l)

        @block.scalar
        def _(act):
            A = nc.scalar.activation
            steps = [0]

            def link(ins):
                steps[0] += 1
                ins.then_inc(act_step, 1)
                act.wait_ge(act_step, steps[0])

            def hi(u, c, round_):
                if c % 2 == 0:
                    act.wait_ge(raw_in[c // 2], 16 * round_ + 16)
                if not (isinstance(u, int) and u < SPLIT):
                    act.wait_ge(unit_used, u - SPLIT + 1)
                A(w_hi[:, c % SPLIT], w_raw[:, c // 2, c % 2], ACT.Copy).then_inc(hi_made, 1)

            def hi_at(u):
                hi(u, u % 8, u // 8)

            def squares(v, tb):
                if v == 0:
                    if tb == 0:
                        act.wait_ge(x_in, 32)
                else:
                    act.wait_ge(x_new, 2 * (v - 1) + tb + 1)
                i = 2 * v + tb
                A(xn[:, tb], x[:, tb], ACT.Square, accum_out=stat[:, S_SS + i:S_SS + i + 1]).then_inc(ss_ok, 1)
                act.wait_ge(ss_ok, i + 1)
                A(stat[:, S_LN + i:S_LN + i + 1], stat[:, S_SS + i:S_SS + i + 1], ACT.Ln, scale=1.0 / D,
                  bias=eps[:, :]).then_inc(ln_ok, 1)
                act.wait_ge(ln_ok, i + 1)
                A(stat[:, S_R0 + i:S_R0 + i + 1], stat[:, S_LN + i:S_LN + i + 1], ACT.Exp, scale=-0.5
                  ).then_inc(r0_ok, 1)

            def modulate_first(quarters):
                for q in quarters:
                    act.wait_ge(mod_ok, 1 + q // 2)
                    act.wait_ge(xT_ok, 2 * (q // 2) + 1)
                    k = 2 * q
                    bank, at = chunk_at(0, k)
                    A(hT[:, k], ps[:, bank, at:at + SEQ], ACT.Identity,
                      scale=modc[:, 0, 1, k:k + 1], bias=modc[:, 0, 0, k:k + 1]).then_inc(hA_ok, 1)
                    act.wait_ge(hA_ok, q + 1)
                    act.wait_ge(hD_ok, q + 1)
                    A(a_hi[:, k:k + 2], hT[:, k:k + 2], ACT.Copy).then_inc(ahi_ok, 1)

            def ada_out(i):
                act.wait_ge(ada_pe, 2 * i + 2)
                if i >= 2:
                    act.wait_ge(col_T, i - 1)
                A(ada_row[i // 4][:, i % 2], ps[0:97, 6 + i % 2 if i < 4 else 0, :], ACT.Copy).then_inc(row_ok, 1)

            def modulate_tile(v, tb, quarters):
                l, s = v // 2, v % 2
                i0, ts = N_PAIRS[v] + 4 * tb, tile(tb)
                act.wait_ge(mod_ok, 2 + v)
                for q in quarters:
                    act.wait_ge(xT_ok, i0 + 2 * (q // 2) + 2)
                    for k in (2 * q, 2 * q + 1):
                        bank, at = chunk_at(v, k)
                        z = A(hT[:, k, ts], ps[:, bank, at + ts.start:at + ts.stop], ACT.Identity,
                              scale=modc[:, l, 2 * s + 1, k:k + 1], bias=modc[:, l, 2 * s, k:k + 1])
                    z.then_inc(hA_ok, 1)
                    act.wait_ge(hA_ok, i0 + q + 1)
                    A(a_hi[:, 2 * q:2 * q + 2, ts], hT[:, 2 * q:2 * q + 2, ts], ACT.Copy).then_inc(ahi_ok, 1)

            def first_norm():
                ada_out(0)
                for tb in range(TB):
                    squares(0, tb)
                ada_out(1)
                for u in range(2):
                    hi_at(u)
                modulate_first(range(2))
                ada_out(2)
                for u in range(2, 4):
                    hi_at(u)
                ada_out(3)
                modulate_first(range(2, 4))

            def norm(v):
                u0 = (mix_base, mlp_base)[v % 2][v // 2]
                squares(v, 0)
                for u in range(3):
                    hi_at(u0 + u)
                modulate_tile(v, 0, range(2))
                squares(v, 1)
                modulate_tile(v, 0, range(2, 4))
                hi_at(u0 + 3)
                modulate_tile(v, 1, range(4))

            def o_hi(l):
                for q in range(4):
                    act.wait_ge(oT_ok, 4 * l + q + 1)
                    A(a_hi[:, 2 * q:2 * q + 2], ps[:, 4 + q, :], ACT.Copy).then_inc(ahi_ok, 1)

            def read_in(l, n, dst, func=ACT.Copy):
                act.wait_ge(unit_used, mix_base[l] + 4 * n + 4)
                for tb in range(TB):
                    A(dst[tb], ps[:, in_bank(n, tb), :], func).then_inc(in_out, 1)

            def gla():
                def glr():
                    act.wait_ge(glr_p, 1)
                    A(glrT[:, :], ps[0:RANK, 0, 0:SEQ], ACT.Copy).then_inc(glr_ok, 1)

                def softplus():
                    act.wait_ge(z_ok, 1)
                    link(A(g_t, g_t, ACT.Exp))
                    A(g_t, g_t, ACT.Ln, bias=1.0).then_inc(ez_ok, 1)

                def decays():
                    act.wait_ge(G_ok, 1)
                    A(g_i, g_s, ACT.Exp, scale=-1.0 / 16).then_inc(eG_ok, 1)
                    A(g_t, g_t, ACT.Exp, scale=1.0 / 16).then_inc(eG_ok, 1)
                    A(g_e, g_s, ACT.Exp, scale=1.0 / 16).then_inc(eG_ok, 1)

                def tail():
                    act.wait_ge(kt_p, 1)
                    for tb in range(TB):
                        z = A(k_tail[:, tb], ps[:, 2 + tb, :].rearrange("p (h d) -> p h d", h=GH), ACT.Copy)
                    z.then_inc(kt_ok, 1)

                def o_squares(pair):
                    act.wait_ge(o_p, pair + 1)
                    for tb in range(TB):
                        for h in (2 * pair, 2 * pair + 1):
                            j = S_O + 4 * tb + h
                            A(o_tok[:, tb, h * DV:(h + 1) * DV],
                              ps[:, 2 * pair + tb, (h % 2) * DV:(h % 2 + 1) * DV],
                              ACT.Square, accum_out=stat[:, j:j + 1]).then_inc(oss_ok, 1)

                def o_root():
                    act.wait_ge(oss_ok, 8)
                    link(A(stat[:, S_O + 8:S_O + 16], stat[:, S_O:S_O + 8], ACT.Ln, scale=1.0 / DV, bias=eps[:, :]))
                    A(stat[:, S_O + 16:S_O + 24], stat[:, S_O + 8:S_O + 16], ACT.Exp, scale=-0.5).then_inc(or0_ok, 1)

                def silu_set():
                    nc.scalar.preload_act_table_set(SETS_SILU_SIN)

                def ln_exp_set():
                    nc.scalar.preload_act_table_set(SETS_LN_EXP)

                def k_in():
                    read_in(0, 0, [g_tok[:, 0, tb] for tb in range(TB)])
                    glr()

                tasks = {
                    (1, 3): [k_in],
                    (2, 0): [softplus],
                    (2, 3): [lambda: read_in(0, 1, [g_tok[:, 1, tb] for tb in range(TB)]), decays],
                    (3, 2): [tail],
                    (3, 3): [lambda: read_in(0, 2, [g_v[:, tb, 0:COLS] for tb in range(TB)])],
                    (4, 3): [lambda: read_in(0, 3, [g_v[:, tb, COLS:D] for tb in range(TB)])],
                    (5, 2): [lambda: o_squares(0)],
                    (5, 3): [lambda: o_squares(1), o_root],
                    (6, 0): [silu_set,
                             lambda: read_in(0, 4, [silu_r[:, tb, 0:COLS] for tb in range(TB)], ACT.Silu)],
                    (6, 2): [lambda: read_in(0, 5, [silu_r[:, tb, COLS:D] for tb in range(TB)], ACT.Silu)],
                }
                for n in range(1, 7):
                    for u in range(4):
                        hi_at(mix_base[0] + 4 * n + u)
                        for t in tasks.get((n, u), []):
                            t()
                o_hi(0)
                ln_exp_set()

            def moba():
                def stats(n):
                    tok, st = b_tok[n % 2], S_B2[n % 2]
                    if n > 1:
                        act.wait_ge(tok_used, n - 1)
                        act.wait_ge(rot_ok, n - 1)
                    read_in(1, n, [tok[:, tb] for tb in range(TB)])
                    if n > 0:
                        act.wait_ge(bss_ok, n)
                    act.wait_ge(in_out, 12 + 2 * n + 2)
                    for tb in range(TB):
                        for h in range(4):
                            j = st + 4 * tb + h
                            z = A(b_sq[:, tb, h * HD:(h + 1) * HD], tok[:, tb, h * HD:(h + 1) * HD],
                                  ACT.Square, accum_out=stat[:, j:j + 1])
                    z.then_inc(bss_ok, 1)
                    act.wait_ge(bss_ok, n + 1)
                    link(A(stat[:, st + 8:st + 16], stat[:, st:st + 8], ACT.Ln, scale=1.0 / HD, bias=eps[:, :]))
                    A(stat[:, st + 16:st + 24], stat[:, st + 8:st + 16], ACT.Exp, scale=-0.5).then_inc(br0_ok, 1)

                def read_rot(n):
                    act.wait_ge(rT_p, n + 1)
                    dst = (b_kT, b_qT)[n % 2]
                    for i in range(2):
                        z = A(dst[:, 4 * (n // 2) + 2 * i:4 * (n // 2) + 2 * i + 2],
                              ps[:, 2 + i, :].rearrange("p (h t) -> p h t", h=2), ACT.Copy)
                    z.then_inc(rT_ok, 1)

                def read_v(half):
                    read_in(1, 4 + half, [b_v[:, tb, half * COLS:(half + 1) * COLS] for tb in range(TB)])

                tasks = {}
                for n in range(4):
                    tasks.setdefault((n + 2, 3), []).append(lambda n=n: ada_out(4 + n))
                    tasks.setdefault((n + 1, 3), []).append(lambda n=n: stats(n))
                    tasks.setdefault((n + 3 if n < 3 else 6, 3 if n == 3 else 0), []).append(lambda n=n: read_rot(n))
                tasks[5, 3] = [lambda: read_v(0), lambda: ada_out(7)]
                tasks[(6, 3)] = [lambda: read_v(1), lambda: read_rot(3)]

                tasks[1, 0] = [sines]
                for n in range(1, 7):
                    for u in range(4):
                        hi_at(mix_base[1] + 4 * n + u)
                        for t in tasks.get((n, u), []):
                            t()

                def exps(h):
                    act.wait_ge(mx_ok, 2 * h + 2)
                    for i, (a, b) in enumerate(((0, P), (P, 3 * P))):
                        j = S_MX + 6 * h + i
                        z = A(b_p[:, h % 4, a:b], b_p[:, h % 4, a:b], ACT.Exp, scale=-1.0, bias=stat[:, j:j + 1],
                              accum_out=stat[:, j + 2:j + 3])
                    z.then_inc(ex_ok, 1)

                def read_pT(h):
                    act.wait_ge(pT_p, h + 1)
                    if h >= 4:
                        act.wait_ge(oT_ok, 4 + (h - 4) // 2 + 1)
                    A(b_pT[:, h % 4], ps[:, 2 + h % 2, 0:3 * P], ACT.Copy).then_inc(pT_ok, 1)

                for i in range(MH + 2):
                    if i < MH:
                        exps(i)
                    if i >= 2:
                        read_pT(i - 2)
                o_hi(1)

            def out_project(l):
                for u in range(4):
                    hi_at(mix_base[l] + 28 + u)

            def mlp(l):
                base, m0 = mlp_base[l], l * NJ

                def relus():
                    act.wait_ge(unit_used, base + 4)
                    for tb in range(TB):
                        A(relu[:, tb], ps[:, tb, :], ACT.Relu).then_inc(relu_ok, 1)

                def squares_of(j, b, src):
                    if not (isinstance(j, int) and m0 + j == 0):
                        act.wait_ge(m_ok, 2 * (m0 + j) - 1 + b)
                    A(sq[:, 2 * b:2 * b + 2], src, ACT.Square).then_inc(sq_ok, 1)

                def first_squares():
                    for b in range(2):
                        act.wait_ge(tr_ok, 2 * l + b + 1)
                        squares_of(0, b, ps[:, 4 + b, :].rearrange("p (c t) -> p c t", c=2))

                def hidden(j, u_done):
                    act.wait_ge(unit_used, u_done)
                    act.wait_ge(sq_ok, 2 * (m0 + j))
                    for b in range(2):
                        A(relu_c[:, 2 * b:2 * b + 2], ps[:, 2 * b:2 * b + 2, 0:SEQ], ACT.Relu).then_inc(relu_ok, 1)
                    for b in range(2):
                        act.wait_ge(relu_ok, 2 * (m0 + j) + b + 1)
                        squares_of(j, b, relu_c[:, 2 * b:2 * b + 2])

                def step(u0, round_, j, first=False, more=True):
                    for c in range(4):
                        hi(u0 + c, c, round_)
                        if c == 1 and first:
                            first_squares()
                    hidden(j + 1, u0)
                    if more:
                        for c in range(4):
                            hi(u0 + 4 + c, 4 + c, round_)

                for u in range(4):
                    hi_at(base + 4 + u)
                    if u == 2:
                        relus()
                step(base + 8, base // 8 + 1, 0, first=True)
                with act.Fori(1, NJ - 2) as j:
                    step(8 * j + base + 8, j + base // 8 + 1, j)
                step(base + 8 * NJ - 8, base // 8 + NJ - 1, NJ - 2, more=False)
                for c in range(4):
                    hi(base + 8 * NJ - 4 + c, 4 + c, base // 8 + NJ - 1)

            def sines():
                nc.scalar.preload_act_table_set(SETS_SILU_SIN)
                act.wait_ge(sc_arg, 1)
                n = TB * HD // 2
                A(r_w[:, 4:6, 0:n], r_w[:, 2:4, 0:n], ACT.Sin).then_inc(sc_ok, 1)
                nc.scalar.preload_act_table_set(SETS_LN_EXP)

            nc.scalar.preload_act_table_set(SETS_SILU_SIN)
            act.wait_ge(c_T, 1)
            A(c_act[:, :], ps[:, 4, 0:KC], ACT.Silu).then_inc(c_ok, 1)
            nc.scalar.preload_act_table_set(SETS_LN_EXP)
            act.wait_ge(set_up, 2)
            first_norm()
            for l in range(DEPTH):
                if l == 0:
                    gla()
                else:
                    norm(2)
                    moba()
                out_project(l)
                norm(2 * l + 1)
                mlp(l)

        @block.vector
        def _(dve):
            V = nc.vector
            steps = [0]

            def link(ins):
                steps[0] += 1
                ins.then_inc(dve_step, 1)
                dve.wait_ge(dve_step, steps[0])

            def lo(u, c):
                dve.wait_ge(hi_made, u + 1)
                V.tensor_tensor(w_lo[:, c % SPLIT], w_raw[:, c // 2, c % 2], w_hi[:, c % SPLIT].bitcast(F32),
                                ALU.subtract).then_inc(lo_made, 1)

            def lo_at(u):
                lo(u, u % 8)

            def ada(b, half, acc=None):
                acc = ada_acc[:, acc_slot(b)] if acc is None else acc
                t = ada_turn(b)
                dve.wait_ge(ada_sw_in[half], 16 * (b - 3))
                raw = ada_raw[:, half]
                for k in range(4):
                    w, s = raw[:, k], c_act[:, 4 * half + k:4 * half + k + 1]
                    if half == 0 and k == 0:
                        z = V.tensor_scalar(acc, w, s, None, ALU.mult)
                    else:
                        dve.wait_ge(ada_mac, 8 * t + 4 * half + k)
                        z = V.scalar_tensor_tensor(acc, w, s, acc, op0=ALU.mult, op1=ALU.add)
                    z.then_inc(ada_mac, 1)

            def first_mods(i, b, bank):
                vec, h = b // 2, slice(4 * (b % 2), 4 * (b % 2) + 4)
                m = modc[:, 0, vec, h]
                dve.wait_ge(col_T, i + 1)
                at = C_AB + vec * KC + h.start
                V.tensor_tensor(m, ps[:, bank, 0:4], cols[:, at:at + 4], ALU.add).then_inc(mod_red, 1)
                if vec == 1:
                    dve.wait_ge(mod_red, i + 1)
                    g = C_MIX + h.start
                    V.scalar_tensor_tensor(m, m, 1.0, cols[:, g:g + 4], op0=ALU.add, op1=ALU.mult
                                           ).then_inc(mod_ok, 1)

            def mods(v, bank):
                l, s = v // 2, v % 2
                if v == 3:
                    dve.wait_ge(col_T, 8)
                else:
                    dve.wait_ge(mod_T, v)
                at = C_AB + (4 * l + 2 * s) * KC
                V.tensor_tensor(modc[:, l, 2 * s:2 * s + 2].rearrange("p a k -> p (a k)"), ps[:, bank, 0:2 * KC],
                                cols[:, at:at + 2 * KC], ALU.add).then_inc(mod_red, 1)
                dve.wait_ge(mod_red, 4 + v)
                g = (C_MLP if s else C_MIX) + l * KC
                m = modc[:, l, 2 * s + 1]
                V.scalar_tensor_tensor(m, m, 1.0, cols[:, g:g + KC], op0=ALU.add, op1=ALU.mult
                                       ).then_inc(mod_ok, 1)

            def gate(i, bank):
                dve.wait_ge(gb_in, 32 * (i // 4 + 1))
                dve.wait_ge(gate_p, i + 1)
                g = gates[:, (i % 4) // 2, (i % 2) * COLS:(i % 2 + 1) * COLS]
                V.tensor_tensor(g, ps[:, bank, :], g, ALU.add).then_inc(gate_ok, 1)

            def newton(r, v, b, r0):
                link(V.tensor_tensor(b, v, r0, ALU.mult))
                link(V.tensor_tensor(b, b, r0, ALU.mult))
                link(V.tensor_scalar(b, b, -0.5, 1.5, ALU.mult, ALU.add))
                link(V.tensor_tensor(r, r0, b, ALU.mult))

            def scaled(v, tb):
                i = 2 * v + tb
                dve.wait_ge(ss_ok, i + 1)
                ss, r0, ms, b = [stat[:, a + i:a + i + 1] for a in (S_SS, S_R0, S_V, S_B)]
                link(V.tensor_scalar(ms, ss, 1.0 / D, EPS, ALU.mult, ALU.add))
                dve.wait_ge(r0_ok, i + 1)
                link(V.scalar_tensor_tensor(b, r0, ms, r0, op0=ALU.mult, op1=ALU.mult))
                link(V.tensor_scalar(b, b, -0.5, 1.5, ALU.mult, ALU.add))
                V.tensor_scalar(xn[:, tb], x[:, tb], r0, b, ALU.mult, ALU.mult).then_inc(xn_ok, 1)

            def modulate_first(quarters, after=None):
                dve.wait_ge(mod_ok, 1 + quarters[0] // 2)

                def odd(q):
                    k = 2 * q + 1
                    bank, at = chunk_at(0, k)
                    dve.wait_ge(xT_ok, 2 * (q // 2) + 2)
                    V.tensor_scalar(hT[:, k], ps[:, bank, at:at + SEQ],
                                    modc[:, 0, 1, k:k + 1], modc[:, 0, 0, k:k + 1],
                                    ALU.mult, ALU.add).then_inc(hD_ok, 1)

                odd(quarters[0])
                for q in quarters:
                    if q + 1 in quarters:
                        odd(q + 1)
                    a_low(q, q, hT[:, 2 * q:2 * q + 2], slice(0, SEQ))
                    if after is not None:
                        after(q)

            def first_norm():
                dve.wait_ge(x_in, 32)
                for tb in range(TB):
                    scaled(0, tb)
                dve.wait_ge(vec_T, 1)
                V.tensor_copy(cols[:, 0:N_ROWS], ps[:, 5, 0:N_ROWS]).then_inc(vec_ok, 1)
                dve.wait_ge(vec_ok, 1)
                for i in range(2):
                    first_mods(i, ADA_FIRST[i], 4 + i)
                modulate_first(range(2), lo_at)
                for u in range(2, 4):
                    lo_at(u)
                for i in range(2, 4):
                    first_mods(i, ADA_FIRST[i], 4 + i)
                modulate_first(range(2, 4))

            def zero_rows():
                dve.wait_ge(a_ok, A_NORM[2] + 8)
                V.memset(ps[:, 0, :], 0.0).then_inc(set_up, 1)

            def norm(v):
                l, s = v // 2, v % 2
                u0 = (mix_base, mlp_base)[s][l]

                def low(tb, q):
                    a_low(A_NORM[v] + 4 * tb + q, q, hT[:, 2 * q:2 * q + 2, tile(tb)], tile(tb))

                scaled(v, 0)
                lo_at(u0)
                dve.wait_ge(unit_used, u0)
                for half in ((1,) if s else (0, 1)):
                    residual(1 - s, 1 - s, half, 1, half == 1)
                low(0, 0)
                lo_at(u0 + 1)
                low(0, 1)
                lo_at(u0 + 2)
                scaled(v, 1)
                low(0, 2)
                low(0, 3)
                lo_at(u0 + 3)
                for q in range(4):
                    low(1, q)

            def a_low(i, q, src, ts):
                dve.wait_ge(ahi_ok, i + 1)
                V.tensor_tensor(a_lo[:, 2 * q:2 * q + 2, ts], src, a_hi[:, 2 * q:2 * q + 2, ts].bitcast(F32),
                                ALU.subtract).then_inc(a_ok, 1)

            def o_low(l, qs=range(4)):
                for q in qs:
                    a_low(A_OUT[l] + q, q, ps[:, 4 + q, :].rearrange("p (c t) -> p c t", c=2), slice(0, SEQ))

            def residual(mlp_, s, half, tb, last):
                cs = slice(half * COLS, (half + 1) * COLS)
                t = xn[:, tb, cs]
                link(V.tensor_tensor(t, ps[:, y_bank(mlp_, half, tb), :], gates[:, s, cs], ALU.mult))
                z = V.tensor_tensor(x[:, tb, cs], x[:, tb, cs], t, ALU.add)
                if last:
                    z.then_inc(x_new, 1)

            def out_project(l):
                for u in range(4):
                    lo_at(mix_base[l] + 28 + u)
                if l == 0:
                    mods(1, 4)
                dve.wait_ge(unit_used, mix_base[l] + 28)
                dve.wait_ge(gate_ok, 4 * l + 2)
                for tb in range(TB):
                    residual(0, 0, 0, tb, False)
                dve.wait_ge(y_ok, 2 * l + 1)
                residual(0, 0, 1, 0, True)

            def gla():
                def logits():
                    dve.wait_ge(z_p, 1)
                    for h in range(GH):
                        z = V.tensor_scalar(g_z[:, h], ps[:, h // 2, (h % 2) * SEQ:(h % 2 + 1) * SEQ],
                                            cols[:, C_BG + h:C_BG + h + 1], None, ALU.add)
                    link(z)
                    V.scalar_tensor_tensor(g_t, g_z, -1.0, g_z, op0=ALU.mult, op1=ALU.min).then_inc(z_ok, 1)

                def cumulate():
                    dve.wait_ge(ez_ok, 1)
                    dve.wait_ge(con_in, 64)
                    link(V.scalar_tensor_tensor(g_z, g_z, 0.0, g_t, op0=ALU.min, op1=ALU.subtract))
                    flat = "p h t -> p (h t)"
                    link(V.tensor_tensor_scan(g_s.rearrange(flat), restart.rearrange("p a b -> p (a b)"),
                                              g_z.rearrange(flat), 0.0, ALU.mult, ALU.add))
                    G = g_s.rearrange("p h (c i) -> p (h c) i", i=L)
                    V.tensor_tensor(g_t.rearrange("p h (c i) -> p (h c) i", i=L),
                                    G[:, :, L - 1:L].to_broadcast([P, GH * NCH, L]), G, ALU.subtract).then_inc(G_ok, 1)

                def keys():
                    dve.wait_ge(kT_p, 1)
                    dve.wait_ge(eG_ok, 2)
                    for i in range(2):
                        kT = ps[:, 2 + i, :].rearrange("p (h t) -> p h t", h=2)
                        V.tensor_tensor(k_inv[:, 2 * i:2 * i + 2], kT, g_i[:, 2 * i:2 * i + 2], ALU.mult)
                        z = V.tensor_tensor(k_tailT[:, 2 * i:2 * i + 2], kT, g_t[:, 2 * i:2 * i + 2], ALU.mult)
                    z.then_inc(kd_ok, 1)

                def queries():
                    dve.wait_ge(qT_p, 1)
                    dve.wait_ge(eG_ok, 3)
                    V.tensor_copy(dec[:, :, :], g_e.rearrange("p h (c i) -> p h c i", i=L)[:, :, :, L - 1])
                    for i in range(2):
                        qT = ps[:, i, :].rearrange("p (h t) -> p h t", h=2)
                        z = V.scalar_tensor_tensor(q_dec[:, 2 * i:2 * i + 2], qT, float(DK) ** -0.5,
                                                   g_e[:, 2 * i:2 * i + 2], op0=ALU.mult, op1=ALU.mult)
                    z.then_inc(qd_ok, 1)

                def zero():
                    dve.wait_ge(qd_ok, 1)
                    V.memset(att[:, :, :, :], 0.0).then_inc(zero_ok, 1)

                def masked():
                    dve.wait_ge(zero_ok, 1)
                    dve.wait_ge(att_p, 1)
                    for tb in range(TB):
                        z = V.copy_predicated(att[:, tb], keep[:, None, :].to_broadcast([P, GH, P]),
                                              ps[:, tb, :].rearrange("p (h q) -> p h q", h=GH))
                    z.then_inc(att_ok, 1)

                def states(h):
                    dve.wait_ge(u_p, h + 1)
                    b = 2 * (h % 2)
                    link(V.tensor_copy(state[1][:, h], ps[:, b, 0:DV]))
                    link(V.scalar_tensor_tensor(state[2][:, h], state[1][:, h], dec[:, h, 1:2], ps[:, b + 1, 0:DV],
                                                op0=ALU.mult, op1=ALU.add))
                    V.scalar_tensor_tensor(state[3][:, h], state[2][:, h], dec[:, h, 2:3], ps[:, b, DV:2 * DV],
                                           op0=ALU.mult, op1=ALU.add).then_inc(st_ok, 1)

                def o_scales():
                    dve.wait_ge(or0_ok, 1)
                    ss, r0, v, b, r = [stat[:, S_O + a:S_O + a + 8] for a in (0, 16, 24, 32, 40)]
                    link(V.tensor_scalar(v, ss, 1.0 / DV, EPS, ALU.mult, ALU.add))
                    newton(r, v, b, r0)

                def normed(pair):
                    r = stat[:, S_O + 40:S_O + 48]
                    for tb in range(TB):
                        for h in (2 * pair, 2 * pair + 1):
                            z = V.scalar_tensor_tensor(o_tok[:, tb, h * DV:(h + 1) * DV],
                                                       ps[:, 2 * pair + tb, (h % 2) * DV:(h % 2 + 1) * DV],
                                                       r[:, 4 * tb + h:4 * tb + h + 1], onorm[:, :],
                                                       op0=ALU.mult, op1=ALU.mult)
                    z.then_inc(on_ok, 1)

                def gated(pair):
                    cs = slice(pair * COLS, (pair + 1) * COLS)
                    dve.wait_ge(in_out, 10 + 2 * pair)
                    dve.wait_ge(on_ok, pair + 1)
                    for tb in range(TB):
                        z = V.tensor_tensor(o_tok[:, tb, cs], o_tok[:, tb, cs], silu_r[:, tb, cs], ALU.mult)
                    z.then_inc(ot_ok, 1)

                tasks = {
                    (2, 0): [logits], (2, 1): [cumulate], (2, 3): [keys], (3, 1): [queries, zero],
                    (3, 3): [masked], (4, 1): [lambda: states(0)], (4, 2): [lambda: states(1)],
                    (5, 0): [lambda: states(2)], (5, 1): [lambda: states(3)],
                    (5, 3): [o_scales, lambda: normed(0)],
                    (6, 0): [lambda: normed(1), lambda: gated(0)],
                }
                slots = [(1, 0), (1, 2), (2, 0), (3, 1), (3, 2), (3, 3), (4, 0), (4, 2), (5, 0), (5, 2)]
                adas = {at: (4 + i // 2, i % 2) for i, at in enumerate(slots)}
                for n in range(1, 7):
                    for u in range(4):
                        lo_at(mix_base[0] + 4 * n + u)
                        for t in tasks.get((n, u), []):
                            t()
                        if (n, u) in adas:
                            ada(*adas[n, u])
                o_low(0, range(2))
                gated(1)
                for i in range(2):
                    gate(i, 2 + i)
                o_low(0, range(2, 4))
                for half in range(2):
                    ada(9, half)

            def moba():
                def cosines(n):
                    dve.wait_ge(tab_ok, 1)
                    if n > 0:
                        dve.wait_ge(rot_ok, n)
                    dve.wait_ge(in_out, 12 + 2 * n + 2)
                    t = tab[:, 1 - n % 2, 0].rearrange("p (a d) -> p a d", a=TB)
                    for tb in range(TB):
                        V.tensor_tensor(b_t[:, tb].rearrange("p (h d) -> p h d", h=4),
                                        b_tok[n % 2][:, tb].rearrange("p (h d) -> p h d", h=4),
                                        t[:, tb:tb + 1].to_broadcast([P, 4, HD]), ALU.mult).then_inc(dve_step, 1)
                        steps[0] += 1

                def rotate(n):
                    t = tab[:, 1 - n % 2, 1].rearrange("p (a s d) -> p a s d", a=TB, s=2)
                    for tb in range(TB):
                        src = b_tok[n % 2][:, tb].rearrange("p (h s d) -> p h s d", h=4, s=2)
                        dst = b_u[:, tb].rearrange("p (h s d) -> p h s d", h=4, s=2)
                        for s in range(2):
                            z = V.tensor_tensor(dst[:, :, s], src[:, :, 1 - s],
                                                t[:, tb, s:s + 1].to_broadcast([P, 4, HD // 2]), ALU.mult)
                    z.then_inc(tok_used, 1)
                    dve.wait_ge(tok_used, n + 1)
                    link(V.tensor_tensor(b_t, b_t, b_u, ALU.add))

                def scale(n):
                    dve.wait_ge(br0_ok, n + 1)
                    st = S_B2[n % 2]
                    ss, r0, v, b, r = [stat[:, a:a + 8] for a in (st, st + 16, S_O + 24, S_O + 32, S_O + 40)]
                    link(V.tensor_scalar(v, ss, 1.0 / HD, EPS, ALU.mult, ALU.add))
                    newton(r, v, b, r0)
                    if n > 0:
                        dve.wait_ge(rT_p, n)
                    V.tensor_tensor(b_r.rearrange("p a (h d) -> p (a h) d", h=4),
                                    b_t.rearrange("p a (h d) -> p (a h) d", h=4),
                                    r[:, :, None].to_broadcast([P, 8, HD]), ALU.mult).then_inc(rot_ok, 1)

                def gate1():
                    for i in range(2):
                        gate(4 + i, 2 + i)

                tasks = {(1, 3): [tables, gate1]}
                for n in range(4):
                    tasks[n + 2, 0] = [lambda n=n: cosines(n)]
                    tasks[n + 2, 1] = [lambda n=n: rotate(n)]
                    tasks[n + 2, 2] = [lambda n=n: scale(n)]
                tasks[6, 2] = [lambda: mods(3, 1)]
                for n in range(1, 7):
                    for u in range(4):
                        lo_at(mix_base[1] + 4 * n + u)
                        for t in tasks.get((n, u), []):
                            t()

                def top(h):
                    dve.wait_ge(s_p, h + 1)
                    if h >= 4:
                        dve.wait_ge(pT_p, h - 3)
                    for i, (a, b) in enumerate(((0, P), (P, 3 * P))):
                        j = S_MX + 6 * h + i
                        V.tensor_tensor_reduce(b_p[:, h % 4, a:b], ps[:, h % 2, a:b], amask[:, a:b],
                                               -float(HD) ** -0.5, -NEG, ALU.add, ALU.min, stat[:, j:j + 1]
                                               ).then_inc(mx_ok, 1)

                def normal(h):
                    dve.wait_ge(ex_ok, h + 1)
                    j = S_MX + 6 * h
                    link(V.reciprocal(stat[:, j + 4:j + 6], stat[:, j + 2:j + 4]))
                    for i, (a, b) in enumerate(((0, P), (P, 3 * P))):
                        z = V.tensor_scalar(b_p[:, h % 4, a:b], b_p[:, h % 4, a:b], stat[:, j + 4 + i:j + 5 + i], None,
                                            ALU.mult)
                    z.then_inc(pn_ok, 1)

                for i in range(MH + 1):
                    if i < MH:
                        top(i)
                    if i >= 1:
                        normal(i - 1)
                o_low(1)

            def mlp(l):
                base, m0 = mlp_base[l], l * NJ

                def hidden(j, used, first=False):
                    for b in range(2):
                        dve.wait_ge(sq_ok, 2 * (m0 + j) + b + 1)
                        if b == 0 and not first:
                            dve.wait_ge(unit_used, used)
                        V.tensor_copy(m_hi[:, 2 * b:2 * b + 2], sq[:, 2 * b:2 * b + 2]).then_inc(mhi_ok, 1)
                    for b in range(2):
                        dve.wait_ge(mhi_ok, 2 * (m0 + j) + b + 1)
                        V.tensor_tensor(m_lo[:, 2 * b:2 * b + 2], sq[:, 2 * b:2 * b + 2],
                                        m_hi[:, 2 * b:2 * b + 2].bitcast(F32), ALU.subtract).then_inc(m_ok, 1)

                def step(u0, j, first=False, more=True, ada_b=None, ada_slot=None):
                    for c in range(4):
                        lo(u0 + c, c)
                        if c == 1:
                            hidden(j, u0 - 4, first)
                        if not more and ada_b is not None and c in (1, 3):
                            ada(ada_b, c // 2)
                    if more:
                        for c in range(4):
                            lo(u0 + 4 + c, 4 + c)
                            if ada_b is not None and c in (1, 3):
                                ada(ada_b, c // 2, ada_slot)

                for u in range(4):
                    lo_at(base + 4 + u)
                    if u in (1, 3):
                        ada(12 * l + 10, u // 2)
                b = 12 * l + 11
                step(base + 8, 0, first=True, ada_b=b, ada_slot=ada_acc[:, acc_slot(b)])
                with dve.Fori(1, NJ - 2) as j:
                    more = dict(ada_b=j + 11, ada_slot=ada_acc[:, bass.ds(j - 1, 1), :].rearrange("p a n -> p (a n)")
                                ) if l == 0 else {}
                    step(8 * j + base + 8, j, **more)
                step(base + 8 * NJ - 8, NJ - 2, more=False, ada_b=12 + NJ - 3 if l == 0 else None)
                for c in range(4):
                    lo(base + 8 * NJ - 4 + c, 4 + c)
                    if c == 1:
                        hidden(NJ - 1, base + 8 * NJ - 4)
                if l == 0:
                    angles(0)
                    angles(1)
                for i in range(2):
                    gate(4 * l + 2 + i, i)
                dve.wait_ge(gate_ok, 4 * l + 4)
                dve.wait_ge(y_ok, 2 * l + 2)
                for half in range(2):
                    residual(1, 1, half, 0, half == 1)
                if l + 1 < DEPTH:
                    mods(2 * l + 2, 2)
                else:
                    dve.wait_ge(y_ok, 2 * l + 3)
                    residual(1, 1, 0, 1, False)
                    dve.wait_ge(unit_used, base + 8 * NJ)
                    residual(1, 1, 1, 1, True)

            def angles(again):
                H2 = HD // 2
                W = TB * H2
                ang, n, r = r_w[:, 0, 0:W], r_w[:, 4:6, 0:W], r_w[:, 2:4, 0:W]
                if not again:
                    dve.wait_ge(tab_in, 64)
                    pos = stat[:, 188:190]
                    link(V.tensor_copy(pos, pos_i[:, :]))
                    for tb in range(TB):
                        z = V.tensor_scalar(ang[:, tb * H2:(tb + 1) * H2], r_w[:, 7, 0:H2], pos[:, tb:tb + 1], None,
                                            ALU.mult)
                    link(z)
                    for i, turn in enumerate((0.0, 0.25)):
                        z = V.tensor_scalar(n[:, i], ang, 1.0 / (2.0 * 3.141592653589793), turn, ALU.mult, ALU.add)
                    link(z)
                    src = r_w[:, 0:1, 0:W].to_broadcast([P, 2, W])
                else:
                    link(V.tensor_scalar(n, r, 1.0 / (2.0 * 3.141592653589793), None, ALU.mult))
                    src = r
                link(V.tensor_scalar(n, n, MAGIC, None, ALU.add))
                link(V.tensor_scalar(n, n, -MAGIC, None, ALU.add))
                for part in TWO_PI:
                    link(V.scalar_tensor_tensor(r, n, -part, src, op0=ALU.mult, op1=ALU.add))
                    src = r
                if not again:
                    link(V.tensor_scalar(r[:, 1], r[:, 1], 1.5707963267948966, None, ALU.add))
                    return
                V.tensor_scalar(r, r, 3.1415925, -3.1415925, ALU.min, ALU.max).then_inc(sc_arg, 1)

            def tables():
                dve.wait_ge(sc_ok, 1)
                H2 = HD // 2
                for which in range(2):
                    gain = r_w[:, 6, which * HD:(which + 1) * HD]
                    for tb in range(TB):
                        sin, cos = r_w[:, 4, tb * H2:(tb + 1) * H2], r_w[:, 5, tb * H2:(tb + 1) * H2]
                        o = tab[:, which].rearrange("p a (b s d) -> p a b s d", b=TB, s=2)
                        for s in range(2):
                            V.tensor_tensor(o[:, 0, tb, s], cos, gain[:, s * H2:(s + 1) * H2], ALU.mult)
                            z = V.scalar_tensor_tensor(o[:, 1, tb, s], sin, 1.0 if s else -1.0,
                                                       gain[:, (1 - s) * H2:(2 - s) * H2], op0=ALU.mult, op1=ALU.mult)
                z.then_inc(tab_ok, 1)

            V.memset(eps[:, :], EPS)
            V.memset(ones[:, :], 1.0).then_inc(set_up, 1)
            V.memset(ps[:, 6:8, :], 0.0).then_inc(set_up, 1)
            first_norm()
            for l in range(DEPTH):
                if l == 0:
                    gla()
                else:
                    norm(2)
                    zero_rows()
                    moba()
                out_project(l)
                norm(2 * l + 1)
                mlp(l)


_INS = ['x', 'c', 'positions', 'ada_w', 'ada_b', 'norm_mix_g', 'norm_mlp_g', 'gla_w_in', 'gla_w_gate_up',
        'gla_b_gate', 'gla_onorm_g', 'gla_w_out', 'moba_w_in', 'moba_q_norm_g', 'moba_k_norm_g', 'moba_w_out',
        'mlp_w1', 'mlp_w2']
_OUTS = [((1, 256, 1024), 'float32')]


def kernel(**inputs):
    import numpy as _np
    import concourse.bacc as _bacc
    from concourse import mybir as _mybir
    from concourse.bass_utils import run_bass_kernel_spmd as _run

    i = _np.arange(128)
    after = i[:, None] <= i[None, :]
    same = i[:, None] // 64 == i[None, :] // 64
    tri = _np.where(after.T, 0.0, -1.0e30)
    consts = {
        "eye": _np.eye(128, dtype=_np.float32),
        "keep": (after & same).astype(_np.int32),
        "amask": _np.concatenate([tri, _np.zeros((128, 128)), tri], axis=1).astype(_np.float32),
        "restart": (_np.arange(1024) % 64 != 0).astype(_np.float32)[None],
        "invf": (10000.0 ** (-_np.arange(64) / 64.0)).astype(_np.float32)[None],
    }
    nc = _bacc.Bacc("TRN2", target_bir_lowering=False, num_devices=1)
    arrays, args = {}, []
    for name in _INS + list(consts):
        a = _np.ascontiguousarray(inputs[name] if name in inputs else consts[name])
        arrays[f"in_{name}_dram"] = a
        args.append(nc.dram_tensor(f"in_{name}_dram", a.shape, _mybir.dt.from_np(a.dtype), kind="ExternalInput").ap())
    for n, (shape, dtype) in enumerate(_OUTS):
        dt = _mybir.dt.from_np(_np.dtype(dtype))
        args.append(nc.dram_tensor(f"out_{n}_dram", shape, dt, kind="ExternalOutput").ap())
    trunk_kernel(nc, *args)
    r = _run(nc, [arrays], core_ids=[0])
    got = tuple(r.results[0][f"out_{n}_dram"] for n in range(len(_OUTS)))
    return got[0]
```
